# Optimizing a Trainium2 kernel written in Bass

```python
import jax, jax.numpy as jnp
from jax import lax
import numpy as np

D_MODEL = 2048
BATCH = 1
SEQ = 512
DEPTH = 2
DEC_BATCH = 8
DEC_SEQ = 4
PAST_LEN = 2048
PAGE_SIZE = 128

WINDOW = 128
ATT_HEAD_DIM = 64
ATT_Q_HEADS = D_MODEL // ATT_HEAD_DIM
ATT_KV_HEADS = 8
ATT_GROUP = ATT_Q_HEADS // ATT_KV_HEADS
ATT_INNER = ATT_Q_HEADS * ATT_HEAD_DIM
ATT_KV_WIDTH = ATT_KV_HEADS * ATT_HEAD_DIM
ATT_BLOCK = WINDOW
ATT_IN_COLS = ATT_INNER + 2 * ATT_KV_WIDTH + ATT_INNER
M_HEADS = 8
M_DV = D_MODEL // M_HEADS
M_DK = M_DV // 2
M_QK_WIDTH = M_HEADS * M_DK
M_INNER = M_HEADS * M_DV
M_CHUNK = 64
M_IN_COLS = 2 * M_QK_WIDTH + 3 * M_INNER + 2 * M_HEADS
N_ATT_LAYERS = (DEPTH + 1) // 2
N_MLSTM_LAYERS = DEPTH // 2
NORM_EPS = 1e-6

kernel_name = "hybrid_swa_sink_mlstm_sandwich_adaln_step"

def rmsnorm(x, g):
    xf = x.astype(jnp.float32)
    y = xf * lax.rsqrt(jnp.mean(xf * xf, axis=-1, keepdims=True) + NORM_EPS)
    return (y * g.astype(jnp.float32)).astype(x.dtype)

def alibi_slopes():
    s = 2.0 ** (-8.0 * np.arange(1, ATT_Q_HEADS + 1) / ATT_Q_HEADS)
    return jnp.asarray(s, jnp.float32).reshape(ATT_KV_HEADS, ATT_GROUP, 1, 1)

def adaln(c, w, b):
    mod = jax.nn.silu(c) @ w + b
    shift, scale, gate = jnp.split(mod[:, None, :], 3, axis=-1)
    return shift, scale, gate

def sink_attend(q, k, v, bias, sinks):
    s = jnp.einsum('...qhgd,...khd->...hgqk', q, k).astype(jnp.float32) * (ATT_HEAD_DIM ** -0.5) + bias
    sink = sinks.astype(jnp.float32)[..., None, None]
    mx = jnp.maximum(jnp.max(s, axis=-1, keepdims=True), sink)
    p = jnp.exp(s - mx)
    p = p / (jnp.sum(p, axis=-1, keepdims=True) + jnp.exp(sink - mx))
    return jnp.einsum('...hgqk,...khd->...qhgd', p.astype(v.dtype), v)

def attention_branch(h, w_in, w_out, sinks, buf_k=None, buf_v=None):
    bn, t, _ = h.shape
    proj = h @ w_in
    q, k, v, z = jnp.split(proj, [ATT_INNER, ATT_INNER + ATT_KV_WIDTH, ATT_INNER + 2 * ATT_KV_WIDTH], axis=-1)
    q = q.reshape(bn, t, ATT_KV_HEADS, ATT_GROUP, ATT_HEAD_DIM)
    k = k.reshape(bn, t, ATT_KV_HEADS, ATT_HEAD_DIM)
    v = v.reshape(bn, t, ATT_KV_HEADS, ATT_HEAD_DIM)
    slopes = alibi_slopes()
    sk = sinks.reshape(ATT_KV_HEADS, ATT_GROUP)
    if buf_k is None:
        nb = t // ATT_BLOCK
        qb = q.reshape(bn, nb, ATT_BLOCK, ATT_KV_HEADS, ATT_GROUP, ATT_HEAD_DIM)
        kb = k.reshape(bn, nb, ATT_BLOCK, ATT_KV_HEADS, ATT_HEAD_DIM)
        vb = v.reshape(bn, nb, ATT_BLOCK, ATT_KV_HEADS, ATT_HEAD_DIM)
        kk = jnp.concatenate([jnp.concatenate([jnp.zeros_like(kb[:, :1]), kb[:, :-1]], axis=1), kb], axis=2)
        vv = jnp.concatenate([jnp.concatenate([jnp.zeros_like(vb[:, :1]), vb[:, :-1]], axis=1), vb], axis=2)
        qi = jnp.arange(ATT_BLOCK)[:, None]
        ki = jnp.arange(2 * ATT_BLOCK)[None, :]
        d = qi + ATT_BLOCK - ki
        blk = jnp.arange(nb)[:, None, None]
        valid = (d >= 0) & (d < WINDOW) & (blk * ATT_BLOCK - ATT_BLOCK + ki >= 0)
        bias = jnp.where(valid[:, None, None], -slopes * d.astype(jnp.float32), -jnp.inf)
        o = sink_attend(qb, kk, vv, bias, sk).reshape(bn, t, ATT_INNER)
        new_k, new_v = k[:, t - WINDOW:], v[:, t - WINDOW:]
    else:
        w = buf_k.shape[1]
        kk = jnp.concatenate([buf_k.astype(k.dtype), k], axis=1)
        vv = jnp.concatenate([buf_v.astype(v.dtype), v], axis=1)
        d = jnp.arange(t)[:, None] - jnp.arange(-w, t)[None, :]
        valid = (d >= 0) & (d < WINDOW)
        bias = jnp.where(valid, -slopes * d.astype(jnp.float32), -jnp.inf)
        o = sink_attend(q, kk, vv, bias, sk).reshape(bn, t, ATT_INNER)
        new_k, new_v = kk[:, -w:], vv[:, -w:]
    y = (o * jax.nn.silu(z)) @ w_out
    return y, new_k, new_v

def mlstm_chunk_step(carry, xs):
    S, n, m = carry
    q, k, v, li, lf = xs
    L = li.shape[-1]
    b = jnp.cumsum(lf, axis=-1)
    mt = b + jnp.maximum(m[..., None], lax.cummax(li - b, axis=2))
    a = jnp.exp(b + m[..., None] - mt)
    causal = jnp.tril(jnp.ones((L, L), dtype=bool))
    dlog = b[..., :, None] - b[..., None, :] + li[..., None, :] - mt[..., :, None]
    dmat = jnp.exp(jnp.where(causal, dlog, -jnp.inf))
    qs = q * (M_DK ** -0.5)
    qk = jnp.einsum('bhtd,bhsd->bhts', qs, k) * dmat
    num = a[..., None] * jnp.einsum('bhtd,bhde->bhte', qs, S) + jnp.einsum('bhts,bhse->bhte', qk, v)
    den = a * jnp.einsum('bhtd,bhd->bht', qs, n) + jnp.sum(qk, axis=-1)
    hout = num / jnp.maximum(jnp.abs(den), jnp.exp(-mt))[..., None]
    m_new = mt[..., -1]
    wts = jnp.exp(b[..., -1:] - b + li - m_new[..., None])
    a_last = a[..., -1]
    S_new = a_last[..., None, None] * S + jnp.einsum('bhs,bhsd,bhse->bhde', wts, k, v)
    n_new = a_last[..., None] * n + jnp.einsum('bhs,bhsd->bhd', wts, k)
    return (S_new, n_new, m_new), hout

def mlstm_branch(h, w_in, b_if, g_head, w_out, S0, n0, m0):
    bn, t, _ = h.shape
    proj = h @ w_in
    cuts = np.cumsum([M_QK_WIDTH, M_QK_WIDTH, M_INNER, M_INNER, M_INNER]).tolist()
    q, k, v, o, z, gates = jnp.split(proj, cuts, axis=-1)
    gates = gates.astype(jnp.float32) + b_if.astype(jnp.float32)
    li = gates[..., :M_HEADS]
    lf = jax.nn.log_sigmoid(gates[..., M_HEADS:])
    L = M_CHUNK if t % M_CHUNK == 0 else t
    nc = t // L

    def to_chunks(a):
        a = a.astype(jnp.float32).reshape((bn, nc, L, M_HEADS) + a.shape[3:])
        return jnp.moveaxis(a, (1, 3), (0, 2))

    xs = (to_chunks(q.reshape(bn, t, M_HEADS, M_DK)), to_chunks(k.reshape(bn, t, M_HEADS, M_DK)),
          to_chunks(v.reshape(bn, t, M_HEADS, M_DV)), to_chunks(li), to_chunks(lf))
    carry0 = (S0.astype(jnp.float32), n0.astype(jnp.float32), m0.astype(jnp.float32))
    (S, n, m), hs = lax.scan(mlstm_chunk_step, carry0, xs)
    hs = jnp.moveaxis(hs, (0, 2), (1, 3)).reshape(bn, t, M_HEADS, M_DV)
    hn = hs * lax.rsqrt(jnp.mean(hs * hs, axis=-1, keepdims=True) + NORM_EPS) * g_head.astype(jnp.float32)
    hn = hn * jax.nn.sigmoid(o.reshape(bn, t, M_HEADS, M_DV).astype(jnp.float32))
    out = hn.astype(h.dtype).reshape(bn, t, M_INNER) * jax.nn.silu(z)
    y = out @ w_out
    return y, S.astype(S0.dtype), n.astype(n0.dtype), m.astype(m0.dtype)

def setup_inputs(seed: int = 0) -> dict:
    key = jax.random.key(seed)
    ks = jax.random.split(key, 24)
    f32 = jnp.float32
    w_buf = min(WINDOW, PAST_LEN)
    nrm = lambda k, shape, s=1.0: (jax.random.normal(k, shape, f32) * s).astype(f32)
    b_if_i = nrm(ks[18], (N_MLSTM_LAYERS, M_HEADS), 0.1)
    b_if_f = jnp.broadcast_to(jnp.linspace(3.0, 6.0, M_HEADS, dtype=f32), (N_MLSTM_LAYERS, M_HEADS)) \
        + nrm(ks[19], (N_MLSTM_LAYERS, M_HEADS), 0.1)
    return {
        "x_prompt": nrm(ks[0], (BATCH, SEQ, D_MODEL)),
        "x_sample": nrm(ks[1], (DEC_BATCH, DEC_SEQ, D_MODEL)),
        "c_prompt": nrm(ks[2], (BATCH, D_MODEL)),
        "c_sample": nrm(ks[3], (DEC_BATCH, D_MODEL)),
        "cache_k": nrm(ks[4], (N_ATT_LAYERS, DEC_BATCH, w_buf, ATT_KV_HEADS, ATT_HEAD_DIM)),
        "cache_v": nrm(ks[5], (N_ATT_LAYERS, DEC_BATCH, w_buf, ATT_KV_HEADS, ATT_HEAD_DIM)),
        "state_C": nrm(ks[6], (N_MLSTM_LAYERS, DEC_BATCH, M_HEADS, M_DK, M_DV)),
        "state_n": nrm(ks[7], (N_MLSTM_LAYERS, DEC_BATCH, M_HEADS, M_DK)),
        "state_m": nrm(ks[8], (N_MLSTM_LAYERS, DEC_BATCH, M_HEADS)),
        "w_ada": nrm(ks[9], (DEPTH, D_MODEL, 3 * D_MODEL), 0.5 * D_MODEL ** -0.5),
        "b_ada": nrm(ks[10], (DEPTH, 3 * D_MODEL), 0.02),
        "g_pre": 1.0 + nrm(ks[11], (DEPTH, D_MODEL), 0.02),
        "g_post": 1.0 + nrm(ks[12], (DEPTH, D_MODEL), 0.02),
        "w_in_attn": nrm(ks[13], (N_ATT_LAYERS, D_MODEL, ATT_IN_COLS), D_MODEL ** -0.5),
        "sinks": nrm(ks[14], (N_ATT_LAYERS, ATT_Q_HEADS), 0.5),
        "w_out_attn": nrm(ks[15], (N_ATT_LAYERS, ATT_INNER, D_MODEL), ATT_INNER ** -0.5),
        "w_in_mlstm": nrm(ks[16], (N_MLSTM_LAYERS, D_MODEL, M_IN_COLS), D_MODEL ** -0.5),
        "b_if_mlstm": jnp.concatenate([b_if_i, b_if_f], axis=-1),
        "g_head_mlstm": 1.0 + nrm(ks[20], (N_MLSTM_LAYERS, M_HEADS, M_DV), 0.02),
        "w_out_mlstm": nrm(ks[17], (N_MLSTM_LAYERS, M_INNER, D_MODEL), M_INNER ** -0.5),
    }

def reference(x_prompt, x_sample, c_prompt, c_sample, cache_k, cache_v, state_C, state_n, state_m,
              w_ada, b_ada, g_pre, g_post, w_in_attn, sinks, w_out_attn,
              w_in_mlstm, b_if_mlstm, g_head_mlstm, w_out_mlstm):
    xp, xs = x_prompt, x_sample
    bp = x_prompt.shape[0]
    kp_l, vp_l, ks_l, vs_l = [], [], [], []
    Cp_l, np_l, mp_l, Cs_l, ns_l, ms_l = [], [], [], [], [], []
    for l in range(DEPTH):
        sh_p, sc_p, gt_p = adaln(c_prompt, w_ada[l], b_ada[l])
        sh_s, sc_s, gt_s = adaln(c_sample, w_ada[l], b_ada[l])
        hp = rmsnorm(xp, g_pre[l]) * (1.0 + sc_p) + sh_p
        hs = rmsnorm(xs, g_pre[l]) * (1.0 + sc_s) + sh_s
        j = l // 2
        if l % 2 == 0:
            yp, kp, vp = attention_branch(hp, w_in_attn[j], w_out_attn[j], sinks[j])
            ys, ksn, vsn = attention_branch(hs, w_in_attn[j], w_out_attn[j], sinks[j], cache_k[j], cache_v[j])
            kp_l.append(kp); vp_l.append(vp); ks_l.append(ksn); vs_l.append(vsn)
        else:
            S0 = jnp.zeros((bp, M_HEADS, M_DK, M_DV), xp.dtype)
            n0 = jnp.zeros((bp, M_HEADS, M_DK), xp.dtype)
            m0 = jnp.zeros((bp, M_HEADS), xp.dtype)
            yp, Cp, npn, mp = mlstm_branch(hp, w_in_mlstm[j], b_if_mlstm[j], g_head_mlstm[j], w_out_mlstm[j], S0, n0, m0)
            ys, Cs, nsn, ms = mlstm_branch(hs, w_in_mlstm[j], b_if_mlstm[j], g_head_mlstm[j], w_out_mlstm[j],
                                           state_C[j], state_n[j], state_m[j])
            Cp_l.append(Cp); np_l.append(npn); mp_l.append(mp)
            Cs_l.append(Cs); ns_l.append(nsn); ms_l.append(ms)
        xp = xp + gt_p * rmsnorm(yp, g_post[l])
        xs = xs + gt_s * rmsnorm(ys, g_post[l])
    new_k_prompt = jnp.stack(kp_l)
    new_v_prompt = jnp.stack(vp_l)
    new_k_sample = jnp.stack(ks_l)
    new_v_sample = jnp.stack(vs_l)
    new_C_prompt = jnp.stack(Cp_l)
    new_n_prompt = jnp.stack(np_l)
    new_m_prompt = jnp.stack(mp_l)
    new_C_sample = jnp.stack(Cs_l)
    new_n_sample = jnp.stack(ns_l)
    new_m_sample = jnp.stack(ms_l)
    return (xp, xs, new_k_prompt, new_v_prompt, new_k_sample, new_v_sample,
            new_C_prompt, new_n_prompt, new_m_prompt, new_C_sample, new_n_sample, new_m_sample)


_drawn_inputs = setup_inputs


def setup_inputs(seed=0):
    import zlib

    import numpy as np

    out = dict(_drawn_inputs(seed))
    spreads = {}
    factors = {'g_post': 5.008, 'g_head_mlstm': 8.0}
    for name, (base, spread) in spreads.items():
        noise = np.random.default_rng([zlib.crc32(name.encode()), seed]).standard_normal(out[name].shape)
        drawn = base * np.exp(spread * noise) if base else spread * noise
        out[name] = __import__('jax').numpy.asarray(drawn.astype(out[name].dtype))
    for name, factor in factors.items():
        out[name] = (out[name] * factor).astype(out[name].dtype)
    return out
```

```python
from contextlib import ExitStack

import numpy as np
import concourse.bass as bass
from concourse import mybir

F32 = mybir.dt.float32
F32R = mybir.dt.float32r
ALU = mybir.AluOpType
ACT = mybir.ActivationFunctionType
AX = mybir.AxisListType.X
ds = bass.ds

P = 128
D = 2048
KT = D // P
TP = 512
NB, ND = 8, 4
TS = NB * ND
T = TP + TS
HT = T // 2
NSEQ = 1 + NB
WIN = 128
QH, KVH, HD = 32, 8, 64
GR = 4
MH, DK, DV = 8, 128, 256
NC_ = TP // P
EPS = 1e-6
BIG = -1e30

OWNER = dict(A="d", Z="d", O="d", Q="a", K="a", V="a", Y="a", G="a")
L0K = "ZZZZAAQVQAQAQK"
L1K = "ZOZOQKVV"
PHASES = [("ada0", 1, "A" * 8), ("l0", GR, L0K), ("out0", 1, "Y" * KT), ("gate", 1, "G"),
          ("l1", MH, L1K), ("out1", 1, "Y" * KT)]


def first_of(kinds, size):
    return {ph: sum(n * sum(size(k) for k in ks) for p, n, ks in PHASES[:i])
            for i, (ph, _, _) in enumerate(PHASES)}


UNITS = dict.fromkeys("ZOQKVYG", 1) | {"A": 4}
KINDS = {ph: ks for ph, _, ks in PHASES}
ITERS = {ph: n for ph, n, _ in PHASES}
ENTRY0 = first_of(PHASES, lambda k: 1)
UNIT0 = first_of(PHASES, lambda k: UNITS[k])
FREED0 = {w: first_of(PHASES, lambda k, w=w: int(OWNER[k] == w)) for w in "ad"}
RAW0 = UNIT0["l0"]

C_ID, C_ONE, C_SLP, C_SLS, C_SEL = 0, 128, 256, 288, 296
C_FIX = 305
C_NEGD, C_NEGS = 305, 305 + 768
C_L0 = C_NEGS + 1056
C_CM, C_SM, C_BM = C_L0, C_L0 + 128, C_L0 + 160
C_ALL = C_L0 + 168


def constants():
    c = np.zeros((P, C_ALL), np.float32)
    c[:, C_ID:C_ID + P] = np.eye(P)
    c[:, C_ONE:C_ONE + P] = 1.0
    slopes = (2.0 ** (-8.0 * np.arange(1, QH + 1) / QH)).astype(np.float32)
    c[:, C_SLP:C_SLP + QH] = slopes
    p = np.arange(P)
    for m in range(GR):
        for half in range(2):
            c[:, C_SLS + 2 * m + half] = slopes[8 * m + 4 * (p // 64) + 2 * (p // 32 % 2) + half]
    for r in range(2 * NSEQ):
        c[32 + r, C_SEL + r % NSEQ] = 1.0
    c[32 + 2 * NSEQ, C_SEL:C_SEL + NSEQ] = 1.0
    q, k = np.arange(P)[:, None], np.arange(2 * P)[None, :]
    d = q + P - k
    neg = np.where((d >= 0) & (d < WIN), -d.astype(np.float32), BIG)
    first = np.where(k < P, BIG, neg)
    c[:, C_NEGD:C_NEGD + 768] = np.concatenate([first, neg, neg], 1)
    tok = p % TS
    b, t = (tok // ND)[:, None], (tok % ND)[:, None]
    j = np.arange(NB * WIN)[None, :]
    dc = t + WIN - j % WIN
    c[:, C_NEGS:C_NEGS + 1024] = np.where((j // WIN == b) & (dc < WIN), -dc, BIG)
    j = np.arange(TS)[None, :]
    dn = t - j % ND
    c[:, C_NEGS + 1024:C_NEGS + 1056] = np.where((j // ND == b) & (dn >= 0), -dn, BIG)
    s, t = np.arange(P)[:, None], np.arange(P)[None, :]
    c[:, C_CM:C_CM + P] = np.where(s <= t, 0.0, BIG)
    s, t = np.arange(TS)[:, None], np.arange(TS)[None, :]
    c[0:TS, C_SM:C_SM + TS] = np.where((s // ND == t // ND) & (s <= t), 0.0, BIG)
    c[0:TS, C_BM:C_BM + NB] = (np.arange(TS)[:, None] // ND == np.arange(NB)[None, :])
    return c


ARENA = 12520


def offsets(sizes, at=0):
    out = {}
    for name, size in sizes:
        out[name] = (at, size)
        at += size
    assert at <= ARENA, at
    return out


XW = offsets([("x", KT * T), ("sq", 2 * T), ("r", T), ("vec", P)])
A0 = offsets([("q", 4 * TP), ("qs", P), ("kT", P + T), ("kS", P + T), ("vT", T), ("vtok", TP),
              ("vks", 256), ("kout", P), ("ckraw", 1024), ("cv", 1024), ("ckT", 1024), ("ckS", 1024),
              ("soft", 1536), ("negd", 768), ("negs", 1056)])
A1 = offsets([("q", T), ("k", T), ("v", 2 * T), ("vtok", 4 * DV), ("wk", 4 * P), ("rows", 3 * T),
              ("S", 4 * DV), ("n", 8), ("D", TP), ("qa", T), ("qn", T), ("emt", T), ("h", 2 * T),
              ("cs", NB * DV), ("sb", 3 * TS), ("Ds", TS), ("Uc", 40), ("wc", 40), ("wb", 64),
              ("nsT", 64), ("nout", 72), ("cm", 128), ("sm", 32), ("bm", 8)])


SLOW = dict(allow_slow_non_contiguous=True)


def val(base, per, it, k=0):
    r, c = it
    n = base + c * per + k
    return n if r is None else r * per + n


def fixed(eng, value):
    return value if isinstance(value, int) else eng.snap(eng.to_reg(value))


class Chain:

    def __init__(self, eng, sem):
        self.eng, self.sem, self.base, self.k, self.it, self.per = eng, sem, 0, 0, (None, 0), 0

    def __call__(self, ins):
        self.k += 1
        ins.then_inc(self.sem, 1)
        self.eng.wait_ge(self.sem, val(self.base, self.per, self.it, self.k))

    def enter(self, reg, per):
        self.base, self.k, self.it, self.per = self.base + self.k, 0, (reg, 0), per

    def leave(self, iters):
        assert self.k == self.per, f"a loop body has {self.k} steps, not {self.per}"
        self.base, self.k, self.it, self.per = self.base + iters * self.per, 0, (None, 0), 0


def trunk(nc, x_prompt, x_sample, c_prompt, c_sample, cache_k, cache_v, state_C, state_n, state_m,
          w_ada, b_ada, g_pre, g_post, w_in_attn, sinks, w_out_attn, w_in_mlstm, b_if_mlstm,
          g_head_mlstm, w_out_mlstm, const,
          y_prompt, y_sample, nk_p, nv_p, nk_s, nv_s, nC_p, nn_p, nm_p, nC_s, nn_s, nm_s, x_spill):
    with ExitStack() as ctx:
        def sb(name, shape, dt=F32):
            return ctx.enter_context(nc.sbuf_tensor(name, shape, dt))

        def sem(name):
            return ctx.enter_context(nc.semaphore(name))

        h_hi = sb("h_hi", [P, KT, T], F32R)
        h_lo = sb("h_lo", [P, KT, T], F32R)
        obuf = sb("obuf", [P, KT, T])
        raw = [sb(f"raw{i}", [P, D]) for i in range(2)]
        w_hi = [sb(f"w_hi{i}", [P, D], F32R) for i in range(2)]
        w_lo = [sb(f"w_lo{i}", [P, D], F32R) for i in range(2)]
        cT = sb("cT", [P, 16 * 18 + 110], F32R)
        modT = sb("modT", [P, 96, NSEQ])
        misc = sb("misc", [P, T])
        gT = sb("gT", [P, 80])
        fix = sb("fix", [P, C_FIX])
        nsink = sb("nsink", [P, QH + 8])
        st = sb("st", [P, 40])
        arena = sb("arena", [P, ARENA])
        PJ = ctx.enter_context(nc.psum_tensor("PJ", [P, 4, 512], F32))
        MX = ctx.enter_context(nc.psum_tensor("MX", [P, 4, 512], F32))

        def area(table, name):
            a, n = table[name]
            return arena[:, a:a + n]

        ident = fix[:, C_ID:C_ID + P]
        ones = fix[:, C_ONE:C_ONE + P]
        xw = area(XW, "x").rearrange("p (k t) -> p k t", k=KT)
        xflat = area(XW, "x")
        sqb = area(XW, "sq").rearrange("p (a t) -> p a t", a=2)
        rB = area(XW, "r")
        gvec = area(XW, "vec")[0:80, :]
        c_rows = area(XW, "x")[0:NSEQ, 0:D]
        c_tanh = area(XW, "x")[0:NSEQ, D:2 * D]
        c_full = area(XW, "x")[:, 2 * D:2 * D + KT * NSEQ]
        q0 = area(A0, "q").rearrange("p (j t) -> p j t", j=4)
        qS = area(A0, "qs")
        kT, kS = area(A0, "kT"), area(A0, "kS")
        vT, vtok = area(A0, "vT"), area(A0, "vtok")
        vks, kout = area(A0, "vks"), area(A0, "kout")
        ckraw = area(A0, "ckraw").rearrange("p (b c) -> p b c", b=NB)
        PTs, PTn = area(A0, "ckraw"), area(A0, "soft")[0:TS, 1056:1184]
        cv = area(A0, "cv").rearrange("p (b c) -> p b c", b=NB)
        ckT, ckS = area(A0, "ckT"), area(A0, "ckS")
        soft = area(A0, "soft")
        SPs = soft[:, 0:1056]
        PP = [soft[:, 0:512], soft[:, 512:1024]]
        PT = soft[:, 1024:1536]
        negd, negs = area(A0, "negd"), area(A0, "negs")
        q1, k1, v1 = area(A1, "q"), area(A1, "k"), area(A1, "v").rearrange("p (a t) -> p a t", a=2)
        hsq = v1
        vt1 = area(A1, "vtok").rearrange("p (c e) -> p c e", c=4)
        wk = area(A1, "wk").rearrange("p (c e) -> p c e", c=4)
        rows = area(A1, "rows")
        wks = rows[0:TS, 0:1024].rearrange("p (b e) -> p b e", b=NB)
        vs = rows[0:TS, 1024:1280]
        GP = slice(64, 64 + MH)
        BP = slice(96, 96 + MH)
        R = rows[GP, :].rearrange("p (j t) -> p j t", j=3)
        RB = rows[BP, :].rearrange("p (j t) -> p j t", j=3)
        S = area(A1, "S").rearrange("p (c e) -> p c e", c=4)
        nn = area(A1, "n")
        Dm = area(A1, "D")
        qa, qn, emt = area(A1, "qa"), area(A1, "qn"), area(A1, "emt")
        hh = area(A1, "h").rearrange("p (a t) -> p a t", a=2)
        aB = area(A1, "h")[:, 0:TP]
        cs = area(A1, "cs").rearrange("p (b e) -> p b e", b=NB)
        sB = area(A1, "sb").rearrange("p (j t) -> p j t", j=3)
        Ds = area(A1, "Ds")
        Uc, wc = area(A1, "Uc"), area(A1, "wc")
        wb = area(A1, "wb").rearrange("p (h b) -> p h b", h=MH)
        nsT = area(A1, "nsT").rearrange("p (b h) -> p b h", b=NB)
        nout = area(A1, "nout")
        cm, sm, bm = area(A1, "cm"), area(A1, "sm"), area(A1, "bm")
        LI = area(A1, "h")[GP, 0:T]
        LF = area(A1, "h")[GP, T:2 * T]
        Ub = area(A1, "qa")[GP, :]
        Wr = area(A1, "qn")[GP, :]
        Bc = area(A1, "emt")[GP, :]
        Mr = area(A1, "S")[GP, 0:T]
        tg = area(A1, "D")[GP, 0:16]
        m0s = area(A1, "D")[GP, 16:24]
        bif = area(A1, "D")[GP, 24:26]
        nrow = area(A1, "wk")[0:64, 0:P]

        const_in, mask_in = sem("const_in"), sem("mask_in")
        c_in = sem("c_in")
        vec_in = sem("vec_in")
        sink_in = sem("sink_in")
        x_in = [sem("x_in0"), sem("x_in1")]
        a0_in = [sem(f"a0_in{i}") for i in range(4)]
        w_in = [sem("w_in0"), sem("w_in1")]
        hi_done = sem("hi_done")
        lo_done = sem("lo_done")
        w_used = sem("w_used")
        freed = {"a": sem("freed_a"), "d": sem("freed_d")}
        mod_copied, mod_turned, bias_in = sem("mod_copied"), sem("mod_turned"), sem("bias_in")
        ct_rows, ct_ps, ct_ready = sem("ct_rows"), sem("ct_ps"), sem("ct_ready")
        ct_tanh, ct_full = sem("ct_tanh"), sem("ct_full")
        vec_ps, g_ready = sem("vec_ps"), sem("g_ready")
        xt_done = sem("xt_done")
        xe_a, xe_d = sem("xe_a"), sem("xe_d")
        sq_made, sq_used = sem("sq_made"), sem("sq_used")
        ms_ready, rt_ready = sem("ms_ready"), sem("rt_ready")
        spilled, reloaded = sem("spilled"), sem("reloaded")
        x_ready = sem("x_ready")
        xs_done = sem("xs_done")
        A_ready = sem("A_ready")
        mod_applied = sem("mod_applied")
        hh_hi = sem("hh_hi")
        h_ready = sem("h_ready")
        dch, ach = sem("dch"), sem("ach")
        pads = sem("pads")
        tv_ready, tv_done = sem("tv_ready"), sem("tv_done")
        kv_stored = sem("kv_stored")
        ck_in, cv_in = sem("ck_in"), sem("cv_in")
        ck_ready, ck_done = sem("ck_ready"), sem("ck_done")
        ss_ready, smax_ready, sexp_ready, sp_ready = (sem("ss_ready"), sem("smax_ready"),
                                                      sem("sexp_ready"), sem("sp_ready"))
        ts_ready, pts_done, pvs_ready = sem("ts_ready"), sem("pts_done"), sem("pvs_ready")
        sc_ready, pmax_ready, pexp_ready, pn_ready = (sem("sc_ready"), sem("pmax_ready"),
                                                      sem("pexp_ready"), sem("pn_ready"))
        tr_ready, pt_done, pv_ready = sem("tr_ready"), sem("pt_done"), sem("pv_ready")
        om_done = sem("om_done")
        gl_in, gate_done = sem("gl_in"), sem("gate_done")
        gate_d, gate_a = sem("gate_d"), sem("gate_a")
        gate_ps, gate_v, gate_cols = sem("gate_ps"), sem("gate_v"), sem("gate_cols")
        tr1_ready, vt_done, wk_done, rb_done = sem("tr1_ready"), sem("vt_done"), sem("wk_done"), sem("rb_done")
        sc1_ready, arg_done, ab_done, emt_done = (sem("sc1_ready"), sem("arg_done"), sem("ab_done"),
                                                  sem("emt_done"))
        Dexp_done, P_done = sem("Dexp_done"), sem("P_done")
        G_ready, sb_done, S_done = sem("G_ready"), sem("sb_done"), sem("S_done")
        dsarg_done, dsexp_done, Ps_done = sem("dsarg_done"), sem("dsexp_done"), sem("Ps_done")
        num_ready, nums_ready, abs_done, abss_done = (sem("num_ready"), sem("nums_ready"),
                                                      sem("abs_done"), sem("abss_done"))
        hout_done, hsq_done = sem("hout_done"), sem("hsq_done")
        cu_ready, cnew_done, ss1_ready = sem("cu_ready"), sem("cnew_done"), sem("ss1_ready")
        ms1_done, rt1_done, head_done = sem("ms1_done"), sem("rt1_done"), sem("head_done")
        th_done = sem("th_done")
        cs_in, cs_out, Sp_out = sem("cs_in"), sem("cs_out"), sem("Sp_out")
        nT_ps, nT_done = sem("nT_ps"), sem("nT_done")
        fin_ready, fin_a, fin_d = sem("fin_ready"), sem("fin_a"), sem("fin_d")
        out_done = sem("out_done")
        y_out = [sem("y_out0"), sem("y_out1")]

        def freed_at(ph, it, e):
            names = [p for p, _, _ in PHASES]
            while e < 0:
                r, c = it
                if r is None and c == 0:
                    ph = names[names.index(ph) - 1]
                    it = (None, ITERS[ph] - 1)
                else:
                    it = (r, c - 1)
                e += len(KINDS[ph])
            w = OWNER[KINDS[ph][e]]
            per = sum(OWNER[k] == w for k in KINDS[ph])
            upto = sum(OWNER[k] == w for k in KINDS[ph][:e + 1])
            return freed[w], val(FREED0[w][ph], per, it, upto)

        def unit_no(ph, it, e, j=0):
            ks = KINDS[ph]
            return val(UNIT0[ph], sum(UNITS[k] for k in ks), it, sum(UNITS[k] for k in ks[:e]) + j)

        def ended(ph, it, e):
            return unit_no(ph, it, e, UNITS[KINDS[ph][e]])

        def slot_of(ph, e, j=0):
            return (UNIT0[ph] + sum(UNITS[k] for k in KINDS[ph][:e]) + j) % 2

        def pair_of(ph, e):
            return (ENTRY0[ph] + e) % 2

        def landed_at(ph, it, e, j=0):
            ks = KINDS[ph]
            per = sum(UNITS[k] for k in ks)
            at = UNIT0[ph] + sum(UNITS[k] for k in ks[:e]) + j - RAW0
            r, c = it
            n = 16 * ((at + c * per) // 2 + 1)
            return n if r is None else r * (8 * per) + n

        def pj(pair, parts=slice(0, P)):
            return PJ[parts, 2 * pair:2 * pair + 2, 0:HT]

        def two(ap):
            return ap.rearrange("p (a t) -> p a t", a=2)

        def per_seq(ap):
            return ap.unsqueeze(3).broadcast_to([P, ap.shape[1], NB, ND])

        def ada_index(it, i):
            return val(8, 4, it, i)

        block = ctx.enter_context(nc.Block())

        @block.sync
        def _(sp):
            ada = w_ada.rearrange("l (k p) n -> p l k n", p=P)
            win0 = w_in_attn[0].rearrange("(k p) n -> p k n", p=P)
            win1 = w_in_mlstm[0].rearrange("(k p) n -> p k n", p=P)
            wout = [w_out_attn[0].rearrange("(k p) n -> p k n", p=P),
                    w_out_mlstm[0].rearrange("(k p) n -> p k n", p=P)]
            ROW4 = dict(k=4)

            for u in range(32):
                if u >= 4:
                    sp.wait_ge(lo_done, u - 3)
                slot = obuf[:, 4 * (u % 4):4 * (u % 4) + 4, 0:512]
                sp.dma_start(slot, ada[:, 0, 4 * (u % 4):4 * (u % 4) + 4,
                                       512 * (u // 4):512 * (u // 4) + 512]).then_inc(a0_in[u % 4], 16)

            def load(ph, it, e, j, src, dst_cols=D):
                s = slot_of(ph, e, j)
                split = fixed(sp, unit_no(ph, it, e, j - 1))
                sp.wait_ge(xt_done, 5)
                sp.wait_ge(lo_done, split)
                k = src.shape[1]
                sp.dma_start(raw[s][:, 0:dst_cols].rearrange("p (k n) -> p k n", k=k), src)\
                    .then_inc(w_in[s], 16)

            def layer0(it):
                r, c = it
                g = c if r is None else r + c
                nz = nq = na = 0
                for e, kind in enumerate(L0K):
                    if kind == "A":
                        for j in range(4):
                            if r is None and c == 0:
                                src = ada[:, 0, 4 * j:4 * j + 4, (8 + na) * 512:(9 + na) * 512]
                            else:
                                cg = (g - 1) * 2048 + na * 512
                                src = ada[:, 1, 4 * j:4 * j + 4, ds(cg, 512)]
                            load("l0", it, e, j, src)
                        na += 1
                        continue
                    if kind == "Z":
                        col = g * 512 + (3072 + 128 * nz)
                        nz += 1
                    elif kind == "Q":
                        col = g * 512 + 128 * nq
                        nq += 1
                    elif kind == "K":
                        col = g * 128 + 2048
                    else:
                        col = g * 128 + 2560
                    load("l0", it, e, 0, win0[:, :, ds(col, P)])

            sp.wait_ge(xt_done, 5)
            layer0((None, 0))
            with sp.Fori(0, GR - 1) as r:
                layer0((r, 1))

            def spill():
                sp.dma_start(x_spill, xflat).then_inc(spilled, 16)

            def out_units(ph, w):
                load(ph, (None, 0), 0, 0, w[:, :, 0:P])
                load(ph, (None, 0), 1, 0, w[:, :, P:2 * P])
                with sp.Fori(0, KT // 2 - 1) as r:
                    for i in range(2):
                        s = slot_of(ph, i)
                        sp.wait_ge(xt_done, 5)
                        sp.wait_ge(lo_done, r * 2 + (UNIT0[ph] + 2 + i - 1))
                        sp.dma_start(raw[s][:, :].rearrange("p (k n) -> p k n", k=KT),
                                     w[:, :, ds(r * 256 + (256 + 128 * i), P)]).then_inc(w_in[s], 16)

            out_units("out0", wout[0])
            load("gate", (None, 0), 0, 0, win1[:, :, 8192:8208], KT * 16)

            def layer1(it):
                r, c = it
                h = c if r is None else r + c
                seen = dict.fromkeys("ZOQKV", 0)
                start = dict(Q=0, K=1024, V=2048, O=4096, Z=6144)
                for e, kind in enumerate(L1K):
                    width = P if kind in "QK" else DV
                    load("l1", it, e, 0, win1[:, :, ds(h * width + (start[kind] + P * seen[kind]), P)])
                    seen[kind] += 1

            layer1((None, 0))
            with sp.Fori(0, MH - 1) as r:
                layer1((r, 1))
            out_units("out1", wout[1])

        @block.gpsimd
        def _(pool):
            bada = b_ada.rearrange("l n -> (l n)").unsqueeze(0)
            brow = misc[50:51, 0:512]

            def bias(a, first=False):
                if not first:
                    pool.wait_ge(mod_turned, a)
                pool.dma_start(brow, bada[:, ds(a * 512, 512)]).then_inc(bias_in, 16)

            for t in range(5):
                if t >= 2:
                    pool.wait_ge(xt_done, t - 1)
                if t < 4:
                    pool.dma_start(raw[t % 2][:, :], x_prompt[0, P * t:P * t + P, :]).then_inc(x_in[t % 2], 16)
                else:
                    pool.dma_start(raw[0][0:TS, :], x_sample.rearrange("b t d -> (b t) d"))\
                        .then_inc(x_in[0], 16)
                if t:
                    bias(t - 1, t == 1)
                if t == 1:
                    pool.dma_start(nsink[:, 0:QH], sinks.broadcast_to([P, QH])).then_inc(sink_in, 16)
                    for a in range(2):
                        for bl in range(2):
                            src = sinks.rearrange("o (m a l h) -> (o a l) m h", m=GR, a=2, l=2)[2 * a + bl]
                            p0 = 64 * a + 32 * bl
                            for h in range(2):
                                dst = nsink[p0:p0 + 32, QH + 4 * h:QH + 4 * h + 4]
                                pool.dma_start(dst, src[:, h:h + 1].rearrange("m h -> h m").broadcast_to([32, GR]), **SLOW)\
                                    .then_inc(sink_in, 16)
            for a in range(4, 8):
                bias(a)
            pool.dma_start(nk_s[0, :, 0:WIN - ND], cache_k[0, :, ND:WIN]).then_inc(kv_stored, 16)
            pool.dma_start(nv_s[0, :, 0:WIN - ND], cache_v[0, :, ND:WIN]).then_inc(kv_stored, 16)
            pool.wait_ge(xe_a, 10)
            pool.wait_ge(xe_d, 10)
            pool.dma_start(x_spill, xflat).then_inc(spilled, 16)
            pool.wait_ge(h_ready, KT)
            pool.dma_start(area(A0, "negd"), const[:, C_NEGD:C_NEGD + 768]).then_inc(mask_in, 16)
            pool.dma_start(area(A0, "negs"), const[:, C_NEGS:C_NEGS + 1056]).then_inc(mask_in, 16)

            def caches(g):
                pool.dma_start(ckraw, cache_k[0].rearrange("b w h d -> w b (h d)")[:, :, ds(g * P, P)])\
                    .then_inc(ck_in, 16)
                pool.dma_start(cv, cache_v[0].rearrange("b w h d -> w b (h d)")[:, :, ds(g * P, P)])\
                    .then_inc(cv_in, 16)

            def store_kv(it):
                r, c = it
                m = c if r is None else r + c
                pool.wait_ge(h_ready, KT)
                pool.wait_ge(tv_done, val(0, 4, it, 4))
                kc = slice(None)
                flat = "o b w h d -> (o b) w (h d)"
                pool.dma_start(nk_p.rearrange(flat)[0][:, ds(m * P, P)], kout).then_inc(kv_stored, 16)
                pool.dma_start(nv_p.rearrange(flat)[0][:, ds(m * P, P)], vtok[:, 384:512]).then_inc(kv_stored, 16)
                for dst, col in ((nv_s, 0), (nk_s, P)):
                    d = dst.rearrange(flat)[:, WIN - ND:WIN, ds(m * P, P)]
                    pool.dma_start(d, vks[0:TS, col:col + P]).then_inc(kv_stored, 16)

            caches(0)
            for i in range(4):
                bias(8 + i)

            def l0_rest(it):
                store_kv(it)
                r, c = it
                for i in range(4):
                    pool.wait_ge(h_ready, KT)
                    pool.wait_ge(mod_turned, val(8, 4, (it[0], it[1] + 1), i))
                    pool.dma_start(brow, bada[:, ds(val(8, 4, (it[0], it[1] + 1), i) * 512, 512)])\
                        .then_inc(bias_in, 16)
                    if i == 1:
                        pool.wait_ge(h_ready, KT)
                        pool.wait_ge(pvs_ready, val(0, 2, it, 2))
                        caches(r + (c + 1))

            with pool.Fori(0, GR - 1) as r:
                l0_rest((r, 0))
            store_kv((None, GR - 1))
            pool.wait_ge(kv_stored, 32 + 64 * GR)
            pool.wait_ge(om_done, 1 + 18 * GR)
            pool.dma_start(xflat, x_spill).then_inc(reloaded, 16)
            pool.wait_ge(x_ready, 1)
            pool.dma_start(x_spill, xflat).then_inc(spilled, 16)
            pool.wait_ge(h_ready, 3 * KT)
            pool.dma_start(cm, const[:, C_CM:C_CM + 128]).then_inc(gl_in, 16)
            pool.dma_start(sm, const[:, C_SM:C_SM + 32]).then_inc(gl_in, 16)
            pool.dma_start(bm, const[:, C_BM:C_BM + 8]).then_inc(gl_in, 16)
            pool.dma_start(m0s, state_m[0].rearrange("b h -> h b"), **SLOW).then_inc(gl_in, 16)
            pool.dma_start(bif, b_if_mlstm.rearrange("o (g h) -> h (o g)", g=2), **SLOW).then_inc(gl_in, 16)
            pool.dma_start(nrow, state_n[0].rearrange("b h d -> (b h) d")).then_inc(gl_in, 16)
            C_in = state_C[0].rearrange("b h k e -> h k b e")
            C_out = nC_s[0].rearrange("b h k e -> h k b e")
            pool.dma_start(cs, C_in[0]).then_inc(cs_in, 16)
            pool.wait_ge(gate_done, 1)
            pool.dma_start(nm_p.rearrange("o b h -> h (o b)"), R[:, 2, TP - 1:TP], **SLOW).then_inc(Sp_out, 16)
            pool.dma_start(nm_s[0].rearrange("b h -> h b"), R[:, 2, TP:T].rearrange("p (b t) -> p b t", t=ND)[:, :, 3], **SLOW)\
                .then_inc(out_done, 16)

            def states(it, more):
                r, c = it
                h = c if r is None else r + c
                pool.wait_ge(gate_done, 1)
                pool.wait_ge(S_done, val(0, 1, it, 1))
                pool.dma_start(nC_p.rearrange("o b h k e -> (o b h) k e")[ds(h, 1)].rearrange("o k e -> (o k) e"),
                               S[:, 3, :]).then_inc(Sp_out, 16)
                new, at = fixed(pool, val(0, NB, it, NB)), fixed(pool, h)
                pool.wait_ge(gate_done, 1)
                pool.wait_ge(cnew_done, new)
                pool.dma_start(C_out[ds(at, 1)].rearrange("o k b e -> (o k) b e"), cs).then_inc(cs_out, 16)
                if more:
                    pool.wait_ge(gate_done, 1)
                    pool.wait_ge(cs_out, val(0, 16, it, 16))
                    pool.dma_start(cs, C_in[ds(h + 1, 1)].rearrange("o k b e -> (o k) b e")).then_inc(cs_in, 16)

            with pool.Fori(0, MH - 1) as r:
                states((r, 0), True)
            states((None, MH - 1), False)
            pool.wait_ge(nT_done, 1)
            nrow2 = area(A1, "wk")[0:72, 0:P]
            pool.dma_start(nn_s[0].rearrange("b h d -> (b h) d"), nrow2[0:64, :]).then_inc(out_done, 16)
            pool.dma_start(nn_p.rearrange("o b h d -> (o b h) d"), nrow2[64:72, :]).then_inc(out_done, 16)
            pool.wait_ge(out_done, 48)
            pool.wait_ge(cs_out, 16 * MH)
            pool.wait_ge(Sp_out, 16 + 16 * MH)
            pool.wait_ge(head_done, 1 + MH)
            pool.wait_ge(spilled, 32)
            pool.dma_start(xflat, x_spill).then_inc(reloaded, 16)
            for t in range(5):
                pool.wait_ge(fin_a, 2 * (t + 1))
                pool.wait_ge(fin_d, 2 * (t + 1))
                dst = y_prompt[0, P * t:P * t + P, :] if t < 4 else y_sample.rearrange("b t d -> (b t) d")
                n = P if t < 4 else TS
                pool.dma_start(dst, raw[t % 2][0:n, :]).then_inc(y_out[t % 2], 16)
            pool.wait_ge(y_out[0], 48)
            pool.wait_ge(y_out[1], 32)

        @block.tensor
        def _(pe):
            mm, tr = pe.matmul, pe.transpose

            def ada_products(ph, it, e, mid=None):
                pair = pair_of(ph, e)
                for j in range(4):
                    s = slot_of(ph, e, j)
                    pe.wait_ge(lo_done, unit_no(ph, it, e, j) + 1)
                    for k in range(4):
                        lhsT = cT[:, (4 * j + k) * 18:(4 * j + k) * 18 + P]
                        for w in (w_hi, w_lo):
                            last = mm(PJ[:, 2 * pair, :], lhsT, w[s][:, k * 512:k * 512 + 512],
                                      start=(j == 0 and k == 0 and w is w_hi),
                                      stop=(j == 3 and k == 3 and w is w_lo))
                    last.then_inc(w_used, 1)
                    if j == 0 and mid:
                        mid()

            def ada_turn(ph, it, e, n):
                pair = pair_of(ph, e)
                pe.wait_ge(mod_copied, n + 1)
                pe.wait_ge(bias_in, n * 16 + 16)
                for j in range(4):
                    last = mm(PJ[:, 2 * pair + 1, 9 * j:9 * j + 9], misc[32:51, P * j:P * j + P],
                              fix[32:51, C_SEL:C_SEL + NSEQ], start=True, stop=True)
                last.then_inc(mod_turned, 1)

            def entry(ph, it, e, mid, h_base=None):
                s, pair = slot_of(ph, e), pair_of(ph, e)
                se, v = freed_at(ph, it, e - 2)
                pe.wait_ge(se, v)
                if KINDS[ph][e] == "A":
                    ada_products(ph, it, e, mid)
                    return
                pe.wait_ge(lo_done, unit_no(ph, it, e) + 1)
                for k in range(KT):
                    if h_base is not None:
                        pe.wait_ge(h_ready, h_base + k + 1)
                    hi = w_hi[s][:, P * k:P * k + P]
                    lo = w_lo[s][:, P * k:P * k + P]
                    for n, (w, h) in enumerate(((hi, h_hi), (hi, h_lo), (lo, h_hi))):
                        for f in range(2):
                            last = mm(PJ[:, 2 * pair + f, 0:HT], w, h[:, k, HT * f:HT * f + HT],
                                      start=(k == 0 and n == 0), stop=(k == KT - 1 and n == 2))
                    if k == KT // 2 - 1:
                        mid()
                last.then_inc(w_used, 1)

            pe.wait_ge(const_in, 16)
            pe.wait_ge(vec_in, 48)
            tr(MX[:, 2, 0:80], gvec, ident[0:80, 0:80]).then_inc(vec_ps, 1)
            pe.wait_ge(ct_rows, 1)
            for k in range(KT):
                last = tr(MX[:, 3, NSEQ * k:NSEQ * k + NSEQ], c_rows[:, P * k:P * k + P], ident[0:NSEQ, 0:NSEQ])
            last.then_inc(ct_ps, 1)
            pe.wait_ge(ct_ready, 1)

            def turn_x(t):
                n = P if t < 4 else TS
                pe.wait_ge(x_in[t % 2], 16 * (t // 2 + 1))
                if t:
                    pe.wait_ge(xe_a, 2 * t)
                    pe.wait_ge(xe_d, 2 * t)
                else:
                    pe.wait_ge(g_ready, 1)
                for k in range(KT):
                    last = tr(MX[:, k // 4, n * (k % 4):n * (k % 4) + n], raw[t % 2][0:n, P * k:P * k + P],
                              ident[0:n, 0:n])
                last.then_inc(xt_done, 1)

            def sums(base):
                for k in range(KT):
                    pe.wait_ge(sq_made, base + k + 1)
                    for f in range(2):
                        last = mm(MX[:, f, 0:HT], ones, sqb[:, k % 2, HT * f:HT * f + HT],
                                  start=(k == 0), stop=(k == KT - 1))
                    last.then_inc(sq_used, 1)

            nop = lambda: None
            it0 = (None, 0)
            for e in range(8):
                if e >= 2:
                    se, v = freed_at("ada0", it0, e - 2)
                    pe.wait_ge(se, v)
                ada_products("ada0", it0, e)
                if e < 5:
                    turn_x(e)
                ada_turn("ada0", it0, e, e)
            pe.wait_ge(xe_a, 10)
            pe.wait_ge(xe_d, 10)
            sums(0)

            def kv_turn(m):
                se, v = freed_at("l0", m, 13)
                pe.wait_ge(se, v)
                pe.wait_ge(om_done, val(1, 18, m))
                for c in range(4):
                    tr(MX[:, 0, P * c:P * c + P], vT[:, P * c:P * c + P], ident)
                tr(MX[:, 1, 0:P], kT[:, P + 384:P + 512], ident)
                tr(MX[0:TS, 1, P:2 * P], vT[:, TP:T], ident)
                tr(MX[0:TS, 1, 2 * P:3 * P], kT[:, P + TP:P + T], ident).then_inc(tv_ready, 1)
                pe.wait_ge(ck_in, val(0, 16, m, 16))
                for b in range(NB):
                    last = tr(MX[:, 2 + b // 4, P * (b % 4):P * (b % 4) + P], ckraw[:, b, :], ident)
                last.then_inc(ck_ready, 1)

            def sample_scores(m, half):
                if half == 0:
                    tv_all, ck_all = fixed(pe, val(0, 4, m, 4)), fixed(pe, val(0, 6, m, 6))
                    pe.wait_ge(pads, 2)
                    pe.wait_ge(tv_done, tv_all)
                    pe.wait_ge(ck_done, ck_all)
                hs = slice(64 * half, 64 * half + 64)
                for a in range(2):
                    ck, kk = (ckT, kT) if a == half else (ckS, kS)
                    lhsT = qS[hs, 64 * a:64 * a + 64]
                    out = slice(64 * a, 64 * a + 64)
                    for j in range(2):
                        mm(MX[out, j, :], lhsT, ck[hs, 512 * j:512 * j + 512], start=True, stop=True)
                    last = mm(MX[out, 2, 0:TS], lhsT, kk[hs, P + TP:P + T], start=True, stop=True)
                last.then_inc(ss_ready, 1)

            def sample_turn(m, half):
                pe.wait_ge(sp_ready, val(0, 2, m, half + 1))
                for b in range(NB):
                    tr(MX[:, b // 4, P * (b % 4):P * (b % 4) + P], SPs[:, P * b:P * b + P], ident)
                tr(MX[0:TS, 2, 0:P], SPs[:, 1024:1056], ident).then_inc(ts_ready, 1)

            def sample_pv(m, half):
                pe.wait_ge(pts_done, val(0, 4, m, 2 * half + 2))
                if half == 0:
                    pe.wait_ge(cv_in, val(0, 16, m, 16))
                out = slice(64 * half, 64 * half + 64)
                for a in range(2):
                    o = MX[out, 3, 64 * a:64 * a + 64]
                    for b in range(NB):
                        mm(o, cv[:, b, 64 * a:64 * a + 64], PTs[:, P * b + 64 * a:P * b + 64 * a + 64],
                           start=(b == 0), stop=False)
                    last = mm(o, vks[0:TS, 64 * a:64 * a + 64], PTn[:, 64 * a:64 * a + 64],
                              start=False, stop=True)
                last.then_inc(pvs_ready, 1)

            def step(x):
                return x // 4, x // 2 % 2, x % 2

            def scores(m, x):
                j, bp, half = step(x)
                hs = slice(64 * half, 64 * half + 64)
                kk = kT if j // 2 == half else kS
                for bl in range(2):
                    b = 2 * bp + bl
                    last = mm(MX[:, half, 256 * bl:256 * bl + 256], q0[hs, j, P * b:P * b + P],
                              kk[hs, P * b:P * b + 2 * P], start=True, stop=True)
                last.then_inc(sc_ready, 1)

            def p_turn(m, x):
                pe.wait_ge(pn_ready, val(0, 32, m, 2 * x + 2))
                for c in range(4):
                    last = tr(MX[:, 2, P * c:P * c + P], PP[x % 2][:, P * c:P * c + P], ident)
                last.then_inc(tr_ready, 1)

            def pv(m, x):
                j, bp, half = step(x)
                a = j // 2
                pe.wait_ge(pt_done, val(0, 16, m, x + 1))
                pe.wait_ge(om_done, val(1, 18, m, max(2, x + 1)))
                for bl in range(2):
                    b = 2 * bp + bl
                    o = MX[64 * half:64 * half + 64, 3, P * bl:P * bl + P]
                    for kb in range(2):
                        if b == 0 and kb == 0:
                            continue
                        last = mm(o, vtok[:, P * (b - 1 + kb) + 64 * a:P * (b - 1 + kb) + 64 * a + 64],
                                  PT[:, 256 * bl + P * kb:256 * bl + P * kb + P],
                                  start=(kb == 0 or b == 0), stop=(kb == 1))
                last.then_inc(pv_ready, 1)

            def attend(m, p):
                if p == 0:
                    kv_turn(m)
                if p in (2, 5):
                    if p == 5:
                        sample_pv(m, 0)
                    sample_scores(m, p // 3)
                if p in (4, 8):
                    sample_turn(m, p // 8)
                if p == 9:
                    sample_pv(m, 1)
                if 0 <= p - 13 < 16:
                    pv(m, p - 13)
                if 0 <= p - 12 < 16:
                    p_turn(m, p - 12)
                if 0 <= p - 10 < 16:
                    scores(m, p - 10)
                if p == 27:
                    pv(m, 15)

            def layer0(it, m, h_base=None):
                na = 0
                for e in range(len(L0K)):
                    def mid(e=e):
                        nonlocal na
                        if e and L0K[e - 1] == "A":
                            ada_turn("l0", it, e - 1, ada_index(it, na))
                            na += 1
                        if m is not None:
                            attend(m, 2 * e)
                    entry("l0", it, e, mid, h_base if e == 0 else None)
                    if m is not None:
                        attend(m, 2 * e + 1)

            layer0((None, 0), None, 0)
            with pe.Fori(0, GR - 1) as r:
                layer0((r, 1), (r, 0))
            for p in range(28):
                attend((None, GR - 1), p)

            def out_product(ph, h_base, sq_base):
                def square_sum(k, i, first=False, end=False):
                    pe.wait_ge(sq_made, k + 1)
                    for f in range(2):
                        last = mm(MX[:, f, 0:HT], ones, sqb[:, i % 2, HT * f:HT * f + HT],
                                  start=first, stop=end)
                    last.then_inc(sq_used, 1)

                entry(ph, it0, 0, nop, h_base)
                entry(ph, it0, 1, lambda: square_sum(sq_base, 0, True))
                with pe.Fori(0, KT // 2 - 1) as r:
                    for i in range(2):
                        s, pair = slot_of(ph, i), pair_of(ph, i)
                        pe.wait_ge(freed["a"], r * 2 + (FREED0["a"][ph] + 1 + i))
                        pe.wait_ge(lo_done, r * 2 + (UNIT0[ph] + 3 + i))
                        for k in range(KT):
                            hi = w_hi[s][:, P * k:P * k + P]
                            lo = w_lo[s][:, P * k:P * k + P]
                            for n, (w, h) in enumerate(((hi, h_hi), (hi, h_lo), (lo, h_hi))):
                                for f in range(2):
                                    last = mm(PJ[:, 2 * pair + f, 0:HT], w, h[:, k, HT * f:HT * f + HT],
                                              start=(k == 0 and n == 0), stop=(k == KT - 1 and n == 2))
                            if k == KT // 2 - 1:
                                square_sum(r * 2 + (sq_base + 1 + i), 1 + i)
                        last.then_inc(w_used, 1)
                square_sum(sq_base + KT - 1, 1, end=True)

            out_product("out0", KT, KT)
            sums(2 * KT)

            entry("gate", it0, 0, nop, 2 * KT)
            pe.wait_ge(gate_d, 1)
            for c in range(5):
                n = P if c < 4 else TS
                tr(MX[0:n, 0, 8 * c:8 * c + 8], Ub[:, P * c:P * c + n], ident[GP, 64:72])
                tr(MX[0:n, 1, 8 * c:8 * c + 8], Wr[:, P * c:P * c + n], ident[GP, 64:72])
            pe.wait_ge(gl_in, 96)
            tr(MX[:, 2, 0:64], nrow, ident[0:64, 0:64]).then_inc(gate_ps, 1)

            def memory(m, p):
                if p == 0:
                    pe.wait_ge(*freed_at("l1", m, 7))
                    pe.wait_ge(head_done, val(1, 1, m))
                    for bank, src in ((0, k1), (1, v1[:, 0, :]), (2, v1[:, 1, :])):
                        for c in range(4):
                            tr(MX[:, bank, P * c:P * c + P], src[:, P * c:P * c + P], ident)
                    for j, src in enumerate((k1, v1[:, 0, :], v1[:, 1, :])):
                        last = tr(MX[0:TS, 3, P * j:P * j + P], src[:, TP:T], ident)
                    last.then_inc(tr1_ready, 1)
                if p == 1:
                    pe.wait_ge(wk_done, val(0, 5, m, 5))
                    pe.wait_ge(vt_done, val(0, 3, m, 3))
                    pe.wait_ge(rb_done, val(0, 1, m, 1))
                    for c in range(4):
                        mm(MX[:, 0, P * c:P * c + P], k1[:, P * c:P * c + P], q1[:, P * c:P * c + P],
                           start=True, stop=True)
                    for j in range(3):
                        last = mm(MX[:, 1 + j, :], fix[BP, C_ONE:C_ONE + P], RB[:, j, 0:TP],
                                  start=True, stop=True)
                    last.then_inc(sc1_ready, 1)
                if p == 2:
                    pe.wait_ge(arg_done, val(0, 1, m, 1))
                    pe.wait_ge(ab_done, val(0, 1, m, 1))
                    pe.wait_ge(emt_done, val(0, 2, m, 1))
                    for c in range(4):
                        mm(MX[:, 1 + c // 2, DV * (c % 2):DV * (c % 2) + DV], wk[:, c, :], vt1[:, c, :],
                           start=True, stop=True)
                    for c in range(4):
                        mm(MX[:, 3, c:c + 1], wk[:, c, :], ones[:, 0:1], start=True, stop=True)
                    mm(MX[0:TS, 3, 64:64 + TS], k1[:, TP:T], q1[:, TP:T], start=True, stop=True)
                    mm(MX[:, 3, P:P + 3 * TS], fix[BP, C_ONE:C_ONE + P], RB[:, :, TP:T],
                       start=True, stop=True).then_inc(G_ready, 1)
                if p == 4:
                    pe.wait_ge(P_done, val(0, 1, m, 1))
                    pe.wait_ge(S_done, val(0, 1, m, 1))
                    for blk in range(2):
                        for c in range(4):
                            o = MX[:, blk, P * c:P * c + P]
                            mm(o, vt1[:, c, P * blk:P * blk + P], Dm[:, P * c:P * c + P],
                               start=True, stop=(c == 0))
                            if c:
                                mm(o, S[:, c - 1, P * blk:P * blk + P], qa[:, P * c:P * c + P],
                                   start=False, stop=True)
                    mm(MX[:, 2, :], ones, Dm[:, :], start=True, stop=False)
                    mm(MX[:, 2, P:TP], ones, qn[:, P:TP], start=False, stop=True).then_inc(num_ready, 1)
                if p == 5:
                    pe.wait_ge(Ps_done, val(0, 1, m, 1))
                    pe.wait_ge(cs_in, val(0, 16, m, 16))
                    for blk in range(2):
                        mm(MX[:, 3, TS * blk:TS * blk + TS], vs[:, P * blk:P * blk + P], Ds[0:TS, :],
                           start=True, stop=False)
                        for b in range(NB):
                            mm(MX[:, 3, TS * blk + ND * b:TS * blk + ND * b + ND],
                               cs[:, b, P * blk:P * blk + P], qa[:, TP + ND * b:TP + ND * b + ND],
                               start=False, stop=(b == NB - 1))
                    mm(MX[:, 3, 64:64 + TS], ones[0:TS, :], Ds[0:TS, :], start=True, stop=False)
                    mm(MX[:, 3, 64:64 + TS], ones, qn[:, TP:T], start=False, stop=True)\
                        .then_inc(nums_ready, 1)
                if p == 7:
                    pe.wait_ge(hout_done, val(0, 1, m, 1))
                    for b in range(NB):
                        last = mm(MX[:, b // 2, DV * (b % 2):DV * (b % 2) + DV], wks[:, b, :], vs,
                                  start=True, stop=True)
                    last.then_inc(cu_ready, 1)
                if p == 8:
                    pe.wait_ge(cnew_done, val(0, NB, m, NB))
                    pe.wait_ge(hsq_done, val(0, 2, m, 2))
                    for b in range(NB):
                        mm(MX[:, 0, b:b + 1], wks[:, b, :], ones[0:TS, 0:1], start=True, stop=True)
                    for f in range(2):
                        for blk in range(2):
                            last = mm(MX[:, 1 + f, 0:HT], ones, hsq[:, blk, HT * f:HT * f + HT],
                                      start=(blk == 0), stop=(blk == 1))
                    last.then_inc(ss1_ready, 1)

            def layer1(it, m):
                for e in range(len(L1K)):
                    entry("l1", it, e, (lambda e=e: memory(m, 2 * e)) if m is not None else nop)
                    if m is not None:
                        memory(m, 2 * e + 1)

            layer1((None, 0), None)
            pe.wait_ge(gate_cols, 1)
            with pe.Fori(0, MH - 1) as r:
                layer1((r, 1), (r, 0))
            for p in range(16):
                memory((None, MH - 1), p)
            pe.wait_ge(head_done, 1 + MH)
            tr(MX[0:72, 0, 0:P], nout, ident).then_inc(nT_ps, 1)
            pe.wait_ge(nT_done, 1)
            out_product("out1", 3 * KT, 3 * KT)

            pe.wait_ge(x_ready, 2)
            for t in range(5):
                n = P if t < 4 else TS
                if t:
                    pe.wait_ge(fin_a, 2 * t)
                    pe.wait_ge(fin_d, 2 * t)
                for k in range(KT):
                    last = tr(MX[0:n, k // 4, P * (k % 4):P * (k % 4) + P], xw[:, k, P * t:P * t + n], ident)
                last.then_inc(fin_ready, 1)

        @block.scalar
        def _(act):
            chain = Chain(act, ach)
            fn = act.activation
            it0 = (None, 0)

            act.dma_start(fix[:, :], const[:, 0:C_FIX]).then_inc(const_in, 16)
            act.dma_start(c_rows[0:1, :], c_prompt).then_inc(c_in, 16)
            act.dma_start(c_rows[1:NSEQ, :], c_sample).then_inc(c_in, 16)
            act.dma_start(gvec[0:32, :], g_pre.rearrange("l (k p) -> (l k) p", p=P)).then_inc(vec_in, 16)
            act.dma_start(gvec[32:64, :], g_post.rearrange("l (k p) -> (l k) p", p=P)).then_inc(vec_in, 16)
            act.dma_start(gvec[64:80, :], g_head_mlstm.rearrange("o h (k p) -> (o h k) p", p=P)).then_inc(vec_in, 16)
            act.wait_ge(c_in, 32)
            fn(c_tanh, c_rows, ACT.Tanh, scale=0.5).then_inc(ct_tanh, 1)
            act.wait_ge(ct_ps, 1)
            act.wait_ge(const_in, 16)
            fn(c_full, MX[:, 3, 0:KT * NSEQ], ACT.Copy).then_inc(ct_full, 1)

            def round_hi(ph, it, e, j=0):
                s = slot_of(ph, e, j)
                if ph == "ada0":
                    u = 4 * e + j
                    act.wait_ge(a0_in[u % 4], 16 * (u // 4 + 1))
                    if u >= 2:
                        act.wait_ge(w_used, u - 1)
                    fn(w_hi[s][:, :].rearrange("p (k n) -> p k n", k=4),
                       obuf[:, 4 * (u % 4):4 * (u % 4) + 4, 0:512], ACT.Copy).then_inc(hi_done, 1)
                    return
                act.wait_ge(w_in[s], landed_at(ph, it, e, j))
                act.wait_ge(w_used, unit_no(ph, it, e, j - 1))
                if ph == "gate":
                    fn(w_hi[s][:, :].rearrange("p (k a n) -> p k a n", k=KT, n=32)[:, :, 0:2, 0:8],
                       raw[s][:, 0:KT * 16].rearrange("p (k a n) -> p k a n", k=KT, n=8),
                       ACT.Copy).then_inc(hi_done, 1)
                    return
                fn(w_hi[s][:, :], raw[s][:, :], ACT.Copy).then_inc(hi_done, 1)

            def mod_copy(ph, e, n, it):
                act.wait_ge(w_used, ended(ph, it, e))
                if ph != "ada0" or n:
                    act.wait_ge(mod_turned, n)
                fn(misc[32:50, 0:512], PJ[0:18, 2 * pair_of(ph, e), :], ACT.Copy).then_inc(mod_copied, 1)

            def squares(base, src=None):
                for k in range(KT):
                    if base + k >= 2:
                        act.wait_ge(sq_used, base + k - 1)
                    fn(sqb[:, k % 2, :], xw[:, k, :], ACT.Square).then_inc(sq_made, 1)

            def root(n):
                act.wait_ge(ms_ready, n)
                fn(rB, rB, ACT.Sqrt).then_inc(rt_ready, 1)

            def modulate(l, n):
                act.wait_ge(A_ready, l + 1)
                with act.Fori(0, KT) as k:
                    act.wait_ge(xs_done, k + (KT * l + 1))
                    xk = xw[:, ds(k, 1), 0:TP].rearrange("p o t -> p (o t)")
                    fn(xk, xk, ACT.Identity, scale=modT[:, ds(k + (48 * l + 16), 1), 0:1].rearrange("p a b -> p (a b)"),
                       bias=modT[:, ds(k + 48 * l, 1), 0:1].rearrange("p a b -> p (a b)")).then_inc(mod_applied, 1)
                    act.wait_ge(mod_applied, k + (KT * l + 1))
                    fn(h_hi[:, ds(k, 1), :].rearrange("p o t -> p (o t)"),
                       xw[:, ds(k, 1), :].rearrange("p o t -> p (o t)"), ACT.Copy).then_inc(hh_hi, 1)

            def split_out():
                with act.Fori(0, KT) as k:
                    fn(h_hi[:, ds(k, 1), :].rearrange("p o t -> p (o t)"),
                       obuf[:, ds(k, 1), :].rearrange("p o t -> p (o t)"), ACT.Copy).then_inc(hh_hi, 1)

            for e in range(8):
                for j in range(4):
                    round_hi("ada0", it0, e, j)
                if e < 5:
                    n = P if e < 4 else TS
                    act.wait_ge(xt_done, e + 1)
                    act.wait_ge(ct_ready, 1)
                    for b in range(2):
                        fn(xw[:, 4 * b:4 * b + 4, P * e:P * e + n],
                           MX[:, b, 0:4 * n].rearrange("p (k t) -> p k t", k=4), ACT.Copy).then_inc(xe_a, 1)
                mod_copy("ada0", e, e, it0)
            act.wait_ge(xe_a, 10)
            act.wait_ge(xe_d, 10)
            round_hi("l0", it0, 0)
            squares(0)
            root(1)
            modulate(0, 0)

            def attend(m, p):
                if p == 0:
                    act.wait_ge(tv_ready, val(0, 1, m, 1))
                    act.wait_ge(kv_stored, val(32, 64, m))
                    fn(vtok, MX[:, 0, :], ACT.Copy).then_inc(tv_done, 1)
                    fn(kout, MX[:, 1, 0:P], ACT.Copy).then_inc(tv_done, 1)
                    fn(vks[0:TS, 0:P], MX[0:TS, 1, P:2 * P], ACT.Copy).then_inc(tv_done, 1)
                    fn(vks[0:TS, P:2 * P], MX[0:TS, 1, 2 * P:3 * P], ACT.Copy).then_inc(tv_done, 1)
                if p in (2, 5):
                    half = p // 3
                    act.wait_ge(smax_ready, val(0, 2, m, half + 1))
                    fn(SPs, SPs, ACT.Exp, bias=st[:, 1:2], accum_out=st[:, 2:3]).then_inc(sexp_ready, 1)
                    fn(st[:, 4:5], st[:, 3:4], ACT.Exp).then_inc(sexp_ready, 1)
                if p in (4, 8):
                    half = p // 8
                    act.wait_ge(ts_ready, val(0, 2, m, half + 1))
                    fn(PTs, MX[:, 0:2, :].rearrange("p a t -> p (a t)"), ACT.Copy).then_inc(pts_done, 1)
                    fn(PTn, MX[0:TS, 2, 0:P], ACT.Copy).then_inc(pts_done, 1)
                if 0 <= p - 12 < 16:
                    x = p - 12
                    act.wait_ge(tr_ready, val(0, 16, m, x + 1))
                    fn(PT, MX[:, 2, :], ACT.Copy).then_inc(pt_done, 1)
                if 0 <= p - 10 < 16:
                    x = p - 10
                    o = 8 + 16 * (x % 2)
                    act.wait_ge(pmax_ready, val(0, 16, m, x + 1))
                    for bl in range(2):
                        pb = PP[x % 2][:, 256 * bl:256 * bl + 256]
                        fn(pb, pb, ACT.Exp, bias=st[:, o + 2 + bl:o + 3 + bl],
                           accum_out=st[:, o + 6 + bl:o + 7 + bl]).then_inc(pexp_ready, 1)
                    fn(st[:, o + 8:o + 10], st[:, o + 4:o + 6], ACT.Exp).then_inc(pexp_ready, 1)

            def empty0(it, m, e, nq, nz):
                kind, pair = L0K[e], pair_of("l0", e)
                act.wait_ge(w_used, ended("l0", it, e))
                r, c = it
                g = c if r is None else r + c
                if kind == "Z":
                    fn(obuf[:, ds(g * 4 + nz, 1), :].rearrange("p o (a t) -> p (o a) t", a=2), pj(pair),
                       ACT.Tanh, scale=0.5).then_inc(th_done, 1)
                if kind == "Q":
                    if m is not None:
                        act.wait_ge(sc_ready, val(0, 16, m, 4 * nq + 4))
                        act.wait_ge(ss_ready, val(0, 2, m, 2))
                    sc = float(HD) ** -0.5
                    chain(fn(q0[:, nq, 0:HT], PJ[:, 2 * pair, 0:HT], ACT.Copy, scale=sc))
                    chain(fn(q0[:, nq, HT:TP], PJ[:, 2 * pair + 1, 0:TP - HT], ACT.Copy, scale=sc))
                    fn(qS[:, TS * nq:TS * nq + TS], PJ[:, 2 * pair + 1, TP - HT:HT], ACT.Copy,
                       scale=sc).then_inc(freed["a"], 1)
                if kind == "K":
                    if m is not None:
                        act.wait_ge(sc_ready, val(0, 16, m, 16))
                    chain(fn(two(kT[:, P:]), pj(pair), ACT.Copy))
                    chain(fn(two(kS[0:64, P:]), pj(pair, slice(64, 128)), ACT.Copy))
                    fn(two(kS[64:128, P:]), pj(pair, slice(0, 64)), ACT.Copy).then_inc(freed["a"], 1)
                if kind == "V":
                    fn(two(vT), pj(pair), ACT.Copy).then_inc(freed["a"], 1)

            def layer0(it, m):
                nq = nz = na = 0
                for e in range(len(L0K) + 1):
                    if e:
                        if L0K[e - 1] == "A":
                            mod_copy("l0", e - 1, ada_index(it, na), it)
                            na += 1
                        else:
                            empty0(it, m, e - 1, nq, nz)
                            nq += L0K[e - 1] == "Q"
                            nz += L0K[e - 1] == "Z"
                    if L0K[e:e + 1] == "A":
                        round_hi("l0", it, e, 1)
                    if m is not None and e:
                        attend(m, 2 * e - 1)
                    if L0K[e:e + 1] == "A":
                        round_hi("l0", it, e, 2)
                        round_hi("l0", it, e, 3)
                    if e + 1 < len(L0K):
                        round_hi("l0", it, e + 1)
                    if m is not None and e < len(L0K):
                        attend(m, 2 * e)

            layer0((None, 0), None)
            LOOP_A = 4 * 2 + 2
            with act.Fori(0, GR - 1) as r:
                chain.enter(r, LOOP_A)
                round_hi("l0", (r, 1), 0)
                layer0((r, 1), (r, 0))
            chain.leave(GR - 1)
            round_hi("out0", it0, 0)
            round_hi("out0", it0, 1)
            for p in range(28):
                attend((None, GR - 1), p)
            act.wait_ge(om_done, 1 + 18 * GR)
            split_out()

            def empty_y(ph, sq_base):
                def one(i, e, sqv):
                    pair = pair_of(ph, i)
                    act.wait_ge(w_used, e)
                    act.wait_ge(sq_used, sqv)
                    fn(two(sqb[:, i, :]), pj(pair), ACT.Square).then_inc(sq_made, 1)

                def copy(i, k):
                    fn(obuf[:, ds(k, 1), :].rearrange("p o (a t) -> p (o a) t", a=2), pj(pair_of(ph, i)),
                       ACT.Copy).then_inc(freed["a"], 1)

                with act.Fori(0, KT // 2 - 1) as r:
                    for i in range(2):
                        one(i, r * 2 + (UNIT0[ph] + 1 + i), r * 2 + (sq_base - 1 + i))
                        copy(i, r * 2 + i)
                        s = slot_of(ph, i)
                        act.wait_ge(w_in[s], r * 16 + landed_at(ph, it0, 2 + i))
                        act.wait_ge(w_used, r * 2 + (UNIT0[ph] + 1 + i))
                        fn(w_hi[s][:, :], raw[s][:, :], ACT.Copy).then_inc(hi_done, 1)
                for i in range(2):
                    one(i, UNIT0[ph] + KT - 1 + i, sq_base + KT - 3 + i)
                    copy(i, KT - 2 + i)

            empty_y("out0", KT)
            round_hi("gate", it0, 0)
            root(2)
            act.wait_ge(x_ready, 1)
            squares(2 * KT)
            root(3)
            modulate(1, 1)

            act.wait_ge(w_used, ended("gate", it0, 0))
            act.wait_ge(h_ready, 3 * KT)
            fn(two(LI), pj(pair_of("gate", 0), slice(0, 8)), ACT.Copy).then_inc(gate_a, 1)
            fn(two(LF), pj(pair_of("gate", 0), slice(32, 40)), ACT.Copy).then_inc(freed["a"], 1)
            round_hi("l1", it0, 0)
            act.wait_ge(gate_v, 1)
            chain(fn(Bc, Bc, ACT.Exp, scale=-1.0))
            fn(Bc, Bc, ACT.Ln, bias=1.0).then_inc(gate_a, 1)
            act.wait_ge(gate_v, 2)
            fn(R[:, 1, :], R[:, 1, :], ACT.Exp).then_inc(gate_a, 1)
            fn(Wr, Wr, ACT.Exp).then_inc(gate_a, 1)

            def memory(m, p):
                r, c = m
                h = c if r is None else r + c
                if p == 0:
                    act.wait_ge(tr1_ready, val(0, 1, m, 1))
                    for j in range(2):
                        fn(vt1[:, :, P * j:P * j + P], MX[:, 1 + j, :].rearrange("p (c e) -> p c e", c=4),
                           ACT.Copy).then_inc(vt_done, 1)
                    fn(vs, MX[0:TS, 3, P:3 * P], ACT.Copy).then_inc(vt_done, 1)
                if p == 1:
                    act.wait_ge(sc1_ready, val(0, 1, m, 1))
                    fn(aB, MX[:, 2, :], ACT.Copy).then_inc(ab_done, 1)
                    fn(emt[:, 0:TP], MX[:, 3, :], ACT.Exp, scale=-1.0).then_inc(emt_done, 1)
                    act.wait_ge(arg_done, val(0, 1, m, 1))
                    for ch in range(4):
                        dc = Dm[:, P * ch:P * ch + P]
                        fn(dc, dc, ACT.Exp, bias=Uc[:, ds(h + 8 * ch, 1)]).then_inc(Dexp_done, 1)
                if p == 2:
                    act.wait_ge(G_ready, val(0, 1, m, 1))
                    fn(sB, MX[:, 3, P:P + 3 * TS].rearrange("p (j t) -> p j t", j=3), ACT.Copy).then_inc(sb_done, 1)
                    act.wait_ge(dsarg_done, val(0, 1, m, 1))
                    fn(Ds[0:TS, :], Ds[0:TS, :], ACT.Exp, bias=Uc[0:TS, ds(h + 32, 1)]).then_inc(dsexp_done, 1)
                    fn(emt[:, TP:T], sB[:, 2, :], ACT.Exp, scale=-1.0).then_inc(emt_done, 1)
                if p == 4:
                    act.wait_ge(num_ready, val(0, 1, m, 1))
                    fn(Dm, MX[:, 2, :], ACT.Abs).then_inc(abs_done, 1)
                if p == 5:
                    act.wait_ge(nums_ready, val(0, 1, m, 1))
                    fn(qn[:, TP:T], MX[:, 3, 64:64 + TS], ACT.Abs).then_inc(abss_done, 1)
                    act.wait_ge(hout_done, val(0, 1, m, 1))
                    for blk in range(2):
                        fn(hsq[:, blk, :], hh[:, blk, :], ACT.Square).then_inc(hsq_done, 1)
                if p == 8:
                    act.wait_ge(ms1_done, val(0, 1, m, 1))
                    fn(qa, qa, ACT.Sqrt).then_inc(rt1_done, 1)

            def empty1(it, m, e, seen):
                kind, pair = L1K[e], pair_of("l1", e)
                act.wait_ge(w_used, ended("l1", it, e))
                r, c = it
                h = c if r is None else r + c
                if kind == "Z":
                    fn(obuf[:, ds(h * 2 + seen, 1), :].rearrange("p o (a t) -> p (o a) t", a=2), pj(pair),
                       ACT.Tanh, scale=0.5).then_inc(th_done, 1)
                if kind == "O":
                    fn(two(misc[:, :]), pj(pair), ACT.Tanh, scale=0.5).then_inc(th_done, 1)
                if kind in "QKV":
                    if m is not None:
                        if kind == "V":
                            act.wait_ge(ss1_ready, val(0, 1, m, 1))
                        else:
                            act.wait_ge(hout_done, val(0, 1, m, 1))
                    dst = {"Q": q1, "K": k1, "V": v1[:, seen, :]}[kind]
                    fn(two(dst), pj(pair), ACT.Copy,
                       scale=float(DK) ** -0.5 if kind == "Q" else 1.0).then_inc(freed["a"], 1)

            def layer1(it, m):
                seen = dict.fromkeys("ZOQKV", 0)
                for e in range(len(L1K) + 1):
                    if e:
                        empty1(it, m, e - 1, seen[L1K[e - 1]])
                        seen[L1K[e - 1]] += 1
                    if e + 1 < len(L1K):
                        round_hi("l1", it, e + 1)
                    if m is not None:
                        if e:
                            memory(m, 2 * e - 1)
                        if e < len(L1K):
                            memory(m, 2 * e)

            layer1((None, 0), None)
            with act.Fori(0, MH - 1) as r:
                round_hi("l1", (r, 1), 0)
                layer1((r, 1), (r, 0))
            round_hi("out1", it0, 0)
            round_hi("out1", it0, 1)
            for p in range(16):
                memory((None, MH - 1), p)
            act.wait_ge(head_done, 1 + MH)
            split_out()
            act.wait_ge(cs_out, 16 * MH)
            empty_y("out1", 3 * KT)
            root(4)
            for t in range(5):
                n = P if t < 4 else TS
                act.wait_ge(fin_ready, t + 1)
                if t >= 2:
                    act.wait_ge(y_out[t % 2], 16 * (t // 2))
                for b in range(2):
                    fn(raw[t % 2][0:n, 512 * b:512 * b + 512], MX[0:n, b, :], ACT.Copy).then_inc(fin_a, 1)

        @block.vector
        def _(dve):
            chain = Chain(dve, dch)
            tt, ts, stt, cp = dve.tensor_tensor, dve.tensor_scalar, dve.scalar_tensor_tensor, dve.tensor_copy
            it0 = (None, 0)

            chain(dve.memset(cT[:, :].bitcast(mybir.dt.uint32), 0))
            dve.memset(st[:, :], 0.0).then_inc(om_done, 1)
            dve.drain().then_inc(head_done, 1)
            dve.wait_ge(ct_tanh, 1)
            chain(stt(c_rows, c_tanh, 1.0, c_rows, ALU.add, ALU.mult))
            ts(c_rows, c_rows, 0.5, None, ALU.mult).then_inc(ct_rows, 1)
            dve.wait_ge(ct_full, 1)
            cv3 = c_full.rearrange("p (k s) -> p k s", k=KT)
            cT3 = cT[:, 0:KT * 18].rearrange("p (k s) -> p k s", k=KT)
            chain(cp(cT3[:, :, 0:NSEQ], cv3))
            tt(cT3[:, :, NSEQ:18], cv3, cT3[:, :, 0:NSEQ].bitcast(F32), ALU.subtract).then_inc(ct_ready, 1)
            dve.wait_ge(vec_ps, 1)
            cp(gT[:, :], MX[:, 2, 0:80]).then_inc(g_ready, 1)
            dve.wait_ge(g_ready, 1)
            chain(ts(gT[:, 64:80], gT[:, 64:80], 0.25, None, ALU.mult))

            def split_lo(ph, it, e, j=0):
                s = slot_of(ph, e, j)
                dve.wait_ge(hi_done, unit_no(ph, it, e, j) + 1)
                if ph == "ada0":
                    u = 4 * e + j
                    tt(w_lo[s][:, :].rearrange("p (k n) -> p k n", k=4),
                       obuf[:, 4 * (u % 4):4 * (u % 4) + 4, 0:512],
                       w_hi[s][:, :].rearrange("p (k n) -> p k n", k=4).bitcast(F32),
                       ALU.subtract).then_inc(lo_done, 1)
                elif ph == "gate":
                    view = "p (k a n) -> p k a n"
                    tt(w_lo[s][:, :].rearrange(view, k=KT, n=32)[:, :, 0:2, 0:8],
                       raw[s][:, 0:KT * 16].rearrange(view, k=KT, n=8),
                       w_hi[s][:, :].bitcast(F32).rearrange(view, k=KT, n=32)[:, :, 0:2, 0:8],
                       ALU.subtract).then_inc(lo_done, 1)
                else:
                    tt(w_lo[s][:, :], raw[s][:, :], w_hi[s][:, :].bitcast(F32), ALU.subtract)\
                        .then_inc(lo_done, 1)

            def mod_empty(ph, e, n):
                dve.wait_ge(mod_turned, n + 1)
                cp(modT[:, ds(n * 4, 4), :], PJ[:, 2 * pair_of(ph, e) + 1, 0:36].rearrange("p (k s) -> p k s", k=4))\
                    .then_inc(freed["d"], 1)

            def inv_rms(n):
                dve.wait_ge(sq_used, KT * n)
                ts(two(rB), MX[:, 0:2, 0:HT], 1.0 / D, EPS, ALU.mult, ALU.add).then_inc(ms_ready, 1)
                dve.wait_ge(rt_ready, n)
                chain(dve.reciprocal(rB, rB))

            def norm_split(l, n):
                inv_rms(n)
                dve.wait_ge(spilled, 16 * (l + 1))
                seq = "p k (b t) -> p k b t"
                xs = xw[:, :, TP:T]
                chain(tt(xs, xs, rB[:, TP:T].unsqueeze(1).broadcast_to([P, KT, TS]), ALU.mult))
                A = modT[:, 48 * l + 16:48 * l + 32, :]
                gp = gT[:, KT * l:KT * l + KT].unsqueeze(2).broadcast_to([P, KT, NSEQ])
                stt(A, A, 1.0, gp, ALU.add, ALU.mult).then_inc(A_ready, 1)
                dve.wait_ge(A_ready, l + 1)
                x4 = xs.rearrange(seq, t=ND)
                chain(tt(x4, x4, per_seq(A[:, :, 1:NSEQ]), ALU.mult))
                chain(tt(x4, x4, per_seq(modT[:, 48 * l:48 * l + 16, 1:NSEQ]), ALU.add))

                def scale(k):
                    xk = xw[:, ds(k, 1), 0:TP].rearrange("p o t -> p (o t)")
                    tt(xk, xk, rB[:, 0:TP], ALU.mult).then_inc(xs_done, 1)

                def low(k):
                    dve.wait_ge(hh_hi, k + (2 * KT * l + 1))
                    hb = h_hi[:, ds(k, 1), :].rearrange("p o t -> p (o t)").bitcast(F32)
                    tt(h_lo[:, ds(k, 1), :].rearrange("p o t -> p (o t)"),
                       xw[:, ds(k, 1), :].rearrange("p o t -> p (o t)"), hb, ALU.subtract).then_inc(h_ready, 1)

                scale(0)
                scale(1)
                with dve.Fori(0, KT - 2) as k:
                    scale(k + 2)
                    low(k)
                low(KT - 2)
                low(KT - 1)

            def split_out(n):
                with dve.Fori(0, KT) as k:
                    dve.wait_ge(hh_hi, k + (n * KT + 1))
                    hb = h_hi[:, ds(k, 1), :].rearrange("p o t -> p (o t)").bitcast(F32)
                    tt(h_lo[:, ds(k, 1), :].rearrange("p o t -> p (o t)"),
                       obuf[:, ds(k, 1), :].rearrange("p o t -> p (o t)"), hb, ALU.subtract).then_inc(h_ready, 1)

            for e in range(8):
                for j in range(4):
                    split_lo("ada0", it0, e, j)
                if e < 5:
                    n = P if e < 4 else TS
                    dve.wait_ge(xt_done, e + 1)
                    for b in range(2, 4):
                        cp(xw[:, 4 * b:4 * b + 4, P * e:P * e + n],
                           MX[:, b, 0:4 * n].rearrange("p (k t) -> p k t", k=4)).then_inc(xe_d, 1)
                mod_empty("ada0", e, e)
            split_lo("l0", it0, 0)
            dve.wait_ge(sink_in, 16 * 9)
            chain(ts(nsink[:, :], nsink[:, :], -1.0, None, ALU.mult))
            norm_split(0, 1)
            dve.wait_ge(h_ready, KT)
            dve.memset(kT[:, 0:P], 0.0).then_inc(pads, 1)
            dve.memset(kS[:, 0:P], 0.0).then_inc(pads, 1)
            dve.wait_ge(mask_in, 32)
            dve.wait_ge(pads, 2)

            def soft_sample(m, half):
                r, c = m
                g = c if r is None else r + c
                dve.wait_ge(ss_ready, val(0, 2, m, half + 1))
                slope = fix[:, ds(g * 2 + (C_SLS + half), 1)]
                nsk = nsink[:, ds(g + (QH + 4 * half), 1)]
                chain(stt(SPs[:, 0:1024], negs[:, 0:1024], slope, MX[:, 0:2, :].rearrange("p a t -> p (a t)"),
                          ALU.mult, ALU.add))
                chain(stt(SPs[:, 1024:1056], negs[:, 1024:1056], slope, MX[:, 2, 0:TS], ALU.mult, ALU.add))
                chain(dve.tensor_reduce(st[:, 0:1], SPs, AX, ALU.max, negate=True))
                chain(tt(st[:, 1:2], st[:, 0:1], nsk, ALU.min))
                tt(st[:, 3:4], st[:, 1:2], nsk, ALU.subtract).then_inc(smax_ready, 1)

            def norm_sample(m, half):
                dve.wait_ge(sexp_ready, val(0, 4, m, 2 * half + 2))
                chain(tt(st[:, 5:6], st[:, 2:3], st[:, 4:5], ALU.add))
                chain(dve.reciprocal(st[:, 6:7], st[:, 5:6]))
                ts(SPs, SPs, st[:, 6:7], 0.5, ALU.mult, ALU.mult).then_inc(sp_ready, 1)

            def gate_sample(m, half):
                r, c = m
                g = c if r is None else r + c
                dve.wait_ge(pvs_ready, val(0, 2, m, half + 1))
                hs = slice(64 * half, 64 * half + 64)
                ob = obuf[hs, ds(g * 4, 4), TP:T]
                tt(ob, ob, MX[hs, 3, 0:P].rearrange("p (k t) -> p k t", k=4), ALU.mult).then_inc(om_done, 1)

            def soft(m, x):
                r, c = m
                g = c if r is None else r + c
                j, bp, half = x // 4, x // 2 % 2, x % 2
                pb, o = PP[x % 2], 8 + 16 * (x % 2)
                dve.wait_ge(sc_ready, val(0, 16, m, x + 1))
                head = g * 8 + (2 * j + half)
                nsk = nsink[:, ds(head, 1)].broadcast_to([P, 2])
                chain(stt(pb, negd[:, 256 * bp:256 * bp + 512], fix[:, ds(head + C_SLP, 1)], MX[:, half, :],
                          ALU.mult, ALU.add))
                chain(dve.tensor_reduce(st[:, o:o + 2], pb.rearrange("p (b k) -> p b k", b=2), AX, ALU.max,
                                        negate=True))
                chain(tt(st[:, o + 2:o + 4], st[:, o:o + 2], nsk, ALU.min))
                tt(st[:, o + 4:o + 6], st[:, o + 2:o + 4], nsk, ALU.subtract).then_inc(pmax_ready, 1)

            def norm(m, x):
                pb, o = PP[x % 2], 8 + 16 * (x % 2)
                dve.wait_ge(pexp_ready, val(0, 48, m, 3 * x + 3))
                chain(tt(st[:, o + 10:o + 12], st[:, o + 6:o + 8], st[:, o + 8:o + 10], ALU.add))
                chain(dve.reciprocal(st[:, o + 12:o + 14], st[:, o + 10:o + 12]))
                for bl in range(2):
                    q = pb[:, 256 * bl:256 * bl + 256]
                    ts(q, q, st[:, o + 12 + bl:o + 13 + bl], 0.5, ALU.mult, ALU.mult).then_inc(pn_ready, 1)

            def gate_prompt(m, x):
                r, c = m
                g = c if r is None else r + c
                j, bp, half = x // 4, x // 2 % 2, x % 2
                dve.wait_ge(pv_ready, val(0, 16, m, x + 1))
                hs = slice(64 * half, 64 * half + 64)
                ob = obuf[hs, ds(g * 4 + j, 1), 256 * bp:256 * bp + 256].rearrange("p o t -> p (o t)")
                tt(ob, ob, MX[hs, 3, 0:256], ALU.mult).then_inc(om_done, 1)

            def attend(m, p):
                if p == 0:
                    dve.wait_ge(ck_ready, val(0, 1, m, 1))
                    for j in range(2):
                        cols = slice(512 * j, 512 * j + 512)
                        cp(ckT[:, cols], MX[:, 2 + j, :]).then_inc(ck_done, 1)
                        cp(ckS[0:64, cols], MX[64:128, 2 + j, :]).then_inc(ck_done, 1)
                        cp(ckS[64:128, cols], MX[0:64, 2 + j, :]).then_inc(ck_done, 1)
                if p == 5:
                    gate_sample(m, 0)
                if p in (2, 5):
                    soft_sample(m, p // 3)
                    norm_sample(m, p // 3)
                if p == 9:
                    gate_sample(m, 1)
                if 10 <= p < 26:
                    soft(m, p - 10)
                if p >= 13:
                    gate_prompt(m, p - 13)
                if 10 <= p < 26:
                    norm(m, p - 10)
                if p == 27:
                    gate_prompt(m, 15)

            def empty_z(ph, it, e, blk, nth):
                dve.wait_ge(th_done, nth)
                ob = obuf[:, ds(blk, 1), :].rearrange("p o (a t) -> p (o a) t", a=2)
                stt(ob, ob, 1.0, pj(pair_of(ph, e)), ALU.add, ALU.mult).then_inc(freed["d"], 1)

            def layer0(it, m):
                r, c = it
                g = c if r is None else r + c
                na = nz = 0
                for e in range(len(L0K) + 1):
                    if e:
                        if L0K[e - 1] == "Z":
                            empty_z("l0", it, e - 1, g * 4 + nz, val(0, 4, it, nz + 1))
                            nz += 1
                    if L0K[e:e + 1] == "A":
                        split_lo("l0", it, e, 1)
                    if m is not None and e:
                        attend(m, 2 * e - 1)
                    if e and L0K[e - 1] == "A":
                        mod_empty("l0", e - 1, ada_index(it, na))
                        na += 1
                    if L0K[e:e + 1] == "A":
                        split_lo("l0", it, e, 2)
                        split_lo("l0", it, e, 3)
                    if e + 1 < len(L0K):
                        split_lo("l0", it, e + 1)
                    if m is not None and e < len(L0K):
                        attend(m, 2 * e)

            LOOP_D = 2 * (4 + 2) + 16 * (3 + 2)
            layer0((None, 0), None)
            with dve.Fori(0, GR - 1) as r:
                chain.enter(r, LOOP_D)
                split_lo("l0", (r, 1), 0)
                layer0((r, 1), (r, 0))
            chain.leave(GR - 1)
            split_lo("out0", it0, 0)
            split_lo("out0", it0, 1)
            for p in range(28):
                attend((None, GR - 1), p)
            dve.wait_ge(om_done, 1 + 18 * GR)
            split_out(1)

            def out_lows(ph):
                with dve.Fori(0, KT // 2 - 1) as r:
                    for i in range(2):
                        s = slot_of(ph, i)
                        dve.wait_ge(hi_done, r * 2 + (UNIT0[ph] + 3 + i))
                        tt(w_lo[s][:, :], raw[s][:, :], w_hi[s][:, :].bitcast(F32), ALU.subtract)\
                            .then_inc(lo_done, 1)

            def residual(l, n):
                inv_rms(n)
                G = modT[:, 48 * l + 32:48 * l + 48, :]
                gp = gT[:, 32 + KT * l:32 + KT * l + KT].unsqueeze(2).broadcast_to([P, KT, NSEQ])
                chain(tt(G, G, gp, ALU.mult))
                dve.wait_ge(freed["a"], FREED0["a"]["out0" if l == 0 else "out1"] + KT)
                dve.wait_ge(reloaded, 16 * (l + 1))
                ys, xs = obuf[:, :, TP:T], xw[:, :, TP:T]
                chain(tt(ys, ys, rB[:, TP:T].unsqueeze(1).broadcast_to([P, KT, TS]), ALU.mult))
                y4 = ys.rearrange("p k (b t) -> p k b t", t=ND)
                chain(tt(y4, y4, per_seq(G[:, :, 1:NSEQ]), ALU.mult))
                chain(tt(xs, xs, ys, ALU.add))
                for k in range(KT):
                    chain(tt(obuf[:, k, 0:TP], obuf[:, k, 0:TP], rB[:, 0:TP], ALU.mult))
                    last = stt(xw[:, k, 0:TP], obuf[:, k, 0:TP], G[:, k, 0:1], xw[:, k, 0:TP], ALU.mult, ALU.add)
                    chain(last)
                dve.drain().then_inc(x_ready, 1)

            out_lows("out0")
            split_lo("gate", it0, 0)
            residual(0, 2)
            norm_split(1, 3)

            dve.wait_ge(gate_a, 1)
            dve.wait_ge(freed["a"], FREED0["a"]["gate"] + 1)
            dve.wait_ge(gl_in, 96)
            chain(ts(LI, LI, bif[:, 0:1], None, ALU.add))
            chain(ts(LF, LF, bif[:, 1:2], None, ALU.add))
            chain(ts(Bc, LF, -1.0, None, ALU.mult))
            tt(Bc, Bc, LF, ALU.max).then_inc(gate_v, 1)
            split_lo("l1", it0, 0)
            dve.wait_ge(gate_a, 2)
            chain(ts(LF, LF, 0.0, None, ALU.min))
            chain(tt(LF, LF, Bc, ALU.subtract))
            orow = fix[GP, C_ONE:C_ONE + P]
            for ch in range(4):
                cc = slice(P * ch, P * ch + P)
                chain(dve.tensor_tensor_scan(Bc[:, cc], orow, LF[:, cc], 0.0, ALU.mult, ALU.add))
            B4 = Bc[:, TP:T].rearrange("p (b t) -> p b t", t=ND)
            F4 = LF[:, TP:T].rearrange("p (b t) -> p b t", t=ND)
            chain(cp(B4[:, :, 0], F4[:, :, 0]))
            for t in range(1, ND):
                chain(tt(B4[:, :, t], B4[:, :, t - 1], F4[:, :, t], ALU.add))
            chain(tt(Ub, LI, Bc, ALU.subtract))
            chain(dve.memset(tg[:, 0:1], 0.0))
            for ch in range(4):
                cc = slice(P * ch, P * ch + P)
                chain(dve.tensor_tensor_scan(Mr[:, cc], orow, Ub[:, cc], tg[:, ch:ch + 1], ALU.mult, ALU.max))
                end = P * ch + P - 1
                chain(tt(tg[:, ch + 1:ch + 2], Bc[:, end:end + 1], Mr[:, end:end + 1], ALU.add))
                chain(ts(R[:, 1, cc], Mr[:, cc], tg[:, ch:ch + 1], -1.0, ALU.subtract, ALU.mult))
                chain(ts(Wr[:, cc], Ub[:, cc], Mr[:, end:end + 1], None, ALU.subtract))
            M4 = Mr[:, TP:T].rearrange("p (b t) -> p b t", t=ND)
            U4 = Ub[:, TP:T].rearrange("p (b t) -> p b t", t=ND)
            chain(tt(M4[:, :, 0], m0s, U4[:, :, 0], ALU.max))
            for t in range(1, ND):
                chain(tt(M4[:, :, t], M4[:, :, t - 1], U4[:, :, t], ALU.max))
            chain(tt(R[:, 1, TP:T].rearrange("p (b t) -> p b t", t=ND), m0s.unsqueeze(2).broadcast_to([MH, NB, ND]),
                     M4, ALU.subtract))
            chain(tt(Wr[:, TP:T].rearrange("p (b t) -> p b t", t=ND), U4,
                     M4[:, :, 3:4].broadcast_to([MH, NB, ND]), ALU.subtract))
            chain(ts(R[:, 0, :], Mr, -1.0, None, ALU.mult))
            tt(R[:, 2, :], Bc, Mr, ALU.add).then_inc(gate_v, 1)
            dve.wait_ge(gate_v, 2)
            dve.wait_ge(gate_a, 4)
            dve.drain().then_inc(gate_d, 1)
            dve.drain().then_inc(gate_done, 1)
            dve.wait_ge(gate_ps, 1)
            for src, dst in ((0, Uc), (1, wc)):
                chain(cp(dst[:, 0:32], MX[:, src, 0:32]))
                chain(cp(dst[0:TS, 32:40], MX[0:TS, src, 32:40]))
            chain(cp(nsT.rearrange("p b h -> p (b h)"), MX[:, 2, 0:64]))
            chain(tt(wb[0:TS], wc[0:TS, 32:40].unsqueeze(2).broadcast_to([TS, MH, NB]),
                     bm[0:TS, :].unsqueeze(1).broadcast_to([TS, MH, NB]), ALU.mult))
            dve.drain().then_inc(gate_cols, 1)

            def memory(m, p):
                r, c = m
                h = c if r is None else r + c
                if p == 0:
                    ts(rows[BP, :], rows[GP, :], fix[GP, ds(h + (C_ID + 64), 1)], None, ALU.mult).then_inc(rb_done, 1)
                    dve.wait_ge(tr1_ready, val(0, 1, m, 1))
                    for ch in range(4):
                        ts(wk[:, ch, :], MX[:, 0, P * ch:P * ch + P], wc[:, ds(h + 8 * ch, 1)], None, ALU.mult)\
                            .then_inc(wk_done, 1)
                    dve.wait_ge(vt_done, val(0, 3, m, 3))
                    tt(wks, MX[0:TS, 3, 0:P].unsqueeze(1).broadcast_to([TS, NB, P]),
                       wb[0:TS, ds(h, 1), :].rearrange("p o b -> p (o b)").unsqueeze(2).broadcast_to([TS, NB, P]),
                       ALU.mult).then_inc(wk_done, 1)
                if p == 1:
                    dve.wait_ge(sc1_ready, val(0, 1, m, 1))
                    tt(Dm.rearrange("p (c t) -> p c t", c=4), MX[:, 1, :].rearrange("p (c t) -> p c t", c=4),
                       cm.unsqueeze(1).broadcast_to([P, 4, P]), ALU.add).then_inc(arg_done, 1)
                    dve.wait_ge(ab_done, val(0, 1, m, 1))
                    chain(tt(qa[:, 0:TP], q1[:, 0:TP], aB, ALU.mult))
                    dve.wait_ge(Dexp_done, val(0, 4, m, 4))
                    tt(Dm, Dm, MX[:, 0, :], ALU.mult).then_inc(P_done, 1)
                if p == 2:
                    dve.wait_ge(G_ready, val(0, 1, m, 1))
                    dve.wait_ge(sb_done, val(0, 1, m, 1))
                    dve.wait_ge(Sp_out, val(16, 16, m))
                    chain(cp(S[:, 0, :], MX[:, 1, 0:DV]))
                    chain(cp(nn[:, 0:1], MX[:, 3, 0:1]))
                    for ch in range(1, 4):
                        al = aB[:, P * ch + P - 1:P * ch + P]
                        chain(stt(S[:, ch, :], S[:, ch - 1, :], al, MX[:, 1 + ch // 2, DV * (ch % 2):DV * (ch % 2) + DV],
                                  ALU.mult, ALU.add))
                        chain(stt(nn[:, ch:ch + 1], nn[:, ch - 1:ch], al, MX[:, 3, ch:ch + 1], ALU.mult, ALU.add))
                        chain(ts(qn[:, P * ch:P * ch + P], qa[:, P * ch:P * ch + P], nn[:, ch - 1:ch], None, ALU.mult))
                    cp(nout[:, ds(h + 64, 1)], nn[:, 3:4]).then_inc(S_done, 1)
                    tt(Ds[0:TS, :], sB[0:TS, 0, :], sm[0:TS, :], ALU.add).then_inc(dsarg_done, 1)
                    chain(tt(qa[:, TP:T], q1[:, TP:T], sB[:, 1, :], ALU.mult))
                    chain(tt(qn[:, TP:T].rearrange("p (b t) -> p b t", t=ND), qa[:, TP:T].rearrange("p (b t) -> p b t", t=ND),
                             nsT[:, :, ds(h, 1)].broadcast_to([P, NB, ND]), ALU.mult))
                    dve.wait_ge(dsexp_done, val(0, 1, m, 1))
                    tt(Ds[0:TS, :], Ds[0:TS, :], MX[0:TS, 3, 64:64 + TS], ALU.mult).then_inc(Ps_done, 1)
                if p == 4:
                    dve.wait_ge(abs_done, val(0, 1, m, 1))
                    dve.wait_ge(emt_done, val(0, 2, m, 2))
                    chain(tt(Dm, Dm, emt[:, 0:TP], ALU.max))
                    chain(dve.reciprocal(Dm, Dm))
                    chain(tt(hh[:, :, 0:TP], MX[:, 0:2, :], Dm.unsqueeze(1).broadcast_to([P, 2, TP]), ALU.mult))
                if p == 5:
                    dve.wait_ge(abss_done, val(0, 1, m, 1))
                    qs_ = qn[:, TP:T]
                    chain(tt(qs_, qs_, emt[:, TP:T], ALU.max))
                    chain(dve.reciprocal(qs_, qs_))
                    tt(hh[:, :, TP:T], MX[:, 3, 0:64].rearrange("p (a t) -> p a t", a=2),
                       qs_.unsqueeze(1).broadcast_to([P, 2, TS]), ALU.mult).then_inc(hout_done, 1)
                if p == 7:
                    dve.wait_ge(cu_ready, val(0, 1, m, 1))
                    for b in range(NB):
                        stt(cs[:, b, :], cs[:, b, :], sB[:, 1, ND * b + 3:ND * b + 4],
                            MX[:, b // 2, DV * (b % 2):DV * (b % 2) + DV], ALU.mult, ALU.add).then_inc(cnew_done, 1)
                if p == 8:
                    dve.wait_ge(ss1_ready, val(0, 1, m, 1))
                    ts(two(qa), MX[:, 1:3, 0:HT], 1.0 / DV, EPS, ALU.mult, ALU.add).then_inc(ms1_done, 1)
                    no = nout[:, 0:64].rearrange("p (b h) -> p b h", b=NB)[:, :, ds(h, 1)].rearrange("p b o -> p (b o)")
                    al = sB[:, 1, :].rearrange("p (b t) -> p b t", t=ND)[:, :, 3]
                    ns = nsT[:, :, ds(h, 1)].rearrange("p b o -> p (b o)")
                    chain(tt(no, ns, al, ALU.mult))
                    chain(tt(no, no, MX[:, 0, 0:NB], ALU.add))
                    dve.wait_ge(rt1_done, val(0, 1, m, 1))
                    chain(dve.reciprocal(qa, qa))
                    chain(tt(hh, hh, qa.unsqueeze(1).broadcast_to([P, 2, T]), ALU.mult))
                    for blk in range(2):
                        ob = obuf[:, ds(h * 2 + blk, 1), :].rearrange("p o t -> p (o t)")
                        last = stt(ob, hh[:, blk, :], gT[:, ds(h * 2 + (64 + blk), 1)], ob, ALU.mult, ALU.mult)
                        if blk == 0:
                            chain(last)
                    last.then_inc(head_done, 1)

            def empty1(it, e, seen):
                kind = L1K[e]
                r, c = it
                h = c if r is None else r + c
                order = e + 1
                if kind == "Z":
                    empty_z("l1", it, e, h * 2 + seen, val(4 * GR, 4, it, order))
                if kind == "O":
                    dve.wait_ge(th_done, val(4 * GR, 4, it, order))
                    dve.wait_ge(*freed_at("l1", it, e - 1))
                    ob = obuf[:, ds(h * 2 + seen, 1), :].rearrange("p o t -> p (o t)")
                    stt(ob, misc[:, :], 1.0, ob, ALU.add, ALU.mult).then_inc(freed["d"], 1)

            def layer1(it, m):
                seen = dict.fromkeys("ZOQKV", 0)
                for e in range(len(L1K) + 1):
                    if e:
                        empty1(it, e - 1, seen[L1K[e - 1]])
                        seen[L1K[e - 1]] += 1
                    if e + 1 < len(L1K):
                        split_lo("l1", it, e + 1)
                    if m is not None:
                        if e:
                            memory(m, 2 * e - 1)
                        if e < len(L1K):
                            memory(m, 2 * e)

            LOOP_M = 1 + (2 + 9 + 2) + 3 + 2 + (2 + 2 + 1)
            layer1((None, 0), None)
            with dve.Fori(0, MH - 1) as r:
                chain.enter(r, LOOP_M)
                split_lo("l1", (r, 1), 0)
                layer1((r, 1), (r, 0))
            chain.leave(MH - 1)
            split_lo("out1", it0, 0)
            split_lo("out1", it0, 1)
            for p in range(16):
                memory((None, MH - 1), p)
            dve.wait_ge(nT_ps, 1)
            cp(area(A1, "wk")[0:72, 0:P], MX[0:72, 0, 0:P]).then_inc(nT_done, 1)
            dve.wait_ge(head_done, 1 + MH)
            split_out(3)
            out_lows("out1")
            residual(1, 4)
            for t in range(5):
                n = P if t < 4 else TS
                dve.wait_ge(fin_ready, t + 1)
                if t >= 2:
                    dve.wait_ge(y_out[t % 2], 16 * (t // 2))
                for b in range(2, 4):
                    cp(raw[t % 2][0:n, 512 * b:512 * b + 512], MX[0:n, b, :]).then_inc(fin_d, 1)


_INS = ["x_prompt", "x_sample", "c_prompt", "c_sample", "cache_k", "cache_v", "state_C", "state_n", "state_m",
        "w_ada", "b_ada", "g_pre", "g_post", "w_in_attn", "sinks", "w_out_attn", "w_in_mlstm", "b_if_mlstm",
        "g_head_mlstm", "w_out_mlstm"]
_OUTS = [(1, TP, D), (NB, ND, D), (1, 1, WIN, KVH, HD), (1, 1, WIN, KVH, HD), (1, NB, WIN, KVH, HD),
         (1, NB, WIN, KVH, HD), (1, 1, MH, DK, DV), (1, 1, MH, DK), (1, 1, MH), (1, NB, MH, DK, DV),
         (1, NB, MH, DK), (1, NB, MH)]


def kernel(**inputs):
    import concourse.bacc as _bacc
    from concourse.bass_utils import run_bass_kernel_spmd as _run

    nc = _bacc.Bacc("TRN2", target_bir_lowering=False, num_devices=1)
    arrays, args = {}, []
    given = [(n, np.ascontiguousarray(inputs[n])) for n in _INS] + [("const", constants())]
    for name, a in given:
        arrays[f"in_{name}"] = a
        args.append(nc.dram_tensor(f"in_{name}", a.shape, mybir.dt.from_np(a.dtype), kind="ExternalInput").ap())
    for i, shape in enumerate(_OUTS):
        args.append(nc.dram_tensor(f"out_{i}", shape, F32, kind="ExternalOutput").ap())
    args.append(nc.dram_tensor("x_spill", (P, KT * T), F32, kind="Internal").ap())
    trunk(nc, *args)
    r = _run(nc, [arrays], core_ids=[0])
    return tuple(r.results[0][f"out_{i}"] for i in range(len(_OUTS)))
```

```python
from contextlib import ExitStack

import numpy as np
import concourse.bass as bass
from concourse import mybir

F32 = mybir.dt.float32
F32R = mybir.dt.float32r
ALU = mybir.AluOpType
ACT = mybir.ActivationFunctionType
AX = mybir.AxisListType.X
ds = bass.ds

P = 128
D = 2048
KT = D // P
TP = 512
NB, ND = 8, 4
TS = NB * ND
T = TP + TS
HT = T // 2
NSEQ = 1 + NB
WIN = 128
QH, KVH, HD = 32, 8, 64
GR = 4
MH, DK, DV = 8, 128, 256
NC_ = TP // P
EPS = 1e-6
BIG = -1e30

OWNER = dict(A="d", Z="d", O="d", Q="a", K="a", V="a", Y="a", G="a")
L0K = "ZZZZQVQQQK"
L1K = "ZOZOQKVV"
PHASES = [("ada0", 1, "A" * 8), ("l0", GR, L0K), ("out0", 1, "Y" * KT), ("gate", 1, "G"),
          ("l1", MH, L1K), ("out1", 1, "Y" * KT)]


def first_of(kinds, size):
    return {ph: sum(n * sum(size(k) for k in ks) for p, n, ks in PHASES[:i])
            for i, (ph, _, _) in enumerate(PHASES)}


UNITS = dict.fromkeys("ZOQKVYG", 1) | {"A": 4}
KINDS = {ph: ks for ph, _, ks in PHASES}
ITERS = {ph: n for ph, n, _ in PHASES}
ENTRY0 = first_of(PHASES, lambda k: 1)
UNIT0 = first_of(PHASES, lambda k: UNITS[k])
FREED0 = {w: first_of(PHASES, lambda k, w=w: int(OWNER[k] == w)) for w in "ad"}
RAW0 = UNIT0["l0"]

SEGS = dict(out0=[(0, 4, (0, 2 * D, 8)), (4, 8, (1, 0, 12)), (12, 2, None)],
            out1=[(0, 4, (1, 2 * D, 20)), (4, 10, None)])
SQ_PARTS = [range(0, 5), range(5, 10), range(10, KT)]
STRIPS = 8
RING = 4
SW = 2 * 512

C_ID, C_ONE, C_SLP, C_SLS, C_SEL = 0, 128, 256, 288, 296
C_FIX = 305
C_NEGD, C_NEGS = 305, 305 + 768
C_L0 = C_NEGS + 1056
C_CM, C_SM, C_BM = C_L0, C_L0 + 128, C_L0 + 160
C_ALL = C_L0 + 168


def constants():
    c = np.zeros((P, C_ALL), np.float32)
    c[:, C_ID:C_ID + P] = np.eye(P)
    c[:, C_ONE:C_ONE + P] = 1.0
    slopes = (2.0 ** (-8.0 * np.arange(1, QH + 1) / QH)).astype(np.float32)
    c[:, C_SLP:C_SLP + QH] = slopes
    p = np.arange(P)
    for m in range(GR):
        for half in range(2):
            c[:, C_SLS + 2 * m + half] = slopes[8 * m + 4 * (p // 64) + 2 * (p // 32 % 2) + half]
    for r in range(2 * NSEQ):
        c[32 + r, C_SEL + r % NSEQ] = 1.0
    c[32 + 2 * NSEQ, C_SEL:C_SEL + NSEQ] = 1.0
    q, k = np.arange(P)[:, None], np.arange(2 * P)[None, :]
    d = q + P - k
    neg = np.where((d >= 0) & (d < WIN), -d.astype(np.float32), BIG)
    first = np.where(k < P, BIG, neg)
    c[:, C_NEGD:C_NEGD + 768] = np.concatenate([first, neg, neg], 1)
    tok = p % TS
    b, t = (tok // ND)[:, None], (tok % ND)[:, None]
    j = np.arange(NB * WIN)[None, :]
    dc = t + WIN - j % WIN
    c[:, C_NEGS:C_NEGS + 1024] = np.where((j // WIN == b) & (dc < WIN), -dc, BIG)
    j = np.arange(TS)[None, :]
    dn = t - j % ND
    c[:, C_NEGS + 1024:C_NEGS + 1056] = np.where((j // ND == b) & (dn >= 0), -dn, BIG)
    s, t = np.arange(P)[:, None], np.arange(P)[None, :]
    c[:, C_CM:C_CM + P] = np.where(s <= t, 0.0, BIG)
    s, t = np.arange(TS)[:, None], np.arange(TS)[None, :]
    c[0:TS, C_SM:C_SM + TS] = np.where((s // ND == t // ND) & (s <= t), 0.0, BIG)
    c[0:TS, C_BM:C_BM + NB] = (np.arange(TS)[:, None] // ND == np.arange(NB)[None, :])
    return c


ARENA = 12520


def offsets(sizes, at=0):
    out = {}
    for name, size in sizes:
        out[name] = (at, size)
        at += size
    assert at <= ARENA, at
    return out


UW = offsets([(f"lo{i}", SW) for i in range(RING)] + [(f"hi{i}", SW) for i in range(RING)])
XW = offsets([("x", KT * T), ("sq", 2 * T), ("r", T), ("vec", P)])
A0 = offsets([("q", 4 * TP), ("qs", P), ("kT", P + T), ("kS", P + T), ("vT", T), ("vtok", TP),
              ("vks", 256), ("kout", P), ("ckraw", 1024), ("cv", 1024), ("ckT", 1024), ("ckS", 1024),
              ("soft", 1536), ("negd", 768), ("negs", 1056)])
A1 = offsets([("q", T), ("k", T), ("v", 2 * T), ("vtok", 4 * DV), ("wk", 4 * P), ("rows", 3 * T),
              ("S", 4 * DV), ("n", 8), ("D", TP), ("qa", T), ("qn", T), ("emt", T), ("h", 2 * T),
              ("cs", NB * DV), ("sb", 3 * TS), ("Ds", TS), ("Uc", 40), ("wc", 40), ("wb", 64),
              ("nsT", 64), ("nout", 72), ("cm", 128), ("sm", 32), ("bm", 8)])


SLOW = dict(allow_slow_non_contiguous=True)


def val(base, per, it, k=0):
    r, c = it
    n = base + c * per + k
    return n if r is None else r * per + n


def fixed(eng, value):
    return value if isinstance(value, int) else eng.snap(eng.to_reg(value))


class Chain:

    def __init__(self, eng, sem):
        self.eng, self.sem, self.base, self.k, self.it, self.per = eng, sem, 0, 0, (None, 0), 0

    def __call__(self, ins):
        self.k += 1
        ins.then_inc(self.sem, 1)
        self.eng.wait_ge(self.sem, val(self.base, self.per, self.it, self.k))

    def enter(self, reg, per):
        self.base, self.k, self.it, self.per = self.base + self.k, 0, (reg, 0), per

    def leave(self, iters):
        assert self.k == self.per, f"a loop body has {self.k} steps, not {self.per}"
        self.base, self.k, self.it, self.per = self.base + iters * self.per, 0, (None, 0), 0


def trunk(nc, x_prompt, x_sample, c_prompt, c_sample, cache_k, cache_v, state_C, state_n, state_m,
          w_ada, b_ada, g_pre, g_post, w_in_attn, sinks, w_out_attn, w_in_mlstm, b_if_mlstm,
          g_head_mlstm, w_out_mlstm, const,
          y_prompt, y_sample, nk_p, nv_p, nk_s, nv_s, nC_p, nn_p, nm_p, nC_s, nn_s, nm_s, x_spill):
    with ExitStack() as ctx:
        def sb(name, shape, dt=F32):
            return ctx.enter_context(nc.sbuf_tensor(name, shape, dt))

        def sem(name):
            return ctx.enter_context(nc.semaphore(name))

        h_hi = sb("h_hi", [P, KT, T], F32R)
        h_lo = sb("h_lo", [P, KT, T], F32R)
        obuf = sb("obuf", [P, KT, T])
        raw = [sb(f"raw{i}", [P, D]) for i in range(2)]
        w_hi = [sb(f"w_hi{i}", [P, D], F32R) for i in range(2)]
        w_lo = [sb(f"w_lo{i}", [P, D], F32R) for i in range(2)]
        cT = sb("cT", [P, 16 * 18 + 110], F32R)
        modT = sb("modT", [P, 96, NSEQ])
        misc = sb("misc", [P, T])
        gT = sb("gT", [P, 80])
        fix = sb("fix", [P, C_FIX])
        nsink = sb("nsink", [P, QH + 8])
        st = sb("st", [P, 40])
        with nc.sbuf_tensor("strips", [P, 2 * RING * SW], F32R) as strips:
            pass
        arena = sb("arena", [P, ARENA])
        PJ = ctx.enter_context(nc.psum_tensor("PJ", [P, 4, 512], F32))
        MX = ctx.enter_context(nc.psum_tensor("MX", [P, 4, 512], F32))

        def area(table, name):
            a, n = table[name]
            return arena[:, a:a + n]

        ident = fix[:, C_ID:C_ID + P]
        ones = fix[:, C_ONE:C_ONE + P]
        xw = area(XW, "x").rearrange("p (k t) -> p k t", k=KT)
        xflat = area(XW, "x")
        sqb = area(XW, "sq").rearrange("p (a t) -> p a t", a=2)
        rB = area(XW, "r")
        gvec = area(XW, "vec")[0:80, :]
        c_rows = area(XW, "x")[0:NSEQ, 0:D]
        c_tanh = area(XW, "x")[0:NSEQ, D:2 * D]
        c_full = area(XW, "x")[:, 2 * D:2 * D + KT * NSEQ]
        u_raw = [area(UW, f"lo{i}") for i in range(RING)]
        u_lo = [strips[:, SW * i:SW * i + SW] for i in range(RING)]
        u_hi = [strips[:, SW * (RING + i):SW * (RING + i + 1)] for i in range(RING)]
        q0 = area(A0, "q").rearrange("p (j t) -> p j t", j=4)
        qS = area(A0, "qs")
        kT, kS = area(A0, "kT"), area(A0, "kS")
        vT, vtok = area(A0, "vT"), area(A0, "vtok")
        vks, kout = area(A0, "vks"), area(A0, "kout")
        ckraw = area(A0, "ckraw").rearrange("p (b c) -> p b c", b=NB)
        PTs, PTn = area(A0, "ckraw"), area(A0, "soft")[0:TS, 1056:1184]
        cv = area(A0, "cv").rearrange("p (b c) -> p b c", b=NB)
        ckT, ckS = area(A0, "ckT"), area(A0, "ckS")
        soft = area(A0, "soft")
        SPs = soft[:, 0:1056]
        PP = [soft[:, 0:512], soft[:, 512:1024]]
        PT = soft[:, 1024:1536]
        negd, negs = area(A0, "negd"), area(A0, "negs")
        q1, k1, v1 = area(A1, "q"), area(A1, "k"), area(A1, "v").rearrange("p (a t) -> p a t", a=2)
        hsq = v1
        vt1 = area(A1, "vtok").rearrange("p (c e) -> p c e", c=4)
        wk = area(A1, "wk").rearrange("p (c e) -> p c e", c=4)
        rows = area(A1, "rows")
        wks = rows[0:TS, 0:1024].rearrange("p (b e) -> p b e", b=NB)
        vs = rows[0:TS, 1024:1280]
        GP = slice(64, 64 + MH)
        BP = slice(96, 96 + MH)
        R = rows[GP, :].rearrange("p (j t) -> p j t", j=3)
        RB = rows[BP, :].rearrange("p (j t) -> p j t", j=3)
        S = area(A1, "S").rearrange("p (c e) -> p c e", c=4)
        nn = area(A1, "n")
        Dm = area(A1, "D")
        qa, qn, emt = area(A1, "qa"), area(A1, "qn"), area(A1, "emt")
        hh = area(A1, "h").rearrange("p (a t) -> p a t", a=2)
        aB = area(A1, "h")[:, 0:TP]
        cs = area(A1, "cs").rearrange("p (b e) -> p b e", b=NB)
        sB = area(A1, "sb").rearrange("p (j t) -> p j t", j=3)
        Ds = area(A1, "Ds")
        Uc, wc = area(A1, "Uc"), area(A1, "wc")
        wb = area(A1, "wb").rearrange("p (h b) -> p h b", h=MH)
        nsT = area(A1, "nsT").rearrange("p (b h) -> p b h", b=NB)
        nout = area(A1, "nout")
        cm, sm, bm = area(A1, "cm"), area(A1, "sm"), area(A1, "bm")
        LI = area(A1, "h")[GP, 0:T]
        LF = area(A1, "h")[GP, T:2 * T]
        Ub = area(A1, "qa")[GP, :]
        Wr = area(A1, "qn")[GP, :]
        Bc = area(A1, "emt")[GP, :]
        Mr = area(A1, "S")[GP, 0:T]
        tg = area(A1, "D")[GP, 0:16]
        m0s = area(A1, "D")[GP, 16:24]
        bif = area(A1, "D")[GP, 24:26]
        nrow = area(A1, "wk")[0:64, 0:P]

        const_in, mask_in = sem("const_in"), sem("mask_in")
        c_in = sem("c_in")
        vec_in = sem("vec_in")
        sink_in = sem("sink_in")
        x_in = [sem("x_in0"), sem("x_in1")]
        a0_in = [sem(f"a0_in{i}") for i in range(4)]
        w_in = [sem("w_in0"), sem("w_in1")]
        hi_done = sem("hi_done")
        lo_done = sem("lo_done")
        w_used = sem("w_used")
        freed = {"a": sem("freed_a"), "d": sem("freed_d")}
        u_in = [sem(f"u_in{i}") for i in range(RING)]
        u_hi_done, u_lo_done = sem("u_hi_done"), sem("u_lo_done")
        u_used = sem("u_used")
        mod_taken = sem("mod_taken")
        sums_ready = sem("sums_ready")
        mod_copied, mod_turned, bias_in = sem("mod_copied"), sem("mod_turned"), sem("bias_in")
        ct_rows, ct_ps, ct_ready = sem("ct_rows"), sem("ct_ps"), sem("ct_ready")
        ct_tanh, ct_full = sem("ct_tanh"), sem("ct_full")
        vec_ps, g_ready = sem("vec_ps"), sem("g_ready")
        xt_done = sem("xt_done")
        xe_a, xe_d = sem("xe_a"), sem("xe_d")
        sq_made, sq_used = sem("sq_made"), sem("sq_used")
        ms_ready, rt_ready = sem("ms_ready"), sem("rt_ready")
        spilled, reloaded = sem("spilled"), sem("reloaded")
        x_ready = sem("x_ready")
        y_scaled = sem("y_scaled")
        acc_done = sem("acc_done")
        xs_done = sem("xs_done")
        A_ready = sem("A_ready")
        mod_applied = sem("mod_applied")
        hh_hi = sem("hh_hi")
        h_ready = sem("h_ready")
        dch, ach = sem("dch"), sem("ach")
        pads = sem("pads")
        tv_ready, tv_done = sem("tv_ready"), sem("tv_done")
        kv_stored = sem("kv_stored")
        ck_in, cv_in = sem("ck_in"), sem("cv_in")
        ck_ready, ck_done = sem("ck_ready"), sem("ck_done")
        ss_ready, smax_ready, sexp_ready, sp_ready = (sem("ss_ready"), sem("smax_ready"),
                                                      sem("sexp_ready"), sem("sp_ready"))
        ts_ready, pts_done, pvs_ready = sem("ts_ready"), sem("pts_done"), sem("pvs_ready")
        sc_ready, pmax_ready, pexp_ready, pn_ready = (sem("sc_ready"), sem("pmax_ready"),
                                                      sem("pexp_ready"), sem("pn_ready"))
        tr_ready, pt_done, pv_ready = sem("tr_ready"), sem("pt_done"), sem("pv_ready")
        om_done = sem("om_done")
        gl_in, gate_done = sem("gl_in"), sem("gate_done")
        gate_d, gate_a = sem("gate_d"), sem("gate_a")
        gate_ps, gate_v, gate_cols = sem("gate_ps"), sem("gate_v"), sem("gate_cols")
        tr1_ready, vt_done, wk_done, rb_done = sem("tr1_ready"), sem("vt_done"), sem("wk_done"), sem("rb_done")
        sc1_ready, arg_done, ab_done, emt_done = (sem("sc1_ready"), sem("arg_done"), sem("ab_done"),
                                                  sem("emt_done"))
        Dexp_done, P_done = sem("Dexp_done"), sem("P_done")
        G_ready, sb_done, S_done = sem("G_ready"), sem("sb_done"), sem("S_done")
        dsarg_done, dsexp_done, Ps_done = sem("dsarg_done"), sem("dsexp_done"), sem("Ps_done")
        num_ready, nums_ready, abs_done, abss_done = (sem("num_ready"), sem("nums_ready"),
                                                      sem("abs_done"), sem("abss_done"))
        hout_done, hsq_done = sem("hout_done"), sem("hsq_done")
        cu_ready, cnew_done, ss1_ready = sem("cu_ready"), sem("cnew_done"), sem("ss1_ready")
        ms1_done, rt1_done, head_done = sem("ms1_done"), sem("rt1_done"), sem("head_done")
        th_done = sem("th_done")
        cs_in, cs_out, Sp_out = sem("cs_in"), sem("cs_out"), sem("Sp_out")
        nT_ps, nT_done = sem("nT_ps"), sem("nT_done")
        fin_ready, fin_a, fin_d = sem("fin_ready"), sem("fin_a"), sem("fin_d")
        out_done = sem("out_done")
        y_out = [sem("y_out0"), sem("y_out1")]

        def freed_at(ph, it, e):
            names = [p for p, _, _ in PHASES]
            while e < 0:
                r, c = it
                if r is None and c == 0:
                    ph = names[names.index(ph) - 1]
                    it = (None, ITERS[ph] - 1)
                else:
                    it = (r, c - 1)
                e += len(KINDS[ph])
            w = OWNER[KINDS[ph][e]]
            per = sum(OWNER[k] == w for k in KINDS[ph])
            upto = sum(OWNER[k] == w for k in KINDS[ph][:e + 1])
            return freed[w], val(FREED0[w][ph], per, it, upto)

        def unit_no(ph, it, e, j=0):
            ks = KINDS[ph]
            return val(UNIT0[ph], sum(UNITS[k] for k in ks), it, sum(UNITS[k] for k in ks[:e]) + j)

        def ended(ph, it, e):
            return unit_no(ph, it, e, UNITS[KINDS[ph][e]])

        def slot_of(ph, e, j=0):
            return (UNIT0[ph] + sum(UNITS[k] for k in KINDS[ph][:e]) + j) % 2

        def pair_of(ph, e):
            return (ENTRY0[ph] + e) % 2

        def landed_at(ph, it, e, j=0):
            ks = KINDS[ph]
            per = sum(UNITS[k] for k in ks)
            at = UNIT0[ph] + sum(UNITS[k] for k in ks[:e]) + j - RAW0
            r, c = it
            n = 16 * ((at + c * per) // 2 + 1)
            return n if r is None else r * (8 * per) + n

        def pj(pair, parts=slice(0, P)):
            return PJ[parts, 2 * pair:2 * pair + 2, 0:HT]

        def two(ap):
            return ap.rearrange("p (a t) -> p a t", a=2)

        def per_seq(ap):
            return ap.unsqueeze(3).broadcast_to([P, ap.shape[1], NB, ND])

        def blocks_of(eng, ph, seg):
            k0, n, _ = seg
            with eng.Fori(0, n // 2) as r:
                for i in range(2):
                    yield r, i, k0 + i

        block = ctx.enter_context(nc.Block())

        @block.sync
        def _(sp):
            ada = w_ada.rearrange("l (k p) n -> p l k n", p=P)
            win0 = w_in_attn[0].rearrange("(k p) n -> p k n", p=P)
            win1 = w_in_mlstm[0].rearrange("(k p) n -> p k n", p=P)
            wout = [w_out_attn[0].rearrange("(k p) n -> p k n", p=P),
                    w_out_mlstm[0].rearrange("(k p) n -> p k n", p=P)]
            for u in range(32):
                if u >= 4:
                    sp.wait_ge(lo_done, u - 3)
                slot = obuf[:, 4 * (u % 4):4 * (u % 4) + 4, 0:512]
                sp.dma_start(slot, ada[:, 0, 4 * (u % 4):4 * (u % 4) + 4,
                                       512 * (u // 4):512 * (u // 4) + 512]).then_inc(a0_in[u % 4], 16)

            def load(ph, it, e, j, src, dst_cols=D):
                s = slot_of(ph, e, j)
                split = fixed(sp, unit_no(ph, it, e, j - 1))
                sp.wait_ge(xt_done, 5)
                sp.wait_ge(lo_done, split)
                k = src.shape[1]
                sp.dma_start(raw[s][:, 0:dst_cols].rearrange("p (k n) -> p k n", k=k), src)\
                    .then_inc(w_in[s], 16)

            def layer0(it):
                r, c = it
                g = c if r is None else r + c
                nz = nq = 0
                for e, kind in enumerate(L0K):
                    if kind == "Z":
                        col = g * 512 + (3072 + 128 * nz)
                        nz += 1
                    elif kind == "Q":
                        col = g * 512 + 128 * nq
                        nq += 1
                    elif kind == "K":
                        col = g * 128 + 2048
                    else:
                        col = g * 128 + 2560
                    load("l0", it, e, 0, win0[:, :, ds(col, P)])

            sp.wait_ge(xt_done, 5)
            layer0((None, 0))
            with sp.Fori(0, GR - 1) as r:
                layer0((r, 1))

            def out_units(ph, w, arena_free=()):
                load(ph, (None, 0), 0, 0, w[:, :, 0:P])

                def block(k, s, split):
                    before = fixed(sp, split)
                    sp.wait_ge(xt_done, 5)
                    sp.wait_ge(lo_done, before)
                    sp.dma_start(raw[s][:, :].rearrange("p (k n) -> p k n", k=KT), w[:, :, ds(k * P, P)])\
                        .then_inc(w_in[s], 16)

                for se, v in arena_free:
                    sp.wait_ge(se, v)
                for seg in SEGS[ph]:
                    for r, i, k in blocks_of(sp, ph, seg):
                        block(r * 2 + (k + 1), slot_of(ph, k + 1), r * 2 + (UNIT0[ph] + k))
                        if seg[2] is None:
                            continue
                        l, col, group = seg[2]
                        first = STRIPS * (group - 8 + i)
                        for j in range(STRIPS):
                            free = fixed(sp, r * (2 * STRIPS) + (first + j + 1))
                            sp.wait_ge(xt_done, 5)
                            sp.wait_ge(u_used, free)
                            sp.dma_start(u_raw[j % RING].rearrange("p (k n) -> p k n", k=2),
                                         ada[:, l, 2 * j:2 * j + 2, ds(r * 1024 + (col + 512 * i), 512)])\
                                .then_inc(u_in[j % RING], 16)
                block(KT - 1, slot_of(ph, KT - 1), UNIT0[ph] + KT - 2)

            sp.wait_ge(xt_done, 5)
            out_units("out0", wout[0], [(kv_stored, 32 + 64 * GR)])
            load("gate", (None, 0), 0, 0, win1[:, :, 8192:8208], KT * 16)

            def layer1(it):
                r, c = it
                h = c if r is None else r + c
                seen = dict.fromkeys("ZOQKV", 0)
                start = dict(Q=0, K=1024, V=2048, O=4096, Z=6144)
                for e, kind in enumerate(L1K):
                    width = P if kind in "QK" else DV
                    load("l1", it, e, 0, win1[:, :, ds(h * width + (start[kind] + P * seen[kind]), P)])
                    seen[kind] += 1

            layer1((None, 0))
            with sp.Fori(0, MH - 1) as r:
                layer1((r, 1))
            out_units("out1", wout[1], [(head_done, 1 + MH), (cs_out, 16 * MH), (Sp_out, 16 + 16 * MH),
                                        (out_done, 48)])

        @block.gpsimd
        def _(pool):
            bada = b_ada.rearrange("l n -> (l n)").unsqueeze(0)
            brow = misc[50:51, 0:512]

            def bias(a, first=False):
                if not first:
                    pool.wait_ge(mod_turned, a)
                pool.dma_start(brow, bada[:, ds(a * 512, 512)]).then_inc(bias_in, 16)

            for t in range(5):
                if t >= 2:
                    pool.wait_ge(xt_done, t - 1)
                if t < 4:
                    pool.dma_start(raw[t % 2][:, :], x_prompt[0, P * t:P * t + P, :]).then_inc(x_in[t % 2], 16)
                else:
                    pool.dma_start(raw[0][0:TS, :], x_sample.rearrange("b t d -> (b t) d"))\
                        .then_inc(x_in[0], 16)
                if t:
                    bias(t - 1, t == 1)
                if t == 1:
                    pool.dma_start(nsink[:, 0:QH], sinks.broadcast_to([P, QH])).then_inc(sink_in, 16)
                    for a in range(2):
                        for bl in range(2):
                            src = sinks.rearrange("o (m a l h) -> (o a l) m h", m=GR, a=2, l=2)[2 * a + bl]
                            p0 = 64 * a + 32 * bl
                            for h in range(2):
                                dst = nsink[p0:p0 + 32, QH + 4 * h:QH + 4 * h + 4]
                                pool.dma_start(dst, src[:, h:h + 1].rearrange("m h -> h m").broadcast_to([32, GR]), **SLOW)\
                                    .then_inc(sink_in, 16)
            for a in range(4, 8):
                bias(a)
            pool.dma_start(nk_s[0, :, 0:WIN - ND], cache_k[0, :, ND:WIN]).then_inc(kv_stored, 16)
            pool.dma_start(nv_s[0, :, 0:WIN - ND], cache_v[0, :, ND:WIN]).then_inc(kv_stored, 16)
            pool.wait_ge(xe_a, 10)
            pool.wait_ge(xe_d, 10)
            pool.dma_start(x_spill, xflat).then_inc(spilled, 16)
            pool.wait_ge(spilled, 16)
            pool.wait_ge(h_ready, KT)
            pool.dma_start(area(A0, "negd"), const[:, C_NEGD:C_NEGD + 768]).then_inc(mask_in, 16)
            pool.dma_start(area(A0, "negs"), const[:, C_NEGS:C_NEGS + 1056]).then_inc(mask_in, 16)

            def caches(g):
                pool.dma_start(ckraw, cache_k[0].rearrange("b w h d -> w b (h d)")[:, :, ds(g * P, P)])\
                    .then_inc(ck_in, 16)
                pool.dma_start(cv, cache_v[0].rearrange("b w h d -> w b (h d)")[:, :, ds(g * P, P)])\
                    .then_inc(cv_in, 16)

            def store_kv(it):
                r, c = it
                m = c if r is None else r + c
                pool.wait_ge(h_ready, KT)
                pool.wait_ge(tv_done, val(0, 4, it, 4))
                kc = slice(None)
                flat = "o b w h d -> (o b) w (h d)"
                pool.dma_start(nk_p.rearrange(flat)[0][:, ds(m * P, P)], kout).then_inc(kv_stored, 16)
                pool.dma_start(nv_p.rearrange(flat)[0][:, ds(m * P, P)], vtok[:, 384:512]).then_inc(kv_stored, 16)
                for dst, col in ((nv_s, 0), (nk_s, P)):
                    d = dst.rearrange(flat)[:, WIN - ND:WIN, ds(m * P, P)]
                    pool.dma_start(d, vks[0:TS, col:col + P]).then_inc(kv_stored, 16)

            caches(0)
            bias(8)

            def l0_rest(it):
                store_kv(it)
                r, c = it
                pool.wait_ge(h_ready, KT)
                pool.wait_ge(pvs_ready, val(0, 2, it, 2))
                caches(r + (c + 1))

            with pool.Fori(0, GR - 1) as r:
                l0_rest((r, 0))
            store_kv((None, GR - 1))
            pool.wait_ge(kv_stored, 32 + 64 * GR)
            pool.wait_ge(om_done, 1 + 18 * GR)
            with pool.Fori(0, 11) as r:
                group = fixed(pool, r + 9)
                pool.wait_ge(h_ready, KT)
                pool.wait_ge(mod_turned, group)
                pool.dma_start(brow, bada[:, ds(r * 512 + 9 * 512, 512)]).then_inc(bias_in, 16)
            pool.wait_ge(u_used, RING + 12 * STRIPS)
            pool.dma_start(xflat, x_spill).then_inc(reloaded, 16)
            pool.wait_ge(x_ready, KT)
            pool.dma_start(x_spill, xflat).then_inc(spilled, 16)
            pool.wait_ge(spilled, 32)
            pool.wait_ge(h_ready, 3 * KT)
            pool.dma_start(cm, const[:, C_CM:C_CM + 128]).then_inc(gl_in, 16)
            pool.dma_start(sm, const[:, C_SM:C_SM + 32]).then_inc(gl_in, 16)
            pool.dma_start(bm, const[:, C_BM:C_BM + 8]).then_inc(gl_in, 16)
            pool.dma_start(m0s, state_m[0].rearrange("b h -> h b"), **SLOW).then_inc(gl_in, 16)
            pool.dma_start(bif, b_if_mlstm.rearrange("o (g h) -> h (o g)", g=2), **SLOW).then_inc(gl_in, 16)
            pool.dma_start(nrow, state_n[0].rearrange("b h d -> (b h) d")).then_inc(gl_in, 16)
            C_in = state_C[0].rearrange("b h k e -> h k b e")
            C_out = nC_s[0].rearrange("b h k e -> h k b e")
            pool.dma_start(cs, C_in[0]).then_inc(cs_in, 16)
            pool.wait_ge(gate_done, 1)
            pool.dma_start(nm_p.rearrange("o b h -> h (o b)"), R[:, 2, TP - 1:TP], **SLOW).then_inc(Sp_out, 16)
            pool.dma_start(nm_s[0].rearrange("b h -> h b"), R[:, 2, TP:T].rearrange("p (b t) -> p b t", t=ND)[:, :, 3], **SLOW)\
                .then_inc(out_done, 16)

            def states(it, more):
                r, c = it
                h = c if r is None else r + c
                pool.wait_ge(gate_done, 1)
                pool.wait_ge(S_done, val(0, 1, it, 1))
                pool.dma_start(nC_p.rearrange("o b h k e -> (o b h) k e")[ds(h, 1)].rearrange("o k e -> (o k) e"),
                               S[:, 3, :]).then_inc(Sp_out, 16)
                new, at = fixed(pool, val(0, NB, it, NB)), fixed(pool, h)
                pool.wait_ge(gate_done, 1)
                pool.wait_ge(cnew_done, new)
                pool.dma_start(C_out[ds(at, 1)].rearrange("o k b e -> (o k) b e"), cs).then_inc(cs_out, 16)
                if more:
                    pool.wait_ge(gate_done, 1)
                    pool.wait_ge(cs_out, val(0, 16, it, 16))
                    pool.dma_start(cs, C_in[ds(h + 1, 1)].rearrange("o k b e -> (o k) b e")).then_inc(cs_in, 16)

            with pool.Fori(0, MH - 1) as r:
                states((r, 0), True)
            states((None, MH - 1), False)
            pool.wait_ge(nT_done, 1)
            nrow2 = area(A1, "wk")[0:72, 0:P]
            pool.dma_start(nn_s[0].rearrange("b h d -> (b h) d"), nrow2[0:64, :]).then_inc(out_done, 16)
            pool.dma_start(nn_p.rearrange("o b h d -> (o b h) d"), nrow2[64:72, :]).then_inc(out_done, 16)
            pool.wait_ge(out_done, 48)
            pool.wait_ge(cs_out, 16 * MH)
            pool.wait_ge(Sp_out, 16 + 16 * MH)
            pool.wait_ge(head_done, 1 + MH)
            bias(20)
            for a in range(21, 24):
                bias(a)
            pool.wait_ge(u_used, RING + 16 * STRIPS)
            pool.dma_start(xflat, x_spill).then_inc(reloaded, 16)
            for t in range(5):
                pool.wait_ge(fin_a, 2 * (t + 1))
                pool.wait_ge(fin_d, 2 * (t + 1))
                dst = y_prompt[0, P * t:P * t + P, :] if t < 4 else y_sample.rearrange("b t d -> (b t) d")
                n = P if t < 4 else TS
                pool.dma_start(dst, raw[t % 2][0:n, :]).then_inc(y_out[t % 2], 16)
            pool.wait_ge(y_out[0], 48)
            pool.wait_ge(y_out[1], 32)

        @block.tensor
        def _(pe):
            mm, tr = pe.matmul, pe.transpose

            def ada_products(ph, it, e, mid=None):
                pair = pair_of(ph, e)
                for j in range(4):
                    s = slot_of(ph, e, j)
                    pe.wait_ge(lo_done, unit_no(ph, it, e, j) + 1)
                    for k in range(4):
                        lhsT = cT[:, (4 * j + k) * 18:(4 * j + k) * 18 + P]
                        for w in (w_hi, w_lo):
                            last = mm(PJ[:, 2 * pair, :], lhsT, w[s][:, k * 512:k * 512 + 512],
                                      start=(j == 0 and k == 0 and w is w_hi),
                                      stop=(j == 3 and k == 3 and w is w_lo))
                    last.then_inc(w_used, 1)
                    if mid:
                        mid(j)

            def ada_turn(ph, it, e, n):
                pair = pair_of(ph, e)
                pe.wait_ge(mod_copied, n + 1)
                pe.wait_ge(bias_in, n * 16 + 16)
                for j in range(4):
                    last = mm(PJ[:, 2 * pair + 1, 9 * j:9 * j + 9], misc[32:51, P * j:P * j + P],
                              fix[32:51, C_SEL:C_SEL + NSEQ], start=True, stop=True)
                last.then_inc(mod_turned, 1)

            def entry(ph, it, e, points={}, h_base=None):
                s, pair = slot_of(ph, e), pair_of(ph, e)
                se, v = freed_at(ph, it, e - 2)
                pe.wait_ge(se, v)
                pe.wait_ge(lo_done, unit_no(ph, it, e) + 1)
                block(s, pair, points, h_base)

            def block(s, pair, points, h_base):
                for k in range(KT):
                    if h_base is not None:
                        pe.wait_ge(h_ready, h_base + k + 1)
                    hi = w_hi[s][:, P * k:P * k + P]
                    lo = w_lo[s][:, P * k:P * k + P]
                    for n, (w, h) in enumerate(((hi, h_hi), (hi, h_lo), (lo, h_hi))):
                        for f in range(2):
                            last = mm(PJ[:, 2 * pair + f, 0:HT], w, h[:, k, HT * f:HT * f + HT],
                                      start=(k == 0 and n == 0), stop=(k == KT - 1 and n == 2))
                    if k == KT - 1:
                        last.then_inc(w_used, 1)
                    if k in points:
                        points[k]()

            pe.wait_ge(const_in, 16)
            pe.wait_ge(vec_in, 48)
            tr(MX[:, 2, 0:80], gvec, ident[0:80, 0:80]).then_inc(vec_ps, 1)
            pe.wait_ge(ct_rows, 1)
            for k in range(KT):
                last = tr(MX[:, 3, NSEQ * k:NSEQ * k + NSEQ], c_rows[:, P * k:P * k + P], ident[0:NSEQ, 0:NSEQ])
            last.then_inc(ct_ps, 1)
            pe.wait_ge(ct_ready, 1)

            def turn_x(t):
                n = P if t < 4 else TS
                pe.wait_ge(x_in[t % 2], 16 * (t // 2 + 1))
                if t:
                    pe.wait_ge(xe_a, 2 * t)
                    pe.wait_ge(xe_d, 2 * t)
                else:
                    pe.wait_ge(g_ready, 1)
                for k in range(KT):
                    last = tr(MX[:, k // 4, n * (k % 4):n * (k % 4) + n], raw[t % 2][0:n, P * k:P * k + P],
                              ident[0:n, 0:n])
                last.then_inc(xt_done, 1)

            def sums(base, blocks=range(KT)):
                for k in blocks:
                    pe.wait_ge(sq_made, base + k + 1)
                    for f in range(2):
                        last = mm(MX[:, f, 0:HT], ones, sqb[:, k % 2, HT * f:HT * f + HT],
                                  start=(k == 0), stop=(k == KT - 1))
                    last.then_inc(sq_used, 1)

            it0 = (None, 0)
            for e in range(8):
                if e >= 2:
                    pe.wait_ge(*freed_at("ada0", it0, e - 2))

                def between(j, e=e):
                    if j == 1 and e:
                        ada_turn("ada0", it0, e - 1, e - 1)
                    if j == 2 and e < 5:
                        turn_x(e)
                ada_products("ada0", it0, e, between)
                if e == 5:
                    pe.wait_ge(xe_a, 10)
                    pe.wait_ge(xe_d, 10)
                if e >= 5:
                    sums(0, SQ_PARTS[e - 5])
            ada_turn("ada0", it0, 7, 7)

            def kv_turn(m):
                se, v = freed_at("l0", m, len(L0K) - 1)
                pe.wait_ge(se, v)
                pe.wait_ge(om_done, val(1, 18, m))
                for c in range(4):
                    tr(MX[:, 0, P * c:P * c + P], vT[:, P * c:P * c + P], ident)
                tr(MX[:, 1, 0:P], kT[:, P + 384:P + 512], ident)
                tr(MX[0:TS, 1, P:2 * P], vT[:, TP:T], ident)
                tr(MX[0:TS, 1, 2 * P:3 * P], kT[:, P + TP:P + T], ident).then_inc(tv_ready, 1)
                pe.wait_ge(ck_in, val(0, 16, m, 16))
                for b in range(NB):
                    last = tr(MX[:, 2 + b // 4, P * (b % 4):P * (b % 4) + P], ckraw[:, b, :], ident)
                last.then_inc(ck_ready, 1)

            def sample_scores(m, half):
                if half == 0:
                    tv_all, ck_all = fixed(pe, val(0, 4, m, 4)), fixed(pe, val(0, 6, m, 6))
                    pe.wait_ge(pads, 2)
                    pe.wait_ge(tv_done, tv_all)
                    pe.wait_ge(ck_done, ck_all)
                hs = slice(64 * half, 64 * half + 64)
                for a in range(2):
                    ck, kk = (ckT, kT) if a == half else (ckS, kS)
                    lhsT = qS[hs, 64 * a:64 * a + 64]
                    out = slice(64 * a, 64 * a + 64)
                    for j in range(2):
                        mm(MX[out, j, :], lhsT, ck[hs, 512 * j:512 * j + 512], start=True, stop=True)
                    last = mm(MX[out, 2, 0:TS], lhsT, kk[hs, P + TP:P + T], start=True, stop=True)
                last.then_inc(ss_ready, 1)

            def sample_turn(m, half):
                pe.wait_ge(sp_ready, val(0, 2, m, half + 1))
                for b in range(NB):
                    tr(MX[:, b // 4, P * (b % 4):P * (b % 4) + P], SPs[:, P * b:P * b + P], ident)
                tr(MX[0:TS, 2, 0:P], SPs[:, 1024:1056], ident).then_inc(ts_ready, 1)

            def sample_pv(m, half):
                pe.wait_ge(pts_done, val(0, 4, m, 2 * half + 2))
                if half == 0:
                    pe.wait_ge(cv_in, val(0, 16, m, 16))
                out = slice(64 * half, 64 * half + 64)
                for a in range(2):
                    o = MX[out, 3, 64 * a:64 * a + 64]
                    for b in range(NB):
                        mm(o, cv[:, b, 64 * a:64 * a + 64], PTs[:, P * b + 64 * a:P * b + 64 * a + 64],
                           start=(b == 0), stop=False)
                    last = mm(o, vks[0:TS, 64 * a:64 * a + 64], PTn[:, 64 * a:64 * a + 64],
                              start=False, stop=True)
                last.then_inc(pvs_ready, 1)

            def step(x):
                return x // 4, x // 2 % 2, x % 2

            def scores(m, x):
                j, bp, half = step(x)
                hs = slice(64 * half, 64 * half + 64)
                kk = kT if j // 2 == half else kS
                for bl in range(2):
                    b = 2 * bp + bl
                    last = mm(MX[:, half, 256 * bl:256 * bl + 256], q0[hs, j, P * b:P * b + P],
                              kk[hs, P * b:P * b + 2 * P], start=True, stop=True)
                last.then_inc(sc_ready, 1)

            def p_turn(m, x):
                pe.wait_ge(pn_ready, val(0, 32, m, 2 * x + 2))
                for c in range(4):
                    last = tr(MX[:, 2, P * c:P * c + P], PP[x % 2][:, P * c:P * c + P], ident)
                last.then_inc(tr_ready, 1)

            def pv(m, x):
                j, bp, half = step(x)
                a = j // 2
                pe.wait_ge(pt_done, val(0, 16, m, x + 1))
                pe.wait_ge(om_done, val(1, 18, m, max(2, x + 1)))
                for bl in range(2):
                    b = 2 * bp + bl
                    o = MX[64 * half:64 * half + 64, 3, P * bl:P * bl + P]
                    for kb in range(2):
                        if b == 0 and kb == 0:
                            continue
                        last = mm(o, vtok[:, P * (b - 1 + kb) + 64 * a:P * (b - 1 + kb) + 64 * a + 64],
                                  PT[:, 256 * bl + P * kb:256 * bl + P * kb + P],
                                  start=(kb == 0 or b == 0), stop=(kb == 1))
                last.then_inc(pv_ready, 1)

            def attend(m, p):
                if p == 0:
                    kv_turn(m)
                if p in (2, 5):
                    if p == 5:
                        sample_pv(m, 0)
                    sample_scores(m, p // 3)
                if p in (4, 8):
                    sample_turn(m, p // 8)
                if p == 9:
                    sample_pv(m, 1)
                if 0 <= p - 13 < 15:
                    pv(m, p - 13)
                if 0 <= p - 12 < 16:
                    p_turn(m, p - 12)
                if 0 <= p - 10 < 16:
                    scores(m, p - 10)
                if p == 27:
                    pv(m, 15)

            POINTS = (4, 10, KT - 1)

            def layer0(it, m, h_base=None):
                for e in range(len(L0K)):
                    points = {}
                    if m is not None:
                        points = {k: (lambda p=3 * e + i: attend(m, p)) for i, k in enumerate(POINTS)}
                    entry("l0", it, e, points, h_base if e == 0 else None)

            layer0((None, 0), None, 0)
            with pe.Fori(0, GR - 1) as r:
                layer0((r, 1), (r, 0))
            for p in range(28):
                attend((None, GR - 1), p)

            def strip(n, j, r=0):
                at = fixed(pe, n + 1)
                pe.wait_ge(ct_ready, 1)
                pe.wait_ge(u_lo_done, at)
                for k in range(2):
                    lhsT = cT[:, (2 * j + k) * 18:(2 * j + k) * 18 + P]
                    for w in (u_hi, u_lo):
                        last = mm(MX[:, 2, :], lhsT, w[j % RING][:, k * 512:k * 512 + 512],
                                  start=(j == 0 and k == 0 and w is u_hi),
                                  stop=(j == STRIPS - 1 and k == 1 and w is u_lo))
                last.then_inc(u_used, 1)

            def turn_group(n):
                pe.wait_ge(ct_ready, 1)
                pe.wait_ge(mod_copied, n + 1)
                pe.wait_ge(bias_in, n * 16 + 16)
                pe.wait_ge(mod_taken, n - 7)
                for j in range(4):
                    last = mm(MX[:, 3, 9 * j:9 * j + 9], misc[32:51, P * j:P * j + P],
                              fix[32:51, C_SEL:C_SEL + NSEQ], start=True, stop=True)
                last.then_inc(mod_turned, 1)

            def out_product(ph, h_base, n):
                def one(k, seg, r, i):
                    pe.wait_ge(freed["a"], r * 2 + (FREED0["a"][ph] + k - 1))
                    pe.wait_ge(lo_done, r * 2 + (UNIT0[ph] + k + 1))
                    points = {}
                    if seg and seg[2]:
                        g = seg[2][2] + i
                        first = STRIPS * (g - 8)

                        def strips(js):
                            for j in js:
                                strip(r * (2 * STRIPS) + (first + j), j)
                        points = {3: lambda: strips(range(4)), 9: lambda: strips(range(4, 8)),
                                  KT - 1: lambda: turn_group(r * 2 + g)}
                    block(slot_of(ph, k), pair_of(ph, k), points, h_base if k == 0 else None)

                for seg in SEGS[ph]:
                    for r, i, k in blocks_of(pe, ph, seg):
                        one(k, seg, r, i)
                for k in range(KT - 2, KT):
                    one(k, None, 0, 0)
                pe.wait_ge(sq_used, KT * n)
                for f in range(2):
                    last = mm(MX[:, f, 0:HT], ones, rB[:, HT * f:HT * f + HT], start=True, stop=True)
                last.then_inc(sums_ready, 1)

            out_product("out0", KT, 2)
            sums(2 * KT)

            entry("gate", it0, 0, {}, 2 * KT)
            pe.wait_ge(gate_d, 1)
            for c in range(5):
                n = P if c < 4 else TS
                tr(MX[0:n, 0, 8 * c:8 * c + 8], Ub[:, P * c:P * c + n], ident[GP, 64:72])
                tr(MX[0:n, 1, 8 * c:8 * c + 8], Wr[:, P * c:P * c + n], ident[GP, 64:72])
            pe.wait_ge(gl_in, 96)
            tr(MX[:, 2, 0:64], nrow, ident[0:64, 0:64]).then_inc(gate_ps, 1)

            def memory(m, p):
                if p == 0:
                    pe.wait_ge(*freed_at("l1", m, 7))
                    pe.wait_ge(head_done, val(1, 1, m))
                    for bank, src in ((0, k1), (1, v1[:, 0, :]), (2, v1[:, 1, :])):
                        for c in range(4):
                            tr(MX[:, bank, P * c:P * c + P], src[:, P * c:P * c + P], ident)
                    for j, src in enumerate((k1, v1[:, 0, :], v1[:, 1, :])):
                        last = tr(MX[0:TS, 3, P * j:P * j + P], src[:, TP:T], ident)
                    last.then_inc(tr1_ready, 1)
                if p == 1:
                    pe.wait_ge(wk_done, val(0, 5, m, 5))
                    pe.wait_ge(vt_done, val(0, 3, m, 3))
                    pe.wait_ge(rb_done, val(0, 1, m, 1))
                    for c in range(4):
                        mm(MX[:, 0, P * c:P * c + P], k1[:, P * c:P * c + P], q1[:, P * c:P * c + P],
                           start=True, stop=True)
                    for j in range(3):
                        last = mm(MX[:, 1 + j, :], fix[BP, C_ONE:C_ONE + P], RB[:, j, 0:TP],
                                  start=True, stop=True)
                    last.then_inc(sc1_ready, 1)
                if p == 2:
                    pe.wait_ge(arg_done, val(0, 1, m, 1))
                    pe.wait_ge(ab_done, val(0, 1, m, 1))
                    pe.wait_ge(emt_done, val(0, 2, m, 1))
                    for c in range(4):
                        mm(MX[:, 1 + c // 2, DV * (c % 2):DV * (c % 2) + DV], wk[:, c, :], vt1[:, c, :],
                           start=True, stop=True)
                    for c in range(4):
                        mm(MX[:, 3, c:c + 1], wk[:, c, :], ones[:, 0:1], start=True, stop=True)
                    mm(MX[0:TS, 3, 64:64 + TS], k1[:, TP:T], q1[:, TP:T], start=True, stop=True)
                    mm(MX[:, 3, P:P + 3 * TS], fix[BP, C_ONE:C_ONE + P], RB[:, :, TP:T],
                       start=True, stop=True).then_inc(G_ready, 1)
                if p == 4:
                    pe.wait_ge(P_done, val(0, 1, m, 1))
                    pe.wait_ge(S_done, val(0, 1, m, 1))
                    for blk in range(2):
                        for c in range(4):
                            o = MX[:, blk, P * c:P * c + P]
                            mm(o, vt1[:, c, P * blk:P * blk + P], Dm[:, P * c:P * c + P],
                               start=True, stop=(c == 0))
                            if c:
                                mm(o, S[:, c - 1, P * blk:P * blk + P], qa[:, P * c:P * c + P],
                                   start=False, stop=True)
                    mm(MX[:, 2, :], ones, Dm[:, :], start=True, stop=False)
                    mm(MX[:, 2, P:TP], ones, qn[:, P:TP], start=False, stop=True).then_inc(num_ready, 1)
                if p == 5:
                    pe.wait_ge(Ps_done, val(0, 1, m, 1))
                    pe.wait_ge(cs_in, val(0, 16, m, 16))
                    for blk in range(2):
                        mm(MX[:, 3, TS * blk:TS * blk + TS], vs[:, P * blk:P * blk + P], Ds[0:TS, :],
                           start=True, stop=False)
                        for b in range(NB):
                            mm(MX[:, 3, TS * blk + ND * b:TS * blk + ND * b + ND],
                               cs[:, b, P * blk:P * blk + P], qa[:, TP + ND * b:TP + ND * b + ND],
                               start=False, stop=(b == NB - 1))
                    mm(MX[:, 3, 64:64 + TS], ones[0:TS, :], Ds[0:TS, :], start=True, stop=False)
                    mm(MX[:, 3, 64:64 + TS], ones, qn[:, TP:T], start=False, stop=True)\
                        .then_inc(nums_ready, 1)
                if p == 7:
                    pe.wait_ge(hout_done, val(0, 1, m, 1))
                    for b in range(NB):
                        last = mm(MX[:, b // 2, DV * (b % 2):DV * (b % 2) + DV], wks[:, b, :], vs,
                                  start=True, stop=True)
                    last.then_inc(cu_ready, 1)
                if p == 8:
                    pe.wait_ge(cnew_done, val(0, NB, m, NB))
                    pe.wait_ge(hsq_done, val(0, 2, m, 2))
                    for b in range(NB):
                        mm(MX[:, 0, b:b + 1], wks[:, b, :], ones[0:TS, 0:1], start=True, stop=True)
                    for f in range(2):
                        for blk in range(2):
                            last = mm(MX[:, 1 + f, 0:HT], ones, hsq[:, blk, HT * f:HT * f + HT],
                                      start=(blk == 0), stop=(blk == 1))
                    last.then_inc(ss1_ready, 1)

            def layer1(it, m):
                for e in range(len(L1K)):
                    points = {}
                    if m is not None:
                        points = {k: (lambda p=2 * e + i: memory(m, p)) for i, k in enumerate((7, KT - 1))}
                    entry("l1", it, e, points)

            layer1((None, 0), None)
            pe.wait_ge(gate_cols, 1)
            with pe.Fori(0, MH - 1) as r:
                layer1((r, 1), (r, 0))
            for p in range(16):
                memory((None, MH - 1), p)
            pe.wait_ge(head_done, 1 + MH)
            tr(MX[0:72, 0, 0:P], nout, ident).then_inc(nT_ps, 1)
            pe.wait_ge(nT_done, 1)
            out_product("out1", 3 * KT, 4)

            pe.wait_ge(x_ready, 2 * KT)
            for t in range(5):
                n = P if t < 4 else TS
                if t:
                    pe.wait_ge(fin_a, 2 * t)
                    pe.wait_ge(fin_d, 2 * t)
                for k in range(KT):
                    last = tr(MX[0:n, k // 4, P * (k % 4):P * (k % 4) + P], xw[:, k, P * t:P * t + n], ident)
                last.then_inc(fin_ready, 1)

        @block.scalar
        def _(act):
            chain = Chain(act, ach)
            fn = act.activation
            it0 = (None, 0)

            act.dma_start(fix[:, :], const[:, 0:C_FIX]).then_inc(const_in, 16)
            act.dma_start(c_rows[0:1, :], c_prompt).then_inc(c_in, 16)
            act.dma_start(c_rows[1:NSEQ, :], c_sample).then_inc(c_in, 16)
            act.dma_start(gvec[0:32, :], g_pre.rearrange("l (k p) -> (l k) p", p=P)).then_inc(vec_in, 16)
            act.dma_start(gvec[32:64, :], g_post.rearrange("l (k p) -> (l k) p", p=P)).then_inc(vec_in, 16)
            act.dma_start(gvec[64:80, :], g_head_mlstm.rearrange("o h (k p) -> (o h k) p", p=P)).then_inc(vec_in, 16)
            act.wait_ge(c_in, 32)
            fn(c_tanh, c_rows, ACT.Tanh, scale=0.5).then_inc(ct_tanh, 1)
            act.wait_ge(ct_ps, 1)
            act.wait_ge(const_in, 16)
            fn(c_full, MX[:, 3, 0:KT * NSEQ], ACT.Copy).then_inc(ct_full, 1)

            def round_hi(ph, it, e, j=0):
                s = slot_of(ph, e, j)
                if ph == "ada0":
                    u = 4 * e + j
                    act.wait_ge(a0_in[u % 4], 16 * (u // 4 + 1))
                    if u >= 2:
                        act.wait_ge(w_used, u - 1)
                    fn(w_hi[s][:, :].rearrange("p (k n) -> p k n", k=4),
                       obuf[:, 4 * (u % 4):4 * (u % 4) + 4, 0:512], ACT.Copy).then_inc(hi_done, 1)
                    return
                act.wait_ge(w_in[s], landed_at(ph, it, e, j))
                act.wait_ge(w_used, unit_no(ph, it, e, j - 1))
                if ph == "gate":
                    fn(w_hi[s][:, :].rearrange("p (k a n) -> p k a n", k=KT, n=32)[:, :, 0:2, 0:8],
                       raw[s][:, 0:KT * 16].rearrange("p (k a n) -> p k a n", k=KT, n=8),
                       ACT.Copy).then_inc(hi_done, 1)
                    return
                fn(w_hi[s][:, :], raw[s][:, :], ACT.Copy).then_inc(hi_done, 1)

            def mod_copy(ph, e, n, it):
                act.wait_ge(w_used, ended(ph, it, e))
                if ph != "ada0" or n:
                    act.wait_ge(mod_turned, n)
                fn(misc[32:50, 0:512], PJ[0:18, 2 * pair_of(ph, e), :], ACT.Copy).then_inc(mod_copied, 1)

            def squares(base, blocks=range(KT), x_from=None):
                for k in blocks:
                    if x_from is not None:
                        act.wait_ge(x_ready, x_from + k + 1)
                    if base + k >= 2:
                        act.wait_ge(sq_used, base + k - 1)
                    fn(sqb[:, k % 2, :], xw[:, k, :], ACT.Square).then_inc(sq_made, 1)

            def root(n):
                act.wait_ge(ms_ready, n)
                fn(rB, rB, ACT.Sqrt).then_inc(rt_ready, 1)

            def modulate(l, n):
                act.wait_ge(A_ready, l + 1)
                with act.Fori(0, KT) as k:
                    act.wait_ge(xs_done, k + (KT * l + 1))
                    xk = obuf[:, ds(k, 1), 0:TP].rearrange("p o t -> p (o t)")
                    fn(xk, xk, ACT.Identity, scale=modT[:, ds(k + (48 * l + 16), 1), 0:1].rearrange("p a b -> p (a b)"),
                       bias=modT[:, ds(k + 48 * l, 1), 0:1].rearrange("p a b -> p (a b)")).then_inc(mod_applied, 1)
                    act.wait_ge(mod_applied, k + (KT * l + 1))
                    fn(h_hi[:, ds(k, 1), :].rearrange("p o t -> p (o t)"),
                       obuf[:, ds(k, 1), :].rearrange("p o t -> p (o t)"), ACT.Copy).then_inc(hh_hi, 1)

            def split_out():
                with act.Fori(0, KT) as k:
                    fn(h_hi[:, ds(k, 1), :].rearrange("p o t -> p (o t)"),
                       obuf[:, ds(k, 1), :].rearrange("p o t -> p (o t)"), ACT.Copy).then_inc(hh_hi, 1)

            for e in range(8):
                for j in range(4):
                    round_hi("ada0", it0, e, j)
                    if j == 1 and e:
                        mod_copy("ada0", e - 1, e - 1, it0)
                if e < 5:
                    n = P if e < 4 else TS
                    act.wait_ge(xt_done, e + 1)
                    act.wait_ge(ct_ready, 1)
                    for b in range(2):
                        fn(xw[:, 4 * b:4 * b + 4, P * e:P * e + n],
                           MX[:, b, 0:4 * n].rearrange("p (k t) -> p k t", k=4), ACT.Copy).then_inc(xe_a, 1)
                if e == 5:
                    act.wait_ge(xe_a, 10)
                    act.wait_ge(xe_d, 10)
                if e >= 5:
                    squares(0, SQ_PARTS[e - 5])
            mod_copy("ada0", 7, 7, it0)
            round_hi("l0", it0, 0)
            root(1)
            modulate(0, 0)
            act.wait_ge(spilled, 16)

            def attend(m, p):
                if p == 0:
                    act.wait_ge(tv_ready, val(0, 1, m, 1))
                    act.wait_ge(kv_stored, val(32, 64, m))
                    fn(vtok, MX[:, 0, :], ACT.Copy).then_inc(tv_done, 1)
                    fn(kout, MX[:, 1, 0:P], ACT.Copy).then_inc(tv_done, 1)
                    fn(vks[0:TS, 0:P], MX[0:TS, 1, P:2 * P], ACT.Copy).then_inc(tv_done, 1)
                    fn(vks[0:TS, P:2 * P], MX[0:TS, 1, 2 * P:3 * P], ACT.Copy).then_inc(tv_done, 1)
                if p in (2, 5):
                    half = p // 3
                    act.wait_ge(smax_ready, val(0, 2, m, half + 1))
                    fn(SPs, SPs, ACT.Exp, bias=st[:, 1:2], accum_out=st[:, 2:3]).then_inc(sexp_ready, 1)
                    fn(st[:, 4:5], st[:, 3:4], ACT.Exp).then_inc(sexp_ready, 1)
                if p in (4, 8):
                    half = p // 8
                    act.wait_ge(ts_ready, val(0, 2, m, half + 1))
                    fn(PTs, MX[:, 0:2, :].rearrange("p a t -> p (a t)"), ACT.Copy).then_inc(pts_done, 1)
                    fn(PTn, MX[0:TS, 2, 0:P], ACT.Copy).then_inc(pts_done, 1)
                if 0 <= p - 12 < 16:
                    x = p - 12
                    act.wait_ge(tr_ready, val(0, 16, m, x + 1))
                    fn(PT, MX[:, 2, :], ACT.Copy).then_inc(pt_done, 1)
                if 0 <= p - 10 < 16:
                    x = p - 10
                    o = 8 + 16 * (x % 2)
                    act.wait_ge(pmax_ready, val(0, 16, m, x + 1))
                    for bl in range(2):
                        pb = PP[x % 2][:, 256 * bl:256 * bl + 256]
                        fn(pb, pb, ACT.Exp, bias=st[:, o + 2 + bl:o + 3 + bl],
                           accum_out=st[:, o + 6 + bl:o + 7 + bl]).then_inc(pexp_ready, 1)
                    fn(st[:, o + 8:o + 10], st[:, o + 4:o + 6], ACT.Exp).then_inc(pexp_ready, 1)

            def empty0(it, m, e, nq, nz):
                kind, pair = L0K[e], pair_of("l0", e)
                act.wait_ge(w_used, ended("l0", it, e))
                r, c = it
                g = c if r is None else r + c
                if kind == "Z":
                    fn(obuf[:, ds(g * 4 + nz, 1), :].rearrange("p o (a t) -> p (o a) t", a=2), pj(pair),
                       ACT.Tanh, scale=0.5).then_inc(th_done, 1)
                if kind == "Q":
                    if m is not None:
                        act.wait_ge(sc_ready, val(0, 16, m, 4 * nq + 4))
                        act.wait_ge(ss_ready, val(0, 2, m, 2))
                    sc = float(HD) ** -0.5
                    chain(fn(q0[:, nq, 0:HT], PJ[:, 2 * pair, 0:HT], ACT.Copy, scale=sc))
                    chain(fn(q0[:, nq, HT:TP], PJ[:, 2 * pair + 1, 0:TP - HT], ACT.Copy, scale=sc))
                    fn(qS[:, TS * nq:TS * nq + TS], PJ[:, 2 * pair + 1, TP - HT:HT], ACT.Copy,
                       scale=sc).then_inc(freed["a"], 1)
                if kind == "K":
                    if m is not None:
                        act.wait_ge(sc_ready, val(0, 16, m, 16))
                    chain(fn(two(kT[:, P:]), pj(pair), ACT.Copy))
                    chain(fn(two(kS[0:64, P:]), pj(pair, slice(64, 128)), ACT.Copy))
                    fn(two(kS[64:128, P:]), pj(pair, slice(0, 64)), ACT.Copy).then_inc(freed["a"], 1)
                if kind == "V":
                    fn(two(vT), pj(pair), ACT.Copy).then_inc(freed["a"], 1)

            def layer0(it, m):
                nq = nz = 0
                for e in range(len(L0K) + 1):
                    if e:
                        empty0(it, m, e - 1, nq, nz)
                        nq += L0K[e - 1] == "Q"
                        nz += L0K[e - 1] == "Z"
                    if m is not None and e:
                        attend(m, 3 * e - 1)
                    if e < len(L0K):
                        round_hi("l0", it, e + 1)
                        if m is not None:
                            attend(m, 3 * e)
                            attend(m, 3 * e + 1)

            layer0((None, 0), None)
            LOOP_A = 4 * 2 + 2
            with act.Fori(0, GR - 1) as r:
                chain.enter(r, LOOP_A)
                layer0((r, 1), (r, 0))
            chain.leave(GR - 1)
            for p in range(28):
                attend((None, GR - 1), p)
            act.wait_ge(om_done, 1 + 18 * GR)
            split_out()

            def out_product(ph):
                def empty(k, used, blk):
                    pair = pair_of(ph, k)
                    base = KT if ph == "out0" else 3 * KT
                    act.wait_ge(w_used, used)
                    act.wait_ge(sq_used, used - (UNIT0[ph] + 2) + base)
                    fn(two(sqb[:, k % 2, :]), pj(pair), ACT.Square).then_inc(sq_made, 1)
                    fn(obuf[:, ds(blk, 1), :].rearrange("p o (a t) -> p (o a) t", a=2), pj(pair),
                       ACT.Copy).then_inc(freed["a"], 1)

                def ahead(k, r):
                    s = slot_of(ph, k + 1)
                    act.wait_ge(w_in[s], r * 16 + landed_at(ph, it0, k + 1))
                    act.wait_ge(w_used, r * 2 + (UNIT0[ph] + k))
                    fn(w_hi[s][:, :], raw[s][:, :], ACT.Copy).then_inc(hi_done, 1)

                for seg in SEGS[ph]:
                    for r, i, k in blocks_of(act, ph, seg):
                        ahead(k, r)
                        if seg[2]:
                            g = seg[2][2] + i
                            for j in range(STRIPS):
                                landed = 16 * (2 * (g - 8) + j // RING + 1)
                                act.wait_ge(u_in[j % RING], r * 64 + landed)
                                fn(u_hi[j % RING], u_raw[j % RING], ACT.Copy).then_inc(u_hi_done, 1)
                            act.wait_ge(u_used, r * (2 * STRIPS) + (RING + STRIPS * (g - 7)))
                            act.wait_ge(mod_turned, r * 2 + g)
                            fn(misc[32:50, 0:512], MX[0:18, 2, :], ACT.Copy).then_inc(mod_copied, 1)
                        empty(k, r * 2 + (UNIT0[ph] + k + 1), r * 2 + k)
                ahead(KT - 2, 0)
                empty(KT - 2, UNIT0[ph] + KT - 1, KT - 2)
                if ph == "out0":
                    round_hi("gate", it0, 0)
                empty(KT - 1, UNIT0[ph] + KT, KT - 1)

            out_product("out0")
            root(2)
            squares(2 * KT, x_from=0)
            root(3)
            modulate(1, 1)

            act.wait_ge(w_used, ended("gate", it0, 0))
            act.wait_ge(spilled, 32)
            act.wait_ge(h_ready, 3 * KT)
            fn(two(LI), pj(pair_of("gate", 0), slice(0, 8)), ACT.Copy).then_inc(gate_a, 1)
            fn(two(LF), pj(pair_of("gate", 0), slice(32, 40)), ACT.Copy).then_inc(freed["a"], 1)
            round_hi("l1", it0, 0)
            act.wait_ge(gate_v, 1)
            chain(fn(Bc, Bc, ACT.Exp, scale=-1.0))
            fn(Bc, Bc, ACT.Ln, bias=1.0).then_inc(gate_a, 1)
            act.wait_ge(gate_v, 2)
            fn(R[:, 1, :], R[:, 1, :], ACT.Exp).then_inc(gate_a, 1)
            fn(Wr, Wr, ACT.Exp).then_inc(gate_a, 1)

            def memory(m, p):
                r, c = m
                h = c if r is None else r + c
                if p == 0:
                    act.wait_ge(tr1_ready, val(0, 1, m, 1))
                    for j in range(2):
                        fn(vt1[:, :, P * j:P * j + P], MX[:, 1 + j, :].rearrange("p (c e) -> p c e", c=4),
                           ACT.Copy).then_inc(vt_done, 1)
                    fn(vs, MX[0:TS, 3, P:3 * P], ACT.Copy).then_inc(vt_done, 1)
                if p == 1:
                    act.wait_ge(sc1_ready, val(0, 1, m, 1))
                    fn(aB, MX[:, 2, :], ACT.Copy).then_inc(ab_done, 1)
                    fn(emt[:, 0:TP], MX[:, 3, :], ACT.Exp, scale=-1.0).then_inc(emt_done, 1)
                    act.wait_ge(arg_done, val(0, 1, m, 1))
                    for ch in range(4):
                        dc = Dm[:, P * ch:P * ch + P]
                        fn(dc, dc, ACT.Exp, bias=Uc[:, ds(h + 8 * ch, 1)]).then_inc(Dexp_done, 1)
                if p == 2:
                    act.wait_ge(G_ready, val(0, 1, m, 1))
                    fn(sB, MX[:, 3, P:P + 3 * TS].rearrange("p (j t) -> p j t", j=3), ACT.Copy).then_inc(sb_done, 1)
                    act.wait_ge(dsarg_done, val(0, 1, m, 1))
                    fn(Ds[0:TS, :], Ds[0:TS, :], ACT.Exp, bias=Uc[0:TS, ds(h + 32, 1)]).then_inc(dsexp_done, 1)
                    fn(emt[:, TP:T], sB[:, 2, :], ACT.Exp, scale=-1.0).then_inc(emt_done, 1)
                if p == 4:
                    act.wait_ge(num_ready, val(0, 1, m, 1))
                    fn(Dm, MX[:, 2, :], ACT.Abs).then_inc(abs_done, 1)
                if p == 5:
                    act.wait_ge(nums_ready, val(0, 1, m, 1))
                    fn(qn[:, TP:T], MX[:, 3, 64:64 + TS], ACT.Abs).then_inc(abss_done, 1)
                    act.wait_ge(hout_done, val(0, 1, m, 1))
                    for blk in range(2):
                        fn(hsq[:, blk, :], hh[:, blk, :], ACT.Square).then_inc(hsq_done, 1)
                if p == 8:
                    act.wait_ge(ms1_done, val(0, 1, m, 1))
                    fn(qa, qa, ACT.Sqrt).then_inc(rt1_done, 1)

            def empty1(it, m, e, seen):
                kind, pair = L1K[e], pair_of("l1", e)
                act.wait_ge(w_used, ended("l1", it, e))
                r, c = it
                h = c if r is None else r + c
                if kind == "Z":
                    fn(obuf[:, ds(h * 2 + seen, 1), :].rearrange("p o (a t) -> p (o a) t", a=2), pj(pair),
                       ACT.Tanh, scale=0.5).then_inc(th_done, 1)
                if kind == "O":
                    fn(two(misc[:, :]), pj(pair), ACT.Tanh, scale=0.5).then_inc(th_done, 1)
                if kind in "QKV":
                    if m is not None:
                        if kind == "V":
                            act.wait_ge(ss1_ready, val(0, 1, m, 1))
                        else:
                            act.wait_ge(hout_done, val(0, 1, m, 1))
                    dst = {"Q": q1, "K": k1, "V": v1[:, seen, :]}[kind]
                    fn(two(dst), pj(pair), ACT.Copy,
                       scale=float(DK) ** -0.5 if kind == "Q" else 1.0).then_inc(freed["a"], 1)

            def layer1(it, m):
                seen = dict.fromkeys("ZOQKV", 0)
                for e in range(len(L1K) + 1):
                    if e:
                        empty1(it, m, e - 1, seen[L1K[e - 1]])
                        seen[L1K[e - 1]] += 1
                    if e < len(L1K):
                        round_hi("l1", it, e + 1)
                    if m is not None:
                        if e:
                            memory(m, 2 * e - 1)
                        if e < len(L1K):
                            memory(m, 2 * e)

            layer1((None, 0), None)
            with act.Fori(0, MH - 1) as r:
                layer1((r, 1), (r, 0))
            for p in range(16):
                memory((None, MH - 1), p)
            act.wait_ge(head_done, 1 + MH)
            split_out()
            act.wait_ge(cs_out, 16 * MH)
            out_product("out1")
            root(4)
            for t in range(5):
                n = P if t < 4 else TS
                act.wait_ge(fin_ready, t + 1)
                if t >= 2:
                    act.wait_ge(y_out[t % 2], 16 * (t // 2))
                for b in range(2):
                    fn(raw[t % 2][0:n, 512 * b:512 * b + 512], MX[0:n, b, :], ACT.Copy).then_inc(fin_a, 1)

        @block.vector
        def _(dve):
            chain = Chain(dve, dch)
            tt, ts, stt, cp = dve.tensor_tensor, dve.tensor_scalar, dve.scalar_tensor_tensor, dve.tensor_copy
            it0 = (None, 0)

            chain(dve.memset(cT[:, :].bitcast(mybir.dt.uint32), 0))
            dve.memset(st[:, :], 0.0).then_inc(om_done, 1)
            dve.drain().then_inc(head_done, 1)
            dve.drain().then_inc(mod_taken, 1)
            dve.wait_ge(ct_tanh, 1)
            chain(stt(c_rows, c_tanh, 1.0, c_rows, ALU.add, ALU.mult))
            ts(c_rows, c_rows, 0.5, None, ALU.mult).then_inc(ct_rows, 1)
            dve.wait_ge(ct_full, 1)
            cv3 = c_full.rearrange("p (k s) -> p k s", k=KT)
            cT3 = cT[:, 0:KT * 18].rearrange("p (k s) -> p k s", k=KT)
            chain(cp(cT3[:, :, 0:NSEQ], cv3))
            tt(cT3[:, :, NSEQ:18], cv3, cT3[:, :, 0:NSEQ].bitcast(F32), ALU.subtract).then_inc(ct_ready, 1)
            dve.wait_ge(vec_ps, 1)
            cp(gT[:, :], MX[:, 2, 0:80]).then_inc(g_ready, 1)
            dve.wait_ge(g_ready, 1)
            chain(ts(gT[:, 64:80], gT[:, 64:80], 0.25, None, ALU.mult))

            def split_lo(ph, it, e, j=0):
                s = slot_of(ph, e, j)
                dve.wait_ge(hi_done, unit_no(ph, it, e, j) + 1)
                if ph == "ada0":
                    u = 4 * e + j
                    tt(w_lo[s][:, :].rearrange("p (k n) -> p k n", k=4),
                       obuf[:, 4 * (u % 4):4 * (u % 4) + 4, 0:512],
                       w_hi[s][:, :].rearrange("p (k n) -> p k n", k=4).bitcast(F32),
                       ALU.subtract).then_inc(lo_done, 1)
                elif ph == "gate":
                    view = "p (k a n) -> p k a n"
                    tt(w_lo[s][:, :].rearrange(view, k=KT, n=32)[:, :, 0:2, 0:8],
                       raw[s][:, 0:KT * 16].rearrange(view, k=KT, n=8),
                       w_hi[s][:, :].bitcast(F32).rearrange(view, k=KT, n=32)[:, :, 0:2, 0:8],
                       ALU.subtract).then_inc(lo_done, 1)
                else:
                    tt(w_lo[s][:, :], raw[s][:, :], w_hi[s][:, :].bitcast(F32), ALU.subtract)\
                        .then_inc(lo_done, 1)

            def mod_empty(ph, e, n):
                dve.wait_ge(mod_turned, n + 1)
                cp(modT[:, ds(n * 4, 4), :], PJ[:, 2 * pair_of(ph, e) + 1, 0:36].rearrange("p (k s) -> p k s", k=4))\
                    .then_inc(freed["d"], 1)

            def inv_rms(n):
                if n % 2:
                    dve.wait_ge(sq_used, KT * n)
                else:
                    dve.wait_ge(sums_ready, n // 2)
                ts(two(rB), MX[:, 0:2, 0:HT], 1.0 / D, EPS, ALU.mult, ALU.add).then_inc(ms_ready, 1)
                dve.wait_ge(rt_ready, n)
                chain(dve.reciprocal(rB, rB))

            def norm_split(l, n):
                inv_rms(n)
                seq = "p k (b t) -> p k b t"
                xs = obuf[:, :, TP:T]
                chain(tt(xs, xw[:, :, TP:T], rB[:, TP:T].unsqueeze(1).broadcast_to([P, KT, TS]), ALU.mult))
                A = modT[:, 48 * l + 16:48 * l + 32, :]
                gp = gT[:, KT * l:KT * l + KT].unsqueeze(2).broadcast_to([P, KT, NSEQ])
                stt(A, A, 1.0, gp, ALU.add, ALU.mult).then_inc(A_ready, 1)
                dve.wait_ge(A_ready, l + 1)
                x4 = xs.rearrange(seq, t=ND)
                chain(tt(x4, x4, per_seq(A[:, :, 1:NSEQ]), ALU.mult))
                chain(tt(x4, x4, per_seq(modT[:, 48 * l:48 * l + 16, 1:NSEQ]), ALU.add))

                def scale(k):
                    row = "p o t -> p (o t)"
                    tt(obuf[:, ds(k, 1), 0:TP].rearrange(row), xw[:, ds(k, 1), 0:TP].rearrange(row), rB[:, 0:TP],
                       ALU.mult).then_inc(xs_done, 1)

                def low(k):
                    dve.wait_ge(hh_hi, k + (2 * KT * l + 1))
                    hb = h_hi[:, ds(k, 1), :].rearrange("p o t -> p (o t)").bitcast(F32)
                    tt(h_lo[:, ds(k, 1), :].rearrange("p o t -> p (o t)"),
                       obuf[:, ds(k, 1), :].rearrange("p o t -> p (o t)"), hb, ALU.subtract).then_inc(h_ready, 1)

                scale(0)
                scale(1)
                with dve.Fori(0, KT - 2) as k:
                    scale(k + 2)
                    low(k)
                low(KT - 2)
                low(KT - 1)

            def split_out(n):
                with dve.Fori(0, KT) as k:
                    dve.wait_ge(hh_hi, k + (n * KT + 1))
                    hb = h_hi[:, ds(k, 1), :].rearrange("p o t -> p (o t)").bitcast(F32)
                    tt(h_lo[:, ds(k, 1), :].rearrange("p o t -> p (o t)"),
                       obuf[:, ds(k, 1), :].rearrange("p o t -> p (o t)"), hb, ALU.subtract).then_inc(h_ready, 1)

            for e in range(8):
                for j in range(4):
                    split_lo("ada0", it0, e, j)
                    if j == 2 and e:
                        mod_empty("ada0", e - 1, e - 1)
                if e < 5:
                    n = P if e < 4 else TS
                    dve.wait_ge(xt_done, e + 1)
                    for b in range(2, 4):
                        cp(xw[:, 4 * b:4 * b + 4, P * e:P * e + n],
                           MX[:, b, 0:4 * n].rearrange("p (k t) -> p k t", k=4)).then_inc(xe_d, 1)
            mod_empty("ada0", 7, 7)
            split_lo("l0", it0, 0)
            dve.wait_ge(sink_in, 16 * 9)
            chain(ts(nsink[:, :], nsink[:, :], -1.0, None, ALU.mult))
            norm_split(0, 1)
            dve.wait_ge(spilled, 16)
            dve.wait_ge(h_ready, KT)
            dve.memset(kT[:, 0:P], 0.0).then_inc(pads, 1)
            dve.memset(kS[:, 0:P], 0.0).then_inc(pads, 1)
            dve.wait_ge(mask_in, 32)
            dve.wait_ge(pads, 2)

            def soft_sample(m, half):
                r, c = m
                g = c if r is None else r + c
                dve.wait_ge(ss_ready, val(0, 2, m, half + 1))
                slope = fix[:, ds(g * 2 + (C_SLS + half), 1)]
                nsk = nsink[:, ds(g + (QH + 4 * half), 1)]
                chain(stt(SPs[:, 0:1024], negs[:, 0:1024], slope, MX[:, 0:2, :].rearrange("p a t -> p (a t)"),
                          ALU.mult, ALU.add))
                chain(stt(SPs[:, 1024:1056], negs[:, 1024:1056], slope, MX[:, 2, 0:TS], ALU.mult, ALU.add))
                chain(dve.tensor_reduce(st[:, 0:1], SPs, AX, ALU.max, negate=True))
                chain(tt(st[:, 1:2], st[:, 0:1], nsk, ALU.min))
                tt(st[:, 3:4], st[:, 1:2], nsk, ALU.subtract).then_inc(smax_ready, 1)

            def norm_sample(m, half):
                dve.wait_ge(sexp_ready, val(0, 4, m, 2 * half + 2))
                chain(tt(st[:, 5:6], st[:, 2:3], st[:, 4:5], ALU.add))
                chain(dve.reciprocal(st[:, 6:7], st[:, 5:6]))
                ts(SPs, SPs, st[:, 6:7], 0.5, ALU.mult, ALU.mult).then_inc(sp_ready, 1)

            def gate_sample(m, half):
                r, c = m
                g = c if r is None else r + c
                dve.wait_ge(pvs_ready, val(0, 2, m, half + 1))
                hs = slice(64 * half, 64 * half + 64)
                ob = obuf[hs, ds(g * 4, 4), TP:T]
                tt(ob, ob, MX[hs, 3, 0:P].rearrange("p (k t) -> p k t", k=4), ALU.mult).then_inc(om_done, 1)

            def soft(m, x):
                r, c = m
                g = c if r is None else r + c
                j, bp, half = x // 4, x // 2 % 2, x % 2
                pb, o = PP[x % 2], 8 + 16 * (x % 2)
                dve.wait_ge(sc_ready, val(0, 16, m, x + 1))
                head = g * 8 + (2 * j + half)
                nsk = nsink[:, ds(head, 1)].broadcast_to([P, 2])
                chain(stt(pb, negd[:, 256 * bp:256 * bp + 512], fix[:, ds(head + C_SLP, 1)], MX[:, half, :],
                          ALU.mult, ALU.add))
                chain(dve.tensor_reduce(st[:, o:o + 2], pb.rearrange("p (b k) -> p b k", b=2), AX, ALU.max,
                                        negate=True))
                chain(tt(st[:, o + 2:o + 4], st[:, o:o + 2], nsk, ALU.min))
                tt(st[:, o + 4:o + 6], st[:, o + 2:o + 4], nsk, ALU.subtract).then_inc(pmax_ready, 1)

            def norm(m, x):
                pb, o = PP[x % 2], 8 + 16 * (x % 2)
                dve.wait_ge(pexp_ready, val(0, 48, m, 3 * x + 3))
                chain(tt(st[:, o + 10:o + 12], st[:, o + 6:o + 8], st[:, o + 8:o + 10], ALU.add))
                chain(dve.reciprocal(st[:, o + 12:o + 14], st[:, o + 10:o + 12]))
                for bl in range(2):
                    q = pb[:, 256 * bl:256 * bl + 256]
                    ts(q, q, st[:, o + 12 + bl:o + 13 + bl], 0.5, ALU.mult, ALU.mult).then_inc(pn_ready, 1)

            def gate_prompt(m, x):
                r, c = m
                g = c if r is None else r + c
                j, bp, half = x // 4, x // 2 % 2, x % 2
                dve.wait_ge(pv_ready, val(0, 16, m, x + 1))
                hs = slice(64 * half, 64 * half + 64)
                ob = obuf[hs, ds(g * 4 + j, 1), 256 * bp:256 * bp + 256].rearrange("p o t -> p (o t)")
                tt(ob, ob, MX[hs, 3, 0:256], ALU.mult).then_inc(om_done, 1)

            def attend(m, p):
                if p == 0:
                    dve.wait_ge(ck_ready, val(0, 1, m, 1))
                    for j in range(2):
                        cols = slice(512 * j, 512 * j + 512)
                        cp(ckT[:, cols], MX[:, 2 + j, :]).then_inc(ck_done, 1)
                        cp(ckS[0:64, cols], MX[64:128, 2 + j, :]).then_inc(ck_done, 1)
                        cp(ckS[64:128, cols], MX[0:64, 2 + j, :]).then_inc(ck_done, 1)
                if p == 5:
                    gate_sample(m, 0)
                if p in (2, 5):
                    soft_sample(m, p // 3)
                    norm_sample(m, p // 3)
                if p == 9:
                    gate_sample(m, 1)
                if 11 <= p < 27:
                    norm(m, p - 11)
                if 10 <= p < 26:
                    soft(m, p - 10)
                if 13 <= p < 27:
                    gate_prompt(m, p - 13)
                if p == 27:
                    gate_prompt(m, 14)
                    gate_prompt(m, 15)

            def empty_z(ph, it, e, blk, nth):
                dve.wait_ge(th_done, nth)
                ob = obuf[:, ds(blk, 1), :].rearrange("p o (a t) -> p (o a) t", a=2)
                stt(ob, ob, 1.0, pj(pair_of(ph, e)), ALU.add, ALU.mult).then_inc(freed["d"], 1)

            def layer0(it, m):
                r, c = it
                g = c if r is None else r + c
                nz = 0
                for e in range(len(L0K) + 1):
                    if e:
                        if L0K[e - 1] == "Z":
                            empty_z("l0", it, e - 1, g * 4 + nz, val(0, 4, it, nz + 1))
                            nz += 1
                        if m is not None:
                            attend(m, 3 * e - 1)
                    if e < len(L0K):
                        split_lo("l0", it, e + 1)
                        if m is not None:
                            attend(m, 3 * e)
                            attend(m, 3 * e + 1)

            LOOP_D = 2 * (4 + 2) + 16 * (3 + 2)
            layer0((None, 0), None)
            with dve.Fori(0, GR - 1) as r:
                chain.enter(r, LOOP_D)
                layer0((r, 1), (r, 0))
            chain.leave(GR - 1)
            for p in range(28):
                attend((None, GR - 1), p)
            dve.wait_ge(om_done, 1 + 18 * GR)
            dve.memset(st[:, 0:1], 0.0).then_inc(u_used, RING)
            split_out(1)

            def out_product(ph):
                base = KT if ph == "out0" else 3 * KT
                dve.memset(rB, 0.0).then_inc(acc_done, 1)

                def ahead(k, r):
                    s = slot_of(ph, k + 1)
                    dve.wait_ge(hi_done, r * 2 + (UNIT0[ph] + k + 2))
                    tt(w_lo[s][:, :], raw[s][:, :], w_hi[s][:, :].bitcast(F32), ALU.subtract).then_inc(lo_done, 1)

                def add(k, r):
                    dve.wait_ge(acc_done, 1 if ph == "out0" else 2)
                    dve.wait_ge(sq_made, r * 2 + (base + k + 1))
                    dve.wait_ge(sq_used, r * 2 + (base + k))
                    tt(rB, rB, sqb[:, k % 2, :], ALU.add).then_inc(sq_used, 1)

                for seg in SEGS[ph]:
                    for r, i, k in blocks_of(dve, ph, seg):
                        ahead(k, r)
                        if seg[2]:
                            g = seg[2][2] + i
                            for j in range(STRIPS):
                                dve.wait_ge(u_hi_done, r * (2 * STRIPS) + (STRIPS * (g - 8) + j + 1))
                                tt(u_lo[j % RING], u_raw[j % RING], u_hi[j % RING].bitcast(F32), ALU.subtract)\
                                    .then_inc(u_lo_done, 1)
                            dve.wait_ge(mod_turned, r * 2 + (g + 1))
                            cp(modT[:, ds(r * 8 + 4 * g, 4), :], MX[:, 3, 0:36].rearrange("p (k s) -> p k s", k=4))\
                                .then_inc(mod_taken, 1)
                        add(k, r)
                ahead(KT - 2, 0)
                add(KT - 2, 0)
                if ph == "out0":
                    split_lo("gate", it0, 0)
                add(KT - 1, 0)

            def residual(l, n):
                inv_rms(n)
                G = modT[:, 48 * l + 32:48 * l + 48, :]
                gp = gT[:, 32 + KT * l:32 + KT * l + KT].unsqueeze(2).broadcast_to([P, KT, NSEQ])
                chain(tt(G, G, gp, ALU.mult))
                dve.wait_ge(freed["a"], FREED0["a"]["out0" if l == 0 else "out1"] + KT)
                dve.wait_ge(reloaded, 16 * (l + 1))
                ys, xs = obuf[:, :, TP:T], xw[:, :, TP:T]
                chain(tt(ys, ys, rB[:, TP:T].unsqueeze(1).broadcast_to([P, KT, TS]), ALU.mult))
                y4 = ys.rearrange("p k (b t) -> p k b t", t=ND)
                chain(tt(y4, y4, per_seq(G[:, :, 1:NSEQ]), ALU.mult))
                chain(tt(xs, xs, ys, ALU.add))

                def scaled(k):
                    yk = obuf[:, ds(k, 1), 0:TP].rearrange("p o t -> p (o t)")
                    stt(yk, yk, G[:, ds(k, 1), 0:1].rearrange("p a b -> p (a b)"), rB[:, 0:TP], ALU.mult, ALU.mult)\
                        .then_inc(y_scaled, 1)

                def added(k):
                    dve.wait_ge(y_scaled, k + (KT * l + 1))
                    xk = xw[:, ds(k, 1), 0:TP].rearrange("p o t -> p (o t)")
                    tt(xk, xk, obuf[:, ds(k, 1), 0:TP].rearrange("p o t -> p (o t)"), ALU.add).then_inc(x_ready, 1)

                scaled(0)
                with dve.Fori(0, KT - 1) as k:
                    scaled(k + 1)
                    added(k)
                added(KT - 1)

            out_product("out0")
            residual(0, 2)
            dve.wait_ge(x_ready, KT)
            norm_split(1, 3)

            dve.wait_ge(gate_a, 1)
            dve.wait_ge(freed["a"], FREED0["a"]["gate"] + 1)
            dve.wait_ge(gl_in, 96)
            chain(ts(LI, LI, bif[:, 0:1], None, ALU.add))
            chain(ts(LF, LF, bif[:, 1:2], None, ALU.add))
            chain(ts(Bc, LF, -1.0, None, ALU.mult))
            tt(Bc, Bc, LF, ALU.max).then_inc(gate_v, 1)
            split_lo("l1", it0, 0)
            dve.wait_ge(gate_a, 2)
            chain(ts(LF, LF, 0.0, None, ALU.min))
            chain(tt(LF, LF, Bc, ALU.subtract))
            orow = fix[GP, C_ONE:C_ONE + P]
            for ch in range(4):
                cc = slice(P * ch, P * ch + P)
                chain(dve.tensor_tensor_scan(Bc[:, cc], orow, LF[:, cc], 0.0, ALU.mult, ALU.add))
            B4 = Bc[:, TP:T].rearrange("p (b t) -> p b t", t=ND)
            F4 = LF[:, TP:T].rearrange("p (b t) -> p b t", t=ND)
            chain(cp(B4[:, :, 0], F4[:, :, 0]))
            for t in range(1, ND):
                chain(tt(B4[:, :, t], B4[:, :, t - 1], F4[:, :, t], ALU.add))
            chain(tt(Ub, LI, Bc, ALU.subtract))
            chain(dve.memset(tg[:, 0:1], 0.0))
            for ch in range(4):
                cc = slice(P * ch, P * ch + P)
                chain(dve.tensor_tensor_scan(Mr[:, cc], orow, Ub[:, cc], tg[:, ch:ch + 1], ALU.mult, ALU.max))
                end = P * ch + P - 1
                chain(tt(tg[:, ch + 1:ch + 2], Bc[:, end:end + 1], Mr[:, end:end + 1], ALU.add))
                chain(ts(R[:, 1, cc], Mr[:, cc], tg[:, ch:ch + 1], -1.0, ALU.subtract, ALU.mult))
                chain(ts(Wr[:, cc], Ub[:, cc], Mr[:, end:end + 1], None, ALU.subtract))
            M4 = Mr[:, TP:T].rearrange("p (b t) -> p b t", t=ND)
            U4 = Ub[:, TP:T].rearrange("p (b t) -> p b t", t=ND)
            chain(tt(M4[:, :, 0], m0s, U4[:, :, 0], ALU.max))
            for t in range(1, ND):
                chain(tt(M4[:, :, t], M4[:, :, t - 1], U4[:, :, t], ALU.max))
            chain(tt(R[:, 1, TP:T].rearrange("p (b t) -> p b t", t=ND), m0s.unsqueeze(2).broadcast_to([MH, NB, ND]),
                     M4, ALU.subtract))
            chain(tt(Wr[:, TP:T].rearrange("p (b t) -> p b t", t=ND), U4,
                     M4[:, :, 3:4].broadcast_to([MH, NB, ND]), ALU.subtract))
            chain(ts(R[:, 0, :], Mr, -1.0, None, ALU.mult))
            tt(R[:, 2, :], Bc, Mr, ALU.add).then_inc(gate_v, 1)
            dve.wait_ge(gate_v, 2)
            dve.wait_ge(gate_a, 4)
            dve.drain().then_inc(gate_d, 1)
            dve.drain().then_inc(gate_done, 1)
            dve.wait_ge(gate_ps, 1)
            for src, dst in ((0, Uc), (1, wc)):
                chain(cp(dst[:, 0:32], MX[:, src, 0:32]))
                chain(cp(dst[0:TS, 32:40], MX[0:TS, src, 32:40]))
            chain(cp(nsT.rearrange("p b h -> p (b h)"), MX[:, 2, 0:64]))
            chain(tt(wb[0:TS], wc[0:TS, 32:40].unsqueeze(2).broadcast_to([TS, MH, NB]),
                     bm[0:TS, :].unsqueeze(1).broadcast_to([TS, MH, NB]), ALU.mult))
            dve.drain().then_inc(gate_cols, 1)

            def memory(m, p):
                r, c = m
                h = c if r is None else r + c
                if p == 0:
                    ts(rows[BP, :], rows[GP, :], fix[GP, ds(h + (C_ID + 64), 1)], None, ALU.mult).then_inc(rb_done, 1)
                    dve.wait_ge(tr1_ready, val(0, 1, m, 1))
                    for ch in range(4):
                        ts(wk[:, ch, :], MX[:, 0, P * ch:P * ch + P], wc[:, ds(h + 8 * ch, 1)], None, ALU.mult)\
                            .then_inc(wk_done, 1)
                    dve.wait_ge(vt_done, val(0, 3, m, 3))
                    tt(wks, MX[0:TS, 3, 0:P].unsqueeze(1).broadcast_to([TS, NB, P]),
                       wb[0:TS, ds(h, 1), :].rearrange("p o b -> p (o b)").unsqueeze(2).broadcast_to([TS, NB, P]),
                       ALU.mult).then_inc(wk_done, 1)
                if p == 1:
                    dve.wait_ge(sc1_ready, val(0, 1, m, 1))
                    tt(Dm.rearrange("p (c t) -> p c t", c=4), MX[:, 1, :].rearrange("p (c t) -> p c t", c=4),
                       cm.unsqueeze(1).broadcast_to([P, 4, P]), ALU.add).then_inc(arg_done, 1)
                    dve.wait_ge(ab_done, val(0, 1, m, 1))
                    chain(tt(qa[:, 0:TP], q1[:, 0:TP], aB, ALU.mult))
                    dve.wait_ge(Dexp_done, val(0, 4, m, 4))
                    tt(Dm, Dm, MX[:, 0, :], ALU.mult).then_inc(P_done, 1)
                if p == 2:
                    dve.wait_ge(G_ready, val(0, 1, m, 1))
                    dve.wait_ge(sb_done, val(0, 1, m, 1))
                    dve.wait_ge(Sp_out, val(16, 16, m))
                    chain(cp(S[:, 0, :], MX[:, 1, 0:DV]))
                    chain(cp(nn[:, 0:1], MX[:, 3, 0:1]))
                    for ch in range(1, 4):
                        al = aB[:, P * ch + P - 1:P * ch + P]
                        chain(stt(S[:, ch, :], S[:, ch - 1, :], al, MX[:, 1 + ch // 2, DV * (ch % 2):DV * (ch % 2) + DV],
                                  ALU.mult, ALU.add))
                        chain(stt(nn[:, ch:ch + 1], nn[:, ch - 1:ch], al, MX[:, 3, ch:ch + 1], ALU.mult, ALU.add))
                        chain(ts(qn[:, P * ch:P * ch + P], qa[:, P * ch:P * ch + P], nn[:, ch - 1:ch], None, ALU.mult))
                    cp(nout[:, ds(h + 64, 1)], nn[:, 3:4]).then_inc(S_done, 1)
                    tt(Ds[0:TS, :], sB[0:TS, 0, :], sm[0:TS, :], ALU.add).then_inc(dsarg_done, 1)
                    chain(tt(qa[:, TP:T], q1[:, TP:T], sB[:, 1, :], ALU.mult))
                    chain(tt(qn[:, TP:T].rearrange("p (b t) -> p b t", t=ND), qa[:, TP:T].rearrange("p (b t) -> p b t", t=ND),
                             nsT[:, :, ds(h, 1)].broadcast_to([P, NB, ND]), ALU.mult))
                    dve.wait_ge(dsexp_done, val(0, 1, m, 1))
                    tt(Ds[0:TS, :], Ds[0:TS, :], MX[0:TS, 3, 64:64 + TS], ALU.mult).then_inc(Ps_done, 1)
                if p == 4:
                    dve.wait_ge(abs_done, val(0, 1, m, 1))
                    dve.wait_ge(emt_done, val(0, 2, m, 2))
                    chain(tt(Dm, Dm, emt[:, 0:TP], ALU.max))
                    chain(dve.reciprocal(Dm, Dm))
                    chain(tt(hh[:, :, 0:TP], MX[:, 0:2, :], Dm.unsqueeze(1).broadcast_to([P, 2, TP]), ALU.mult))
                if p == 5:
                    dve.wait_ge(abss_done, val(0, 1, m, 1))
                    qs_ = qn[:, TP:T]
                    chain(tt(qs_, qs_, emt[:, TP:T], ALU.max))
                    chain(dve.reciprocal(qs_, qs_))
                    tt(hh[:, :, TP:T], MX[:, 3, 0:64].rearrange("p (a t) -> p a t", a=2),
                       qs_.unsqueeze(1).broadcast_to([P, 2, TS]), ALU.mult).then_inc(hout_done, 1)
                if p == 7:
                    dve.wait_ge(cu_ready, val(0, 1, m, 1))
                    for b in range(NB):
                        stt(cs[:, b, :], cs[:, b, :], sB[:, 1, ND * b + 3:ND * b + 4],
                            MX[:, b // 2, DV * (b % 2):DV * (b % 2) + DV], ALU.mult, ALU.add).then_inc(cnew_done, 1)
                if p == 8:
                    dve.wait_ge(ss1_ready, val(0, 1, m, 1))
                    ts(two(qa), MX[:, 1:3, 0:HT], 1.0 / DV, EPS, ALU.mult, ALU.add).then_inc(ms1_done, 1)
                    no = nout[:, 0:64].rearrange("p (b h) -> p b h", b=NB)[:, :, ds(h, 1)].rearrange("p b o -> p (b o)")
                    al = sB[:, 1, :].rearrange("p (b t) -> p b t", t=ND)[:, :, 3]
                    ns = nsT[:, :, ds(h, 1)].rearrange("p b o -> p (b o)")
                    chain(tt(no, ns, al, ALU.mult))
                    chain(tt(no, no, MX[:, 0, 0:NB], ALU.add))
                    dve.wait_ge(rt1_done, val(0, 1, m, 1))
                    chain(dve.reciprocal(qa, qa))
                    chain(tt(hh, hh, qa.unsqueeze(1).broadcast_to([P, 2, T]), ALU.mult))
                    for blk in range(2):
                        ob = obuf[:, ds(h * 2 + blk, 1), :].rearrange("p o t -> p (o t)")
                        last = stt(ob, hh[:, blk, :], gT[:, ds(h * 2 + (64 + blk), 1)], ob, ALU.mult, ALU.mult)
                        if blk == 0:
                            chain(last)
                    last.then_inc(head_done, 1)

            def empty1(it, e, seen):
                kind = L1K[e]
                r, c = it
                h = c if r is None else r + c
                order = e + 1
                if kind == "Z":
                    empty_z("l1", it, e, h * 2 + seen, val(4 * GR, 4, it, order))
                if kind == "O":
                    dve.wait_ge(th_done, val(4 * GR, 4, it, order))
                    dve.wait_ge(*freed_at("l1", it, e - 1))
                    ob = obuf[:, ds(h * 2 + seen, 1), :].rearrange("p o t -> p (o t)")
                    stt(ob, misc[:, :], 1.0, ob, ALU.add, ALU.mult).then_inc(freed["d"], 1)

            def layer1(it, m):
                seen = dict.fromkeys("ZOQKV", 0)
                for e in range(len(L1K) + 1):
                    if e:
                        empty1(it, e - 1, seen[L1K[e - 1]])
                        seen[L1K[e - 1]] += 1
                    if e < len(L1K):
                        split_lo("l1", it, e + 1)
                    if m is not None:
                        if e:
                            memory(m, 2 * e - 1)
                        if e < len(L1K):
                            memory(m, 2 * e)

            LOOP_M = 1 + (2 + 9 + 2) + 3 + 2 + (2 + 2 + 1)
            layer1((None, 0), None)
            with dve.Fori(0, MH - 1) as r:
                chain.enter(r, LOOP_M)
                layer1((r, 1), (r, 0))
            chain.leave(MH - 1)
            for p in range(16):
                memory((None, MH - 1), p)
            dve.wait_ge(nT_ps, 1)
            cp(area(A1, "wk")[0:72, 0:P], MX[0:72, 0, 0:P]).then_inc(nT_done, 1)
            dve.wait_ge(head_done, 1 + MH)
            split_out(3)
            dve.wait_ge(cs_out, 16 * MH)
            dve.wait_ge(Sp_out, 16 + 16 * MH)
            out_product("out1")
            residual(1, 4)
            for t in range(5):
                n = P if t < 4 else TS
                dve.wait_ge(fin_ready, t + 1)
                if t >= 2:
                    dve.wait_ge(y_out[t % 2], 16 * (t // 2))
                for b in range(2, 4):
                    cp(raw[t % 2][0:n, 512 * b:512 * b + 512], MX[0:n, b, :]).then_inc(fin_d, 1)


_INS = ["x_prompt", "x_sample", "c_prompt", "c_sample", "cache_k", "cache_v", "state_C", "state_n", "state_m",
        "w_ada", "b_ada", "g_pre", "g_post", "w_in_attn", "sinks", "w_out_attn", "w_in_mlstm", "b_if_mlstm",
        "g_head_mlstm", "w_out_mlstm"]
_OUTS = [(1, TP, D), (NB, ND, D), (1, 1, WIN, KVH, HD), (1, 1, WIN, KVH, HD), (1, NB, WIN, KVH, HD),
         (1, NB, WIN, KVH, HD), (1, 1, MH, DK, DV), (1, 1, MH, DK), (1, 1, MH), (1, NB, MH, DK, DV),
         (1, NB, MH, DK), (1, NB, MH)]


def kernel(**inputs):
    import concourse.bacc as _bacc
    from concourse.bass_utils import run_bass_kernel_spmd as _run

    nc = _bacc.Bacc("TRN2", target_bir_lowering=False, num_devices=1)
    arrays, args = {}, []
    given = [(n, np.ascontiguousarray(inputs[n])) for n in _INS] + [("const", constants())]
    for name, a in given:
        arrays[f"in_{name}"] = a
        args.append(nc.dram_tensor(f"in_{name}", a.shape, mybir.dt.from_np(a.dtype), kind="ExternalInput").ap())
    for i, shape in enumerate(_OUTS):
        args.append(nc.dram_tensor(f"out_{i}", shape, F32, kind="ExternalOutput").ap())
    args.append(nc.dram_tensor("x_spill", (P, KT * T), F32, kind="Internal").ap())
    trunk(nc, *args)
    r = _run(nc, [arrays], core_ids=[0])
    return tuple(r.results[0][f"out_{i}"] for i in range(len(_OUTS)))
```

```python
from contextlib import ExitStack

import numpy as np
import concourse.bass as bass
from concourse import mybir

F32 = mybir.dt.float32
F32R = mybir.dt.float32r
ALU = mybir.AluOpType
ACT = mybir.ActivationFunctionType
AX = mybir.AxisListType.X
ds = bass.ds

P = 128
D = 2048
KT = D // P
TP = 512
NB, ND = 8, 4
TS = NB * ND
T = TP + TS
HT = T // 2
NSEQ = 1 + NB
WIN = 128
QH, KVH, HD = 32, 8, 64
GR = 4
MH, DK, DV = 8, 128, 256
NC_ = TP // P
EPS = 1e-6
BIG = -1e30

OWNER = dict(A="d", Z="d", O="d", Q="a", K="a", V="a", Y="a", G="a")
L0K = "VQQQQKZZZZ"
L1K = "QKVVZOZO"
PHASES = [("ada0", 1, "A" * 8), ("l0", GR, L0K), ("out0", 1, "Y" * KT), ("gate", 1, "G"),
          ("l1", MH, L1K), ("out1", 1, "Y" * KT)]


def first_of(kinds, size):
    return {ph: sum(n * sum(size(k) for k in ks) for p, n, ks in PHASES[:i])
            for i, (ph, _, _) in enumerate(PHASES)}


UNITS = dict.fromkeys("ZOQKVYG", 1) | {"A": 8}
KINDS = {ph: ks for ph, _, ks in PHASES}
ITERS = {ph: n for ph, n, _ in PHASES}
ENTRY0 = first_of(PHASES, lambda k: 1)
UNIT0 = first_of(PHASES, lambda k: UNITS[k])
FREED0 = {w: first_of(PHASES, lambda k, w=w: int(OWNER[k] == w)) for w in "ad"}
RAW0 = UNIT0["l0"]

SEGS = dict(out0=[(0, 2, None), (2, 4, (0, 2 * D, 8)), (6, 8, (1, 0, 12))],
            out1=[(0, 2, None), (2, 4, (1, 2 * D, 20)), (6, 8, None)])
SQ_PARTS = {(5, 3): range(0, 4), (5, 7): range(4, 8), (6, 3): range(8, 12), (6, 7): range(12, KT)}
STRIPS = 8
RING = 4
PIECES = [(kg, t) for kg in range(4) for t in range(5)]
SW = 2 * 512

C_ID, C_ONE, C_SLP, C_SLS, C_SEL = 0, 128, 256, 288, 296
C_FIX = 305
C_NEGD, C_NEGS = 305, 305 + 768
C_L0 = C_NEGS + 1056
C_CM, C_SM, C_BM = C_L0, C_L0 + 128, C_L0 + 160
C_ALL = C_L0 + 168


def constants():
    c = np.zeros((P, C_ALL), np.float32)
    c[:, C_ID:C_ID + P] = np.eye(P)
    c[:, C_ONE:C_ONE + P] = 1.0
    slopes = (2.0 ** (-8.0 * np.arange(1, QH + 1) / QH)).astype(np.float32)
    c[:, C_SLP:C_SLP + QH] = slopes
    p = np.arange(P)
    for m in range(GR):
        for half in range(2):
            c[:, C_SLS + 2 * m + half] = slopes[8 * m + 4 * (p // 64) + 2 * (p // 32 % 2) + half]
    for r in range(2 * NSEQ):
        c[32 + r, C_SEL + r % NSEQ] = 1.0
    c[32 + 2 * NSEQ, C_SEL:C_SEL + NSEQ] = 1.0
    q, k = np.arange(P)[:, None], np.arange(2 * P)[None, :]
    d = q + P - k
    neg = np.where((d >= 0) & (d < WIN), -d.astype(np.float32), BIG)
    first = np.where(k < P, BIG, neg)
    c[:, C_NEGD:C_NEGD + 768] = np.concatenate([first, neg, neg], 1)
    tok = p % TS
    b, t = (tok // ND)[:, None], (tok % ND)[:, None]
    j = np.arange(NB * WIN)[None, :]
    dc = t + WIN - j % WIN
    c[:, C_NEGS:C_NEGS + 1024] = np.where((j // WIN == b) & (dc < WIN), -dc, BIG)
    j = np.arange(TS)[None, :]
    dn = t - j % ND
    c[:, C_NEGS + 1024:C_NEGS + 1056] = np.where((j // ND == b) & (dn >= 0), -dn, BIG)
    s, t = np.arange(P)[:, None], np.arange(P)[None, :]
    c[:, C_CM:C_CM + P] = np.where(s <= t, 0.0, BIG)
    s, t = np.arange(TS)[:, None], np.arange(TS)[None, :]
    c[0:TS, C_SM:C_SM + TS] = np.where((s // ND == t // ND) & (s <= t), 0.0, BIG)
    c[0:TS, C_BM:C_BM + NB] = (np.arange(TS)[:, None] // ND == np.arange(NB)[None, :])
    return c


ARENA = 12520


def offsets(sizes, at=0):
    out = {}
    for name, size in sizes:
        out[name] = (at, size)
        at += size
    assert at <= ARENA, at
    return out


UW = offsets([(f"lo{i}", SW) for i in range(RING)] + [(f"hi{i}", SW) for i in range(RING)])
XW = offsets([("x", KT * T), ("sq", 2 * T), ("r", T), ("vec", P)])
A0 = offsets([("q", 4 * TP), ("qs", P), ("kT", P + T), ("kS", P + T), ("vT", T), ("vtok", TP),
              ("vks", 256), ("kout", P), ("ckraw", 1024), ("cv", 1024), ("ckT", 1024), ("ckS", 1024),
              ("soft", 1536), ("negd", 768), ("negs", 1056)])
A1 = offsets([("q", T), ("k", T), ("v", 2 * T), ("vtok", 4 * DV), ("wk", 4 * P), ("rows", 3 * T),
              ("S", 4 * DV), ("n", 8), ("D", TP), ("qa", T), ("qn", T), ("emt", T), ("h", 2 * T),
              ("cs", NB * DV), ("sb", 3 * TS), ("Ds", TS), ("Uc", 40), ("wc", 40), ("wb", 64),
              ("nsT", 64), ("nout", 72), ("cm", 128), ("sm", 32), ("bm", 8)])


SLOW = dict(allow_slow_non_contiguous=True)


def val(base, per, it, k=0):
    r, c = it
    n = base + c * per + k
    return n if r is None else r * per + n


def fixed(eng, value):
    return value if isinstance(value, int) else eng.snap(eng.to_reg(value))


class Chain:

    def __init__(self, eng, sem):
        self.eng, self.sem, self.base, self.k, self.it, self.per = eng, sem, 0, 0, (None, 0), 0

    def __call__(self, ins):
        self.k += 1
        ins.then_inc(self.sem, 1)
        self.eng.wait_ge(self.sem, val(self.base, self.per, self.it, self.k))

    def enter(self, reg, per):
        self.base, self.k, self.it, self.per = self.base + self.k, 0, (reg, 0), per

    def leave(self, iters):
        assert self.k == self.per, f"a loop body has {self.k} steps, not {self.per}"
        self.base, self.k, self.it, self.per = self.base + iters * self.per, 0, (None, 0), 0


def trunk(nc, x_prompt, x_sample, c_prompt, c_sample, cache_k, cache_v, state_C, state_n, state_m,
          w_ada, b_ada, g_pre, g_post, w_in_attn, sinks, w_out_attn, w_in_mlstm, b_if_mlstm,
          g_head_mlstm, w_out_mlstm, const,
          y_prompt, y_sample, nk_p, nv_p, nk_s, nv_s, nC_p, nn_p, nm_p, nC_s, nn_s, nm_s, x_spill):
    with ExitStack() as ctx:
        def sb(name, shape, dt=F32):
            return ctx.enter_context(nc.sbuf_tensor(name, shape, dt))

        def sem(name):
            return ctx.enter_context(nc.semaphore(name))

        h_hi = sb("h_hi", [P, KT, T], F32R)
        h_lo = sb("h_lo", [P, KT, T], F32R)
        obuf = sb("obuf", [P, KT, T])
        raw = [sb(f"raw{i}", [P, D]) for i in range(2)]
        w_hi = [sb(f"w_hi{i}", [P, D], F32R) for i in range(2)]
        w_lo = [sb(f"w_lo{i}", [P, D], F32R) for i in range(2)]
        cT = sb("cT", [P, 16 * 18 + 110], F32R)
        modT = sb("modT", [P, 96, NSEQ])
        misc = sb("misc", [P, T])
        gT = sb("gT", [P, 80])
        fix = sb("fix", [P, C_FIX])
        nsink = sb("nsink", [P, QH + 8])
        st = sb("st", [P, 40])
        warm = sb("warm", [P, 1])
        with nc.sbuf_tensor("strips", [P, 2 * RING * SW], F32R) as strips:
            pass
        arena = sb("arena", [P, ARENA])
        PJ = ctx.enter_context(nc.psum_tensor("PJ", [P, 4, 512], F32))
        MX = ctx.enter_context(nc.psum_tensor("MX", [P, 4, 512], F32))

        def area(table, name):
            a, n = table[name]
            return arena[:, a:a + n]

        ident = fix[:, C_ID:C_ID + P]
        ones = fix[:, C_ONE:C_ONE + P]
        xw = area(XW, "x").rearrange("p (k t) -> p k t", k=KT)
        xflat = area(XW, "x")
        sqb = area(XW, "sq").rearrange("p (a t) -> p a t", a=2)
        rB = area(XW, "r")
        gvec = area(XW, "vec")[0:80, :]
        c_rows = area(XW, "x")[0:NSEQ, 0:D]
        c_tanh = area(XW, "x")[0:NSEQ, D:2 * D]
        c_full = area(XW, "x")[:, 2 * D:2 * D + KT * NSEQ]
        u_raw = [area(UW, f"lo{i}") for i in range(RING)]
        u_lo = [strips[:, SW * i:SW * i + SW] for i in range(RING)]
        u_hi = [strips[:, SW * (RING + i):SW * (RING + i + 1)] for i in range(RING)]
        q0 = area(A0, "q").rearrange("p (j t) -> p j t", j=4)
        qS = area(A0, "qs")
        kT, kS = area(A0, "kT"), area(A0, "kS")
        vT, vtok = area(A0, "vT"), area(A0, "vtok")
        vks, kout = area(A0, "vks"), area(A0, "kout")
        ckraw = area(A0, "ckraw").rearrange("p (b c) -> p b c", b=NB)
        PTs, PTn = area(A0, "ckraw"), area(A0, "soft")[0:TS, 1056:1184]
        cv = area(A0, "cv").rearrange("p (b c) -> p b c", b=NB)
        ckT, ckS = area(A0, "ckT"), area(A0, "ckS")
        soft = area(A0, "soft")
        SPs = soft[:, 0:1056]
        PP = [soft[:, 0:512], soft[:, 512:1024]]
        PT = soft[:, 1024:1536]
        negd, negs = area(A0, "negd"), area(A0, "negs")
        q1, k1, v1 = area(A1, "q"), area(A1, "k"), area(A1, "v").rearrange("p (a t) -> p a t", a=2)
        hsq = v1
        vt1 = area(A1, "vtok").rearrange("p (c e) -> p c e", c=4)
        wk = area(A1, "wk").rearrange("p (c e) -> p c e", c=4)
        rows = area(A1, "rows")
        wks = rows[0:TS, 0:1024].rearrange("p (b e) -> p b e", b=NB)
        ksv = rows[0:TS, 1024:1408]
        ks, vs = ksv[:, 0:P], ksv[:, P:3 * P]
        wbh = rows[0:TS, 1408:1416]
        GP = slice(64, 64 + MH)
        BP = slice(96, 96 + MH)
        R = rows[GP, :].rearrange("p (j t) -> p j t", j=3)
        RB = rows[BP, :].rearrange("p (j t) -> p j t", j=3)
        S = area(A1, "S").rearrange("p (c e) -> p c e", c=4)
        nn = area(A1, "n")
        Dm = area(A1, "D")
        qa, qn, emt = area(A1, "qa"), area(A1, "qn"), area(A1, "emt")
        hh = area(A1, "h").rearrange("p (a t) -> p a t", a=2)
        aB = area(A1, "h")[:, 0:TP]
        cs = area(A1, "cs").rearrange("p (b e) -> p b e", b=NB)
        sB = area(A1, "sb").rearrange("p (j t) -> p j t", j=3)
        Ds = area(A1, "Ds")
        Uc, wc = area(A1, "Uc"), area(A1, "wc")
        wb = area(A1, "wb").rearrange("p (h b) -> p h b", h=MH)
        nsT = area(A1, "nsT").rearrange("p (b h) -> p b h", b=NB)
        nout = area(A1, "nout")
        cm, sm, bm = area(A1, "cm"), area(A1, "sm"), area(A1, "bm")
        LI = area(A1, "h")[GP, 0:T]
        LF = area(A1, "h")[GP, T:2 * T]
        Ub = area(A1, "qa")[GP, :]
        Wr = area(A1, "qn")[GP, :]
        Bc = area(A1, "emt")[GP, :]
        Mr = area(A1, "S")[GP, 0:T]
        tg = area(A1, "D")[GP, 0:16]
        m0s = area(A1, "D")[GP, 16:24]
        bif = area(A1, "D")[GP, 24:26]
        nrow = area(A1, "wk")[0:64, 0:P]

        const_in, mask_in = sem("const_in"), sem("mask_in")
        c_in = sem("c_in")
        vec_in = sem("vec_in")
        sink_in = sem("sink_in")
        x_in = [sem("x_in0"), sem("x_in1")]
        a0_in = [sem(f"a0_in{i}") for i in range(4)]
        w_in = [sem("w_in0"), sem("w_in1")]
        hi_done = sem("hi_done")
        lo_done = sem("lo_done")
        w_used = sem("w_used")
        freed = {"a": sem("freed_a"), "d": sem("freed_d")}
        u_in = [sem(f"u_in{i}") for i in range(RING)]
        u_hi_done, u_lo_done = sem("u_hi_done"), sem("u_lo_done")
        u_used = sem("u_used")
        mod_taken = sem("mod_taken")
        sums_ready = sem("sums_ready")
        mod_copied, mod_turned, bias_in = sem("mod_copied"), sem("mod_turned"), sem("bias_in")
        ct_rows, ct_ps, ct_ready = sem("ct_rows"), sem("ct_ps"), sem("ct_ready")
        ct_tanh, ct_full = sem("ct_tanh"), sem("ct_full")
        vec_ps, g_ready = sem("vec_ps"), sem("g_ready")
        xt_done = sem("xt_done")
        xe_a, xe_d = sem("xe_a"), sem("xe_d")
        sq_made, sq_used = sem("sq_made"), sem("sq_used")
        ms_ready, rt_ready = sem("ms_ready"), sem("rt_ready")
        spilled, reloaded = sem("spilled"), sem("reloaded")
        x_ready = sem("x_ready")
        y_scaled = sem("y_scaled")
        acc_done = sem("acc_done")
        warm_set = sem("warm_set")
        xs_done = sem("xs_done")
        A_ready = sem("A_ready")
        hs_done, hs_hi, hs_ready = sem("hs_done"), sem("hs_hi"), sem("hs_ready")
        hh_hi = sem("hh_hi")
        h_ready = sem("h_ready")
        dch, ach = sem("dch"), sem("ach")
        pads = sem("pads")
        tv_ready, tv_done = sem("tv_ready"), sem("tv_done")
        kv_stored = sem("kv_stored")
        ck_in, cv_in = sem("ck_in"), sem("cv_in")
        ck_ready, ck_done = sem("ck_ready"), sem("ck_done")
        ss_ready, smax_ready, sexp_ready, sp_ready = (sem("ss_ready"), sem("smax_ready"),
                                                      sem("sexp_ready"), sem("sp_ready"))
        ts_ready, pts_done, pvs_ready = sem("ts_ready"), sem("pts_done"), sem("pvs_ready")
        sc_ready, pmax_ready, pexp_ready, pn_ready = (sem("sc_ready"), sem("pmax_ready"),
                                                      sem("pexp_ready"), sem("pn_ready"))
        tr_ready, pt_done, pv_ready = sem("tr_ready"), sem("pt_done"), sem("pv_ready")
        om_done = sem("om_done")
        gl_in, gate_done = sem("gl_in"), sem("gate_done")
        gate_d, gate_a = sem("gate_d"), sem("gate_a")
        gate_ps, gate_v, gate_cols = sem("gate_ps"), sem("gate_v"), sem("gate_cols")
        tr1_ready, vt_done, wk_done, rb_done = sem("tr1_ready"), sem("vt_done"), sem("wk_done"), sem("rb_done")
        sc1_ready, arg_done, ab_done, emt_done = (sem("sc1_ready"), sem("arg_done"), sem("ab_done"),
                                                  sem("emt_done"))
        Dexp_done, P_done = sem("Dexp_done"), sem("P_done")
        G_ready, sb_done, S_done = sem("G_ready"), sem("sb_done"), sem("S_done")
        dsarg_done, dsexp_done, Ps_done = sem("dsarg_done"), sem("dsexp_done"), sem("Ps_done")
        num_ready, nums_ready, abs_done, abss_done = (sem("num_ready"), sem("nums_ready"),
                                                      sem("abs_done"), sem("abss_done"))
        hout_done, hsq_done = sem("hout_done"), sem("hsq_done")
        cu_ready, cnew_done, ss1_ready = sem("cu_ready"), sem("cnew_done"), sem("ss1_ready")
        ms1_done, rt1_done, head_done = sem("ms1_done"), sem("rt1_done"), sem("head_done")
        th_done = sem("th_done")
        cs_in, cs_out, Sp_out = sem("cs_in"), sem("cs_out"), sem("Sp_out")
        nT_ps, nT_done = sem("nT_ps"), sem("nT_done")
        fin_ready, fin_a = sem("fin_ready"), sem("fin_a")
        out_done = sem("out_done")
        y_out = [sem("y_out0"), sem("y_out1")]

        def freed_at(ph, it, e):
            names = [p for p, _, _ in PHASES]
            while e < 0:
                r, c = it
                if r is None and c == 0:
                    ph = names[names.index(ph) - 1]
                    it = (None, ITERS[ph] - 1)
                else:
                    it = (r, c - 1)
                e += len(KINDS[ph])
            w = OWNER[KINDS[ph][e]]
            per = sum(OWNER[k] == w for k in KINDS[ph])
            upto = sum(OWNER[k] == w for k in KINDS[ph][:e + 1])
            return freed[w], val(FREED0[w][ph], per, it, upto)

        def unit_no(ph, it, e, j=0):
            ks = KINDS[ph]
            return val(UNIT0[ph], sum(UNITS[k] for k in ks), it, sum(UNITS[k] for k in ks[:e]) + j)

        def ended(ph, it, e):
            return unit_no(ph, it, e, UNITS[KINDS[ph][e]])

        def slot_of(ph, e, j=0):
            return (UNIT0[ph] + sum(UNITS[k] for k in KINDS[ph][:e]) + j) % 2

        def pair_of(ph, e):
            return (ENTRY0[ph] + e) % 2

        def landed_at(ph, it, e, j=0):
            ks = KINDS[ph]
            per = sum(UNITS[k] for k in ks)
            at = UNIT0[ph] + sum(UNITS[k] for k in ks[:e]) + j - RAW0
            r, c = it
            n = 16 * ((at + c * per) // 2 + 1)
            return n if r is None else r * (8 * per) + n

        def pj(pair, parts=slice(0, P)):
            return PJ[parts, 2 * pair:2 * pair + 2, 0:HT]

        def two(ap):
            return ap.rearrange("p (a t) -> p a t", a=2)

        def per_seq(ap):
            return ap.unsqueeze(3).broadcast_to([P, ap.shape[1], NB, ND])

        def attend_points(e, i):
            p = 3 * (e - L0K.index("Z")) + i
            return (0, p) if p >= 0 else (1, 3 * (len(L0K) - L0K.index("Z") + e) + i)

        def memory_points(e, i):
            p = 2 * (e - L1K.index("Z")) + i
            return (0, p) if p >= 0 else (1, 2 * (len(L1K) - L1K.index("Z") + e) + i)

        def half_unit(w, u):
            return w[u // 2 % 2][:, SW * (u % 2):SW * (u % 2) + SW].rearrange("p (k n) -> p k n", k=2)

        def half_raw(u):
            k = 2 * (u % 8)
            return obuf[:, k:k + 2, 0:512]

        def blocks_of(eng, ph, seg):
            k0, n, _ = seg
            with eng.Fori(0, n // 2) as r:
                for i in range(2):
                    yield r, i, k0 + i

        block = ctx.enter_context(nc.Block())

        @block.sync
        def _(sp):
            ada = w_ada.rearrange("l (k p) n -> p l k n", p=P)
            win0 = w_in_attn[0].rearrange("(k p) n -> p k n", p=P)
            win1 = w_in_mlstm[0].rearrange("(k p) n -> p k n", p=P)
            wout = [w_out_attn[0].rearrange("(k p) n -> p k n", p=P),
                    w_out_mlstm[0].rearrange("(k p) n -> p k n", p=P)]
            def load(ph, it, e, j, src, dst_cols=D):
                s = slot_of(ph, e, j)
                if not (ph == "l0" and it[0] is None and e < 2):
                    split = fixed(sp, unit_no(ph, it, e, j - 1))
                    sp.wait_ge(xt_done, 5)
                    sp.wait_ge(lo_done, split)
                k = src.shape[1]
                sp.dma_start(raw[s][:, 0:dst_cols].rearrange("p (k n) -> p k n", k=k), src)\
                    .then_inc(w_in[s], 16)

            def load_entry(it, e):
                r, c = it
                g = c if r is None else r + c
                kind, n = L0K[e], L0K[:e].count(L0K[e])
                start, per = dict(Q=(0, 512), K=(2048, 128), V=(2560, 128), Z=(3072, 512))[kind]
                load("l0", it, e, 0, win0[:, :, ds(g * per + (start + P * n), P)])

            sp.wait_ge(c_in, 32)
            for u in range(32):
                if u >= 4:
                    sp.wait_ge(lo_done, 2 * (u - 3))
                if u == 28:
                    sp.wait_ge(xt_done, 5)
                    for e in range(2):
                        load_entry((None, 0), e)
                slot = obuf[:, 4 * (u % 4):4 * (u % 4) + 4, 0:512]
                sp.dma_start(slot, ada[:, 0, 4 * (u % 4):4 * (u % 4) + 4,
                                       512 * (u // 4):512 * (u // 4) + 512]).then_inc(a0_in[u % 4], 16)

            for e in range(2, len(L0K)):
                load_entry((None, 0), e)
            with sp.Fori(0, GR - 1) as r:
                for e in range(len(L0K)):
                    load_entry((r, 1), e)

            def out_units(ph, w, arena_free=()):
                load(ph, (None, 0), 0, 0, w[:, :, 0:P])

                def block(k, s, split):
                    before = fixed(sp, split)
                    sp.wait_ge(xt_done, 5)
                    sp.wait_ge(lo_done, before)
                    sp.dma_start(raw[s][:, :].rearrange("p (k n) -> p k n", k=KT), w[:, :, ds(k * P, P)])\
                        .then_inc(w_in[s], 16)

                for seg in SEGS[ph]:
                    if seg[2]:
                        for se, v in arena_free:
                            sp.wait_ge(se, v)
                    for r, i, k in blocks_of(sp, ph, seg):
                        block(r * 2 + (k + 1), slot_of(ph, k + 1), r * 2 + (UNIT0[ph] + k))
                        if seg[2] is None:
                            continue
                        l, col, group = seg[2]
                        first = STRIPS * (group - 8 + i)
                        for j in range(STRIPS):
                            free = fixed(sp, r * (2 * STRIPS) + (first + j + 1))
                            sp.wait_ge(xt_done, 5)
                            sp.wait_ge(u_used, free)
                            sp.dma_start(u_raw[j % RING].rearrange("p (k n) -> p k n", k=2),
                                         ada[:, l, 2 * j:2 * j + 2, ds(r * 1024 + (col + 512 * i), 512)])\
                                .then_inc(u_in[j % RING], 16)
                block(KT - 1, slot_of(ph, KT - 1), UNIT0[ph] + KT - 2)

            sp.wait_ge(xt_done, 5)
            out_units("out0", wout[0], [(kv_stored, 32 + 64 * GR)])
            load("gate", (None, 0), 0, 0, win1[:, :, 8192:8208], KT * 16)

            def layer1(it):
                r, c = it
                h = c if r is None else r + c
                seen = dict.fromkeys("ZOQKV", 0)
                start = dict(Q=0, K=1024, V=2048, O=4096, Z=6144)
                for e, kind in enumerate(L1K):
                    width = P if kind in "QK" else DV
                    load("l1", it, e, 0, win1[:, :, ds(h * width + (start[kind] + P * seen[kind]), P)])
                    seen[kind] += 1

            layer1((None, 0))
            with sp.Fori(0, MH - 1) as r:
                layer1((r, 1))
            out_units("out1", wout[1], [(head_done, 1 + MH), (cs_out, 16 * MH), (Sp_out, 16 + 16 * MH),
                                        (out_done, 48)])

            for n, (kg, t) in enumerate(PIECES):
                sp.wait_ge(fin_a, n + 1)
                rows_, cols = (P if t < 4 else TS), slice(512 * kg, 512 * kg + 512)
                dst = y_prompt[0, P * t:P * t + P, cols] if t < 4 else y_sample.rearrange("b t d -> (b t) d")[:, cols]
                sp.dma_start(dst, raw[n // 4 % 2][0:rows_, 512 * (n % 4):512 * (n % 4) + 512])\
                    .then_inc(y_out[n // 4 % 2], 16)
            sp.wait_ge(y_out[0], 16 * 12)
            sp.wait_ge(y_out[1], 16 * 8)

        @block.gpsimd
        def _(pool):
            bada = b_ada.rearrange("l n -> (l n)").unsqueeze(0)
            brow = misc[50:51, 0:512]

            def bias(a, first=False):
                if not first:
                    pool.wait_ge(mod_turned, a)
                pool.dma_start(brow, bada[:, ds(a * 512, 512)]).then_inc(bias_in, 16)

            for t in range(5):
                if t >= 2:
                    pool.wait_ge(xt_done, t - 1)
                if t < 4:
                    pool.dma_start(raw[t % 2][:, :], x_prompt[0, P * t:P * t + P, :]).then_inc(x_in[t % 2], 16)
                else:
                    pool.dma_start(raw[0][0:TS, :], x_sample.rearrange("b t d -> (b t) d"))\
                        .then_inc(x_in[0], 16)
                if t:
                    bias(t - 1, t == 1)
                if t == 1:
                    pool.dma_start(nsink[:, 0:QH], sinks.broadcast_to([P, QH])).then_inc(sink_in, 16)
                    for a in range(2):
                        for bl in range(2):
                            src = sinks.rearrange("o (m a l h) -> (o a l) m h", m=GR, a=2, l=2)[2 * a + bl]
                            p0 = 64 * a + 32 * bl
                            for h in range(2):
                                dst = nsink[p0:p0 + 32, QH + 4 * h:QH + 4 * h + 4]
                                pool.dma_start(dst, src[:, h:h + 1].rearrange("m h -> h m").broadcast_to([32, GR]), **SLOW)\
                                    .then_inc(sink_in, 16)
            for a in range(4, 8):
                bias(a)
            pool.wait_ge(xe_a, 10)
            pool.wait_ge(xe_d, 10)
            pool.dma_start(x_spill, xflat).then_inc(spilled, 16)
            pool.wait_ge(spilled, 16)
            pool.wait_ge(h_ready, KT)
            pool.dma_start(area(A0, "negd"), const[:, C_NEGD:C_NEGD + 768]).then_inc(mask_in, 16)
            pool.dma_start(area(A0, "negs"), const[:, C_NEGS:C_NEGS + 1056]).then_inc(mask_in, 16)

            def caches(g):
                pool.dma_start(ckraw, cache_k[0].rearrange("b w h d -> w b (h d)")[:, :, ds(g * P, P)])\
                    .then_inc(ck_in, 16)
                pool.dma_start(cv, cache_v[0].rearrange("b w h d -> w b (h d)")[:, :, ds(g * P, P)])\
                    .then_inc(cv_in, 16)

            def store_kv(it):
                r, c = it
                m = c if r is None else r + c
                pool.wait_ge(h_ready, KT)
                pool.wait_ge(tv_done, val(0, 4, it, 4))
                flat = "o b w h d -> (o b) w (h d)"
                pool.dma_start(nk_p.rearrange(flat)[0][:, ds(m * P, P)], kout).then_inc(kv_stored, 16)
                pool.dma_start(nv_p.rearrange(flat)[0][:, ds(m * P, P)], vtok[:, 384:512]).then_inc(kv_stored, 16)
                for dst, col in ((nv_s, 0), (nk_s, P)):
                    d = dst.rearrange(flat)[:, WIN - ND:WIN, ds(m * P, P)]
                    pool.dma_start(d, vks[0:TS, col:col + P]).then_inc(kv_stored, 16)

            caches(0)
            bias(8)
            pool.dma_start(nk_s[0, :, 0:WIN - ND], cache_k[0, :, ND:WIN]).then_inc(kv_stored, 16)
            pool.dma_start(nv_s[0, :, 0:WIN - ND], cache_v[0, :, ND:WIN]).then_inc(kv_stored, 16)

            def l0_rest(it):
                store_kv(it)
                r, c = it
                pool.wait_ge(h_ready, KT)
                pool.wait_ge(pvs_ready, val(0, 2, it, 2))
                caches(r + (c + 1))

            with pool.Fori(0, GR - 1) as r:
                l0_rest((r, 0))
            store_kv((None, GR - 1))
            pool.wait_ge(kv_stored, 32 + 64 * GR)
            pool.wait_ge(om_done, 1 + 18 * GR)
            with pool.Fori(0, 11) as r:
                group = fixed(pool, r + 9)
                pool.wait_ge(h_ready, KT)
                pool.wait_ge(mod_turned, group)
                pool.dma_start(brow, bada[:, ds(r * 512 + 9 * 512, 512)]).then_inc(bias_in, 16)
            pool.wait_ge(u_used, RING + 12 * STRIPS)
            pool.dma_start(xflat, x_spill).then_inc(reloaded, 16)
            pool.wait_ge(x_ready, KT)
            pool.dma_start(x_spill, xflat).then_inc(spilled, 16)
            pool.wait_ge(spilled, 32)
            pool.wait_ge(h_ready, 3 * KT)
            pool.dma_start(cm, const[:, C_CM:C_CM + 128]).then_inc(gl_in, 16)
            pool.dma_start(sm, const[:, C_SM:C_SM + 32]).then_inc(gl_in, 16)
            pool.dma_start(bm, const[:, C_BM:C_BM + 8]).then_inc(gl_in, 16)
            pool.dma_start(m0s, state_m[0].rearrange("b h -> h b"), **SLOW).then_inc(gl_in, 16)
            pool.dma_start(bif, b_if_mlstm.rearrange("o (g h) -> h (o g)", g=2), **SLOW).then_inc(gl_in, 16)
            pool.dma_start(nrow, state_n[0].rearrange("b h d -> (b h) d")).then_inc(gl_in, 16)
            C_in = state_C[0].rearrange("b h k e -> h k b e")
            C_out = nC_s[0].rearrange("b h k e -> h k b e")
            pool.dma_start(cs, C_in[0]).then_inc(cs_in, 16)
            pool.wait_ge(gate_done, 1)
            pool.dma_start(nm_p.rearrange("o b h -> h (o b)"), R[:, 2, TP - 1:TP], **SLOW).then_inc(Sp_out, 16)
            pool.dma_start(nm_s[0].rearrange("b h -> h b"), R[:, 2, TP:T].rearrange("p (b t) -> p b t", t=ND)[:, :, 3], **SLOW)\
                .then_inc(out_done, 16)

            def states(it, more):
                r, c = it
                h = c if r is None else r + c
                pool.wait_ge(gate_done, 1)
                pool.wait_ge(S_done, val(0, 1, it, 1))
                pool.dma_start(nC_p.rearrange("o b h k e -> (o b h) k e")[ds(h, 1)].rearrange("o k e -> (o k) e"),
                               S[:, 3, :]).then_inc(Sp_out, 16)
                new, at = fixed(pool, val(0, NB, it, NB)), fixed(pool, h)
                pool.wait_ge(gate_done, 1)
                pool.wait_ge(cnew_done, new)
                pool.dma_start(C_out[ds(at, 1)].rearrange("o k b e -> (o k) b e"), cs).then_inc(cs_out, 16)
                if more:
                    pool.wait_ge(gate_done, 1)
                    pool.wait_ge(cs_out, val(0, 16, it, 16))
                    pool.dma_start(cs, C_in[ds(h + 1, 1)].rearrange("o k b e -> (o k) b e")).then_inc(cs_in, 16)

            with pool.Fori(0, MH - 1) as r:
                states((r, 0), True)
            states((None, MH - 1), False)
            pool.wait_ge(nT_done, 1)
            nrow2 = area(A1, "wk")[0:72, 0:P]
            pool.dma_start(nn_s[0].rearrange("b h d -> (b h) d"), nrow2[0:64, :]).then_inc(out_done, 16)
            pool.dma_start(nn_p.rearrange("o b h d -> (o b h) d"), nrow2[64:72, :]).then_inc(out_done, 16)
            pool.wait_ge(out_done, 48)
            pool.wait_ge(cs_out, 16 * MH)
            pool.wait_ge(Sp_out, 16 + 16 * MH)
            pool.wait_ge(head_done, 1 + MH)
            bias(20)
            for a in range(21, 24):
                bias(a)
            pool.wait_ge(u_used, RING + 16 * STRIPS)
            pool.dma_start(xflat, x_spill).then_inc(reloaded, 16)
            pool.wait_ge(reloaded, 32)

        @block.tensor
        def _(pe):
            mm, tr = pe.matmul, pe.transpose

            def ada_products(ph, it, e, mid=None):
                pair = pair_of(ph, e)
                for j in range(8):
                    s = j // 2 % 2
                    pe.wait_ge(lo_done, unit_no(ph, it, e, j) + 1)
                    for k in range(2):
                        lhsT = cT[:, (2 * j + k) * 18:(2 * j + k) * 18 + P]
                        at = SW * (j % 2) + k * 512
                        for w in (w_hi, w_lo):
                            last = mm(PJ[:, 2 * pair, :], lhsT, w[s][:, at:at + 512],
                                      start=(j == 0 and k == 0 and w is w_hi),
                                      stop=(j == 7 and k == 1 and w is w_lo))
                    last.then_inc(w_used, 1)
                    if mid:
                        mid(j)

            def ada_turn(ph, it, e, n):
                pair = pair_of(ph, e)
                pe.wait_ge(mod_copied, n + 1)
                pe.wait_ge(bias_in, n * 16 + 16)
                for j in range(4):
                    last = mm(PJ[:, 2 * pair + 1, 9 * j:9 * j + 9], misc[32:51, P * j:P * j + P],
                              fix[32:51, C_SEL:C_SEL + NSEQ], start=True, stop=True)
                last.then_inc(mod_turned, 1)

            def entry(ph, it, e, points={}, h_base=None):
                s, pair = slot_of(ph, e), pair_of(ph, e)
                se, v = freed_at(ph, it, e - 2)
                pe.wait_ge(se, v)
                pe.wait_ge(lo_done, unit_no(ph, it, e) + 1)
                block(s, pair, points, h_base)

            def block(s, pair, points, h_base):
                if h_base in (0, 2 * KT):
                    pe.wait_ge(hs_ready, h_base // (2 * KT) + 1)
                for k in range(KT):
                    if h_base is not None:
                        pe.wait_ge(h_ready, h_base + k + 1)
                    hi = w_hi[s][:, P * k:P * k + P]
                    lo = w_lo[s][:, P * k:P * k + P]
                    for n, (w, h) in enumerate(((hi, h_hi), (hi, h_lo), (lo, h_hi))):
                        for f in range(2):
                            last = mm(PJ[:, 2 * pair + f, 0:HT], w, h[:, k, HT * f:HT * f + HT],
                                      start=(k == 0 and n == 0), stop=(k == KT - 1 and n == 2))
                    if k == KT - 1:
                        last.then_inc(w_used, 1)
                    if k in points:
                        points[k]()

            pe.wait_ge(const_in, 16)
            pe.wait_ge(vec_in, 48)
            tr(MX[:, 2, 0:80], gvec, ident[0:80, 0:80]).then_inc(vec_ps, 1)
            pe.wait_ge(ct_rows, 1)
            for k in range(KT):
                last = tr(MX[:, 3, NSEQ * k:NSEQ * k + NSEQ], c_rows[:, P * k:P * k + P], ident[0:NSEQ, 0:NSEQ])
            last.then_inc(ct_ps, 1)
            pe.wait_ge(ct_ready, 1)

            def turn_x(t):
                n = P if t < 4 else TS
                pe.wait_ge(x_in[t % 2], 16 * (t // 2 + 1))
                if t:
                    pe.wait_ge(xe_a, 2 * t)
                    pe.wait_ge(xe_d, 2 * t)
                else:
                    pe.wait_ge(g_ready, 1)
                for k in range(KT):
                    last = tr(MX[:, k // 4, n * (k % 4):n * (k % 4) + n], raw[t % 2][0:n, P * k:P * k + P],
                              ident[0:n, 0:n])
                last.then_inc(xt_done, 1)

            def sums(base, blocks=range(KT)):
                for k in blocks:
                    pe.wait_ge(sq_made, base + k + 1)
                    for f in range(2):
                        last = mm(MX[:, f, 0:HT], ones, sqb[:, k % 2, HT * f:HT * f + HT],
                                  start=(k == 0), stop=(k == KT - 1))
                    last.then_inc(sq_used, 1)

            it0 = (None, 0)
            for e in range(8):
                if e >= 2:
                    pe.wait_ge(*freed_at("ada0", it0, e - 2))

                def between(j, e=e):
                    if j == 3 and e:
                        ada_turn("ada0", it0, e - 1, e - 1)
                    if j == 5 and e < 5:
                        turn_x(e)
                    if (e, j + 1) in SQ_PARTS:
                        sums(0, SQ_PARTS[e, j + 1])
                ada_products("ada0", it0, e, between)
            ada_turn("ada0", it0, 7, 7)

            def kv_turn(m):
                se, v = freed_at("l0", m, L0K.index("K"))
                pe.wait_ge(se, v)
                pe.wait_ge(om_done, val(1, 18, m))
                for c in range(4):
                    tr(MX[:, 0, P * c:P * c + P], vT[:, P * c:P * c + P], ident)
                tr(MX[:, 1, 0:P], kT[:, P + 384:P + 512], ident)
                tr(MX[0:TS, 1, P:2 * P], vT[:, TP:T], ident)
                tr(MX[0:TS, 1, 2 * P:3 * P], kT[:, P + TP:P + T], ident).then_inc(tv_ready, 1)
                pe.wait_ge(ck_in, val(0, 16, m, 16))
                for b in range(NB):
                    last = tr(MX[:, 2 + b // 4, P * (b % 4):P * (b % 4) + P], ckraw[:, b, :], ident)
                last.then_inc(ck_ready, 1)

            def sample_scores(m, half):
                if half == 0:
                    tv_all, ck_all = fixed(pe, val(0, 4, m, 4)), fixed(pe, val(0, 6, m, 6))
                    pe.wait_ge(pads, 2)
                    pe.wait_ge(tv_done, tv_all)
                    pe.wait_ge(ck_done, ck_all)
                hs = slice(64 * half, 64 * half + 64)
                for a in range(2):
                    ck, kk = (ckT, kT) if a == half else (ckS, kS)
                    lhsT = qS[hs, 64 * a:64 * a + 64]
                    out = slice(64 * a, 64 * a + 64)
                    for j in range(2):
                        mm(MX[out, j, :], lhsT, ck[hs, 512 * j:512 * j + 512], start=True, stop=True)
                    last = mm(MX[out, 2, 0:TS], lhsT, kk[hs, P + TP:P + T], start=True, stop=True)
                last.then_inc(ss_ready, 1)

            def sample_turn(m, half):
                pe.wait_ge(sp_ready, val(0, 2, m, half + 1))
                for b in range(NB):
                    tr(MX[:, b // 4, P * (b % 4):P * (b % 4) + P], SPs[:, P * b:P * b + P], ident)
                tr(MX[0:TS, 2, 0:P], SPs[:, 1024:1056], ident).then_inc(ts_ready, 1)

            def sample_pv(m, half):
                pe.wait_ge(pts_done, val(0, 4, m, 2 * half + 2))
                if half == 0:
                    pe.wait_ge(cv_in, val(0, 16, m, 16))
                out = slice(64 * half, 64 * half + 64)
                for a in range(2):
                    o = MX[out, 3, 64 * a:64 * a + 64]
                    for b in range(NB):
                        mm(o, cv[:, b, 64 * a:64 * a + 64], PTs[:, P * b + 64 * a:P * b + 64 * a + 64],
                           start=(b == 0), stop=False)
                    last = mm(o, vks[0:TS, 64 * a:64 * a + 64], PTn[:, 64 * a:64 * a + 64],
                              start=False, stop=True)
                last.then_inc(pvs_ready, 1)

            def step(x):
                return x // 4, x // 2 % 2, x % 2

            def scores(m, x):
                j, bp, half = step(x)
                hs = slice(64 * half, 64 * half + 64)
                kk = kT if j // 2 == half else kS
                if x >= 2:
                    pe.wait_ge(pmax_ready, val(0, 16, m, x - 1))
                for bl in range(2):
                    b = 2 * bp + bl
                    last = mm(MX[:, half, 256 * bl:256 * bl + 256], q0[hs, j, P * b:P * b + P],
                              kk[hs, P * b:P * b + 2 * P], start=True, stop=True)
                last.then_inc(sc_ready, 1)

            def p_turn(m, x):
                pe.wait_ge(pn_ready, val(0, 32, m, 2 * x + 2))
                for c in range(4):
                    last = tr(MX[:, 2, P * c:P * c + P], PP[x % 2][:, P * c:P * c + P], ident)
                last.then_inc(tr_ready, 1)

            def pv(m, x):
                j, bp, half = step(x)
                a = j // 2
                pe.wait_ge(pt_done, val(0, 16, m, x + 1))
                pe.wait_ge(om_done, val(1, 18, m, max(2, x + 1)))
                for bl in range(2):
                    b = 2 * bp + bl
                    o = MX[64 * half:64 * half + 64, 3, P * bl:P * bl + P]
                    for kb in range(2):
                        if b == 0 and kb == 0:
                            continue
                        last = mm(o, vtok[:, P * (b - 1 + kb) + 64 * a:P * (b - 1 + kb) + 64 * a + 64],
                                  PT[:, 256 * bl + P * kb:256 * bl + P * kb + P],
                                  start=(kb == 0 or b == 0), stop=(kb == 1))
                last.then_inc(pv_ready, 1)

            def attend(m, p):
                if p == 0:
                    kv_turn(m)
                if p in (2, 5):
                    if p == 5:
                        sample_pv(m, 0)
                    sample_scores(m, p // 3)
                if p in (4, 8):
                    sample_turn(m, p // 8)
                if p == 9:
                    sample_pv(m, 1)
                if 0 <= p - 13 < 15:
                    pv(m, p - 13)
                if 0 <= p - 10 < 16:
                    scores(m, p - 10)
                if 0 <= p - 12 < 16:
                    p_turn(m, p - 12)
                if p == 27:
                    pv(m, 15)

            POINTS = (4, 10, KT - 1)

            def layer0(it, prev, h_base=None):
                for e in range(len(L0K)):
                    points = {}
                    for i, k in enumerate(POINTS):
                        age, p = attend_points(e, i)
                        m = (it, prev)[age]
                        if m is not None:
                            points[k] = lambda m=m, p=p: attend(m, p)
                    entry("l0", it, e, points, h_base if e == 0 else None)

            layer0((None, 0), None, 0)
            with pe.Fori(0, GR - 1) as r:
                layer0((r, 1), (r, 0))
            for p in range(3 * L0K.count("Z"), 28):
                attend((None, GR - 1), p)

            def strip(n, j):
                at = fixed(pe, n + 1)
                pe.wait_ge(ct_ready, 1)
                pe.wait_ge(u_lo_done, at)
                for k in range(2):
                    lhsT = cT[:, (2 * j + k) * 18:(2 * j + k) * 18 + P]
                    for w in (u_hi, u_lo):
                        last = mm(MX[:, 2, :], lhsT, w[j % RING][:, k * 512:k * 512 + 512],
                                  start=(j == 0 and k == 0 and w is u_hi),
                                  stop=(j == STRIPS - 1 and k == 1 and w is u_lo))
                last.then_inc(u_used, 1)

            def turn_group(n):
                pe.wait_ge(ct_ready, 1)
                pe.wait_ge(mod_copied, n + 1)
                pe.wait_ge(bias_in, n * 16 + 16)
                pe.wait_ge(mod_taken, n - 7)
                for j in range(4):
                    last = mm(MX[:, 3, 9 * j:9 * j + 9], misc[32:51, P * j:P * j + P],
                              fix[32:51, C_SEL:C_SEL + NSEQ], start=True, stop=True)
                last.then_inc(mod_turned, 1)

            def out_product(ph, h_base, n, extra={}):
                def one(k, seg, r, i):
                    pe.wait_ge(freed["a"], r * 2 + (FREED0["a"][ph] + k - 1))
                    pe.wait_ge(lo_done, r * 2 + (UNIT0[ph] + k + 1))
                    points = extra if k == 0 else {}
                    if seg and seg[2]:
                        g = seg[2][2] + i
                        first = STRIPS * (g - 8)

                        def strips(js):
                            for j in js:
                                strip(r * (2 * STRIPS) + (first + j), j)
                        points = {at: (lambda j=j: strips([j])) for j, at in enumerate((4, 5, 6, 8, 9, 10, 12, 13))}
                        points[KT - 1] = lambda: turn_group(r * 2 + g)
                    block(slot_of(ph, k), pair_of(ph, k), points, h_base if k == 0 else None)

                pe.wait_ge(*freed_at(ph, it0, -2))
                pe.wait_ge(*freed_at(ph, it0, -1))
                for seg in SEGS[ph]:
                    for r, i, k in blocks_of(pe, ph, seg):
                        one(k, seg, r, i)
                for k in range(KT - 2, KT):
                    one(k, None, 0, 0)
                pe.wait_ge(sq_used, KT * n)
                for f in range(2):
                    last = mm(MX[:, f, 0:HT], ones, rB[:, HT * f:HT * f + HT], start=True, stop=True)
                last.then_inc(sums_ready, 1)

            out_product("out0", KT, 2)
            sums(2 * KT)

            entry("gate", it0, 0, {}, 2 * KT)

            def gate_turn():
                pe.wait_ge(gate_d, 1)
                for c in range(5):
                    n = P if c < 4 else TS
                    tr(MX[0:n, 0, 8 * c:8 * c + 8], Ub[:, P * c:P * c + n], ident[GP, 64:72])
                    tr(MX[0:n, 1, 8 * c:8 * c + 8], Wr[:, P * c:P * c + n], ident[GP, 64:72])
                pe.wait_ge(gl_in, 96)
                tr(MX[:, 2, 0:64], nrow, ident[0:64, 0:64]).then_inc(gate_ps, 1)

            def memory(m, p):
                if p == 0:
                    pe.wait_ge(gate_cols, 1)
                    pe.wait_ge(*freed_at("l1", m, L1K.rindex("V")))
                    pe.wait_ge(head_done, val(1, 1, m))
                    for bank, src in ((0, k1), (1, v1[:, 0, :]), (2, v1[:, 1, :])):
                        for c in range(4):
                            tr(MX[:, bank, P * c:P * c + P], src[:, P * c:P * c + P], ident)
                    for j, src in enumerate((k1, v1[:, 0, :], v1[:, 1, :])):
                        last = tr(MX[0:TS, 3, P * j:P * j + P], src[:, TP:T], ident)
                    last.then_inc(tr1_ready, 1)
                if p == 1:
                    pe.wait_ge(wk_done, val(0, 6, m, 6))
                    pe.wait_ge(vt_done, val(0, 3, m, 3))
                    pe.wait_ge(rb_done, val(0, 1, m, 1))
                    for c in range(4):
                        mm(MX[:, 0, P * c:P * c + P], k1[:, P * c:P * c + P], q1[:, P * c:P * c + P],
                           start=True, stop=True)
                    for j in range(3):
                        last = mm(MX[:, 1 + j, :], fix[BP, C_ONE:C_ONE + P], RB[:, j, 0:TP],
                                  start=True, stop=True)
                    last.then_inc(sc1_ready, 1)
                if p == 2:
                    pe.wait_ge(arg_done, val(0, 1, m, 1))
                    pe.wait_ge(ab_done, val(0, 1, m, 1))
                    pe.wait_ge(emt_done, val(0, 2, m, 1))
                    for c in range(4):
                        mm(MX[:, 1 + c // 2, DV * (c % 2):DV * (c % 2) + DV], wk[:, c, :], vt1[:, c, :],
                           start=True, stop=True)
                    for c in range(4):
                        mm(MX[:, 3, c:c + 1], wk[:, c, :], ones[:, 0:1], start=True, stop=True)
                    mm(MX[0:TS, 3, 64:64 + TS], k1[:, TP:T], q1[:, TP:T], start=True, stop=True)
                    mm(MX[:, 3, P:P + 3 * TS], fix[BP, C_ONE:C_ONE + P], RB[:, :, TP:T],
                       start=True, stop=True).then_inc(G_ready, 1)
                if p == 4:
                    pe.wait_ge(P_done, val(0, 1, m, 1))
                    pe.wait_ge(S_done, val(0, 1, m, 1))
                    for blk in range(2):
                        for c in range(4):
                            o = MX[:, blk, P * c:P * c + P]
                            mm(o, vt1[:, c, P * blk:P * blk + P], Dm[:, P * c:P * c + P],
                               start=True, stop=(c == 0))
                            if c:
                                mm(o, S[:, c - 1, P * blk:P * blk + P], qa[:, P * c:P * c + P],
                                   start=False, stop=True)
                    mm(MX[:, 2, :], ones, Dm[:, :], start=True, stop=False)
                    mm(MX[:, 2, P:TP], ones, qn[:, P:TP], start=False, stop=True).then_inc(num_ready, 1)
                if p == 5:
                    pe.wait_ge(Ps_done, val(0, 1, m, 1))
                    pe.wait_ge(cs_in, val(0, 16, m, 16))
                    for blk in range(2):
                        mm(MX[:, 3, TS * blk:TS * blk + TS], vs[:, P * blk:P * blk + P], Ds[0:TS, :],
                           start=True, stop=False)
                        for b in range(NB):
                            mm(MX[:, 3, TS * blk + ND * b:TS * blk + ND * b + ND],
                               cs[:, b, P * blk:P * blk + P], qa[:, TP + ND * b:TP + ND * b + ND],
                               start=False, stop=(b == NB - 1))
                    mm(MX[:, 3, 64:64 + TS], ones[0:TS, :], Ds[0:TS, :], start=True, stop=False)
                    mm(MX[:, 3, 64:64 + TS], ones, qn[:, TP:T], start=False, stop=True)\
                        .then_inc(nums_ready, 1)
                if p == 7:
                    pe.wait_ge(hout_done, val(0, 1, m, 1))
                    for b in range(NB):
                        last = mm(MX[:, b // 2, DV * (b % 2):DV * (b % 2) + DV], wks[:, b, :], vs,
                                  start=True, stop=True)
                    last.then_inc(cu_ready, 1)
                if p == 8:
                    pe.wait_ge(cnew_done, val(0, NB, m, NB))
                    pe.wait_ge(hsq_done, val(0, 2, m, 2))
                    mm(MX[:, 0, 0:NB], ks, wbh, start=True, stop=True)
                    for f in range(2):
                        for blk in range(2):
                            last = mm(MX[:, 1 + f, 0:HT], ones, hsq[:, blk, HT * f:HT * f + HT],
                                      start=(blk == 0), stop=(blk == 1))
                    last.then_inc(ss1_ready, 1)

            def layer1(it, prev):
                for e in range(len(L1K)):
                    points = {}
                    for i, k in enumerate((7, KT - 1)):
                        age, p = memory_points(e, i)
                        m = (it, prev)[age]
                        if m is not None:
                            points[k] = lambda m=m, p=p: memory(m, p)
                        elif e == 3 and i == 0:
                            points[k] = gate_turn
                    entry("l1", it, e, points)

            layer1((None, 0), None)
            with pe.Fori(0, MH - 1) as r:
                layer1((r, 1), (r, 0))
            memory((None, MH - 1), 8)

            def normaliser_turn():
                pe.wait_ge(head_done, 1 + MH)
                tr(MX[0:72, 0, 0:P], nout, ident).then_inc(nT_ps, 1)

            out_product("out1", 3 * KT, 4, {14: normaliser_turn})

            for n, (kg, t) in enumerate(PIECES):
                w = P if t < 4 else TS
                if t == 0:
                    pe.wait_ge(x_ready, KT + 4 * kg + 4)
                if n >= 4:
                    pe.wait_ge(fin_a, n - 3)
                for k in range(4):
                    last = tr(MX[0:w, n % 4, P * k:P * k + P], xw[:, 4 * kg + k, P * t:P * t + w], ident)
                last.then_inc(fin_ready, 1)

        @block.scalar
        def _(act):
            chain = Chain(act, ach)
            fn = act.activation
            it0 = (None, 0)

            act.dma_start(c_rows[0:1, :], c_prompt).then_inc(c_in, 16)
            act.dma_start(c_rows[1:NSEQ, :], c_sample).then_inc(c_in, 16)
            act.dma_start(fix[:, :], const[:, 0:C_FIX]).then_inc(const_in, 16)
            act.dma_start(gvec[0:32, :], g_pre.rearrange("l (k p) -> (l k) p", p=P)).then_inc(vec_in, 16)
            act.dma_start(gvec[32:64, :], g_post.rearrange("l (k p) -> (l k) p", p=P)).then_inc(vec_in, 16)
            act.dma_start(gvec[64:80, :], g_head_mlstm.rearrange("o h (k p) -> (o h k) p", p=P)).then_inc(vec_in, 16)
            act.wait_ge(warm_set, 1)
            act.wait_ge(c_in, 32)
            fn(c_tanh, c_rows, ACT.Tanh, scale=0.5).then_inc(ct_tanh, 1)
            act.wait_ge(ct_ps, 1)
            act.wait_ge(const_in, 16)
            fn(c_full, MX[:, 3, 0:KT * NSEQ], ACT.Copy).then_inc(ct_full, 1)

            def round_hi(ph, it, e, j=0):
                if ph == "ada0":
                    u = 8 * e + j
                    act.wait_ge(a0_in[u // 2 % 4], 16 * (u // 8 + 1))
                    if u >= 4:
                        act.wait_ge(w_used, u - 3)
                    fn(half_unit(w_hi, u), half_raw(u), ACT.Copy).then_inc(hi_done, 1)
                    return
                s = slot_of(ph, e, j)
                act.wait_ge(w_in[s], landed_at(ph, it, e, j))
                act.wait_ge(w_used, unit_no(ph, it, e, j - 1))
                if ph == "gate":
                    fn(w_hi[s][:, :].rearrange("p (k a n) -> p k a n", k=KT, n=32)[:, :, 0:2, 0:8],
                       raw[s][:, 0:KT * 16].rearrange("p (k a n) -> p k a n", k=KT, n=8),
                       ACT.Copy).then_inc(hi_done, 1)
                    return
                fn(w_hi[s][:, :], raw[s][:, :], ACT.Copy).then_inc(hi_done, 1)

            def mod_copy(ph, e, n, it):
                act.wait_ge(w_used, ended(ph, it, e))
                if ph != "ada0" or n:
                    act.wait_ge(mod_turned, n)
                fn(misc[32:50, 0:512], PJ[0:18, 2 * pair_of(ph, e), :], ACT.Copy).then_inc(mod_copied, 1)

            def squares(base, blocks=range(KT), x_from=None):
                for k in blocks:
                    if x_from is not None:
                        act.wait_ge(x_ready, x_from + k + 1)
                    if base + k >= 2:
                        act.wait_ge(sq_used, base + k - 1)
                    fn(sqb[:, k % 2, :], xw[:, k, :], ACT.Square).then_inc(sq_made, 1)

            def root(n):
                fn(warm[:, 0:1], warm[:, 0:1], ACT.Sqrt)
                act.wait_ge(ms_ready, n)
                fn(rB, rB, ACT.Sqrt).then_inc(rt_ready, 1)

            def modulate(l, n):
                act.wait_ge(hs_done, l + 1)
                fn(h_hi[:, :, TP:T], obuf[:, :, TP:T], ACT.Copy).then_inc(hs_hi, 1)
                act.wait_ge(A_ready, l + 1)
                with act.Fori(0, KT // 2) as r:
                    for i in range(2):
                        act.wait_ge(xs_done, r * 2 + (KT * l + i + 1))
                        fn(h_hi[:, ds(r * 2 + i, 1), 0:TP].rearrange("p o t -> p (o t)"),
                           obuf[:, ds(r * 2 + i, 1), 0:TP].rearrange("p o t -> p (o t)"), ACT.Identity,
                           bias=modT[:, ds(r * 2 + (48 * l + i), 1), 0:1].rearrange("p a b -> p (a b)"))\
                            .then_inc(hh_hi, 1)

            def split_out(blocks):
                for k in blocks:
                    fn(h_hi[:, k, :], obuf[:, k, :], ACT.Copy).then_inc(hh_hi, 1)

            for e in range(8):
                for j in range(8):
                    round_hi("ada0", it0, e, j)
                    if j == 3 and e:
                        mod_copy("ada0", e - 1, e - 1, it0)
                    if (e, j) == (5, 3):
                        act.wait_ge(xe_a, 10)
                        act.wait_ge(xe_d, 10)
                    if (e, j) in SQ_PARTS:
                        squares(0, SQ_PARTS[e, j])
                    if (e, j) == (7, 5):
                        root(1)
                if e < 5:
                    n = P if e < 4 else TS
                    act.wait_ge(xt_done, e + 1)
                    act.wait_ge(ct_ready, 1)
                    for b in range(2):
                        fn(xw[:, 4 * b:4 * b + 4, P * e:P * e + n],
                           MX[:, b, 0:4 * n].rearrange("p (k t) -> p k t", k=4), ACT.Copy).then_inc(xe_a, 1)
            mod_copy("ada0", 7, 7, it0)
            round_hi("l0", it0, 0)
            modulate(0, 0)
            act.wait_ge(spilled, 16)

            def attend(m, p):
                if p == 0:
                    act.wait_ge(tv_ready, val(0, 1, m, 1))
                    act.wait_ge(kv_stored, val(32, 64, m))
                    fn(vtok, MX[:, 0, :], ACT.Copy).then_inc(tv_done, 1)
                    fn(kout, MX[:, 1, 0:P], ACT.Copy).then_inc(tv_done, 1)
                    fn(vks[0:TS, 0:P], MX[0:TS, 1, P:2 * P], ACT.Copy).then_inc(tv_done, 1)
                    fn(vks[0:TS, P:2 * P], MX[0:TS, 1, 2 * P:3 * P], ACT.Copy).then_inc(tv_done, 1)
                if p in (2, 5):
                    half = p // 3
                    act.wait_ge(smax_ready, val(0, 2, m, half + 1))
                    fn(SPs, SPs, ACT.Exp, bias=st[:, 1:2], accum_out=st[:, 2:3]).then_inc(sexp_ready, 1)
                    fn(st[:, 4:5], st[:, 3:4], ACT.Exp).then_inc(sexp_ready, 1)
                if p in (4, 8):
                    half = p // 8
                    act.wait_ge(ts_ready, val(0, 2, m, half + 1))
                    fn(PTs, MX[:, 0:2, :].rearrange("p a t -> p (a t)"), ACT.Copy).then_inc(pts_done, 1)
                    fn(PTn, MX[0:TS, 2, 0:P], ACT.Copy).then_inc(pts_done, 1)
                if 0 <= p - 12 < 16:
                    x = p - 12
                    act.wait_ge(tr_ready, val(0, 16, m, x + 1))
                    fn(PT, MX[:, 2, :], ACT.Copy).then_inc(pt_done, 1)
                if 0 <= p - 10 < 16:
                    x = p - 10
                    o = 8 + 16 * (x % 2)
                    act.wait_ge(pmax_ready, val(0, 16, m, x + 1))
                    for bl in range(2):
                        pb = PP[x % 2][:, 256 * bl:256 * bl + 256]
                        fn(pb, pb, ACT.Exp, bias=st[:, o + 2 + bl:o + 3 + bl],
                           accum_out=st[:, o + 6 + bl:o + 7 + bl]).then_inc(pexp_ready, 1)
                    fn(st[:, o + 8:o + 10], st[:, o + 4:o + 6], ACT.Exp).then_inc(pexp_ready, 1)

            def empty0(it, m, e, nq, nz):
                kind, pair = L0K[e], pair_of("l0", e)
                act.wait_ge(w_used, ended("l0", it, e))
                r, c = it
                g = c if r is None else r + c
                if kind == "Z":
                    fn(obuf[:, ds(g * 4 + nz, 1), :].rearrange("p o (a t) -> p (o a) t", a=2), pj(pair),
                       ACT.Tanh, scale=0.5).then_inc(th_done, 1)
                if kind == "Q":
                    if m is not None:
                        act.wait_ge(sc_ready, val(0, 16, m, 4 * nq + 4))
                        act.wait_ge(ss_ready, val(0, 2, m, 2))
                    sc = float(HD) ** -0.5
                    chain(fn(q0[:, nq, 0:HT], PJ[:, 2 * pair, 0:HT], ACT.Copy, scale=sc))
                    chain(fn(q0[:, nq, HT:TP], PJ[:, 2 * pair + 1, 0:TP - HT], ACT.Copy, scale=sc))
                    fn(qS[:, TS * nq:TS * nq + TS], PJ[:, 2 * pair + 1, TP - HT:HT], ACT.Copy,
                       scale=sc).then_inc(freed["a"], 1)
                if kind == "K":
                    if m is not None:
                        act.wait_ge(sc_ready, val(0, 16, m, 16))
                    chain(fn(two(kT[:, P:]), pj(pair), ACT.Copy))
                    chain(fn(two(kS[0:64, P:]), pj(pair, slice(64, 128)), ACT.Copy))
                    fn(two(kS[64:128, P:]), pj(pair, slice(0, 64)), ACT.Copy).then_inc(freed["a"], 1)
                if kind == "V":
                    fn(two(vT), pj(pair), ACT.Copy).then_inc(freed["a"], 1)

            def point(it, prev, e, i):
                age, p = attend_points(e, i)
                if (it, prev)[age] is not None:
                    attend((it, prev)[age], p)

            def layer0(it, m):
                nq = nz = 0
                for e in range(len(L0K) + 1):
                    if e:
                        empty0(it, m, e - 1, nq, nz)
                        nq += L0K[e - 1] == "Q"
                        nz += L0K[e - 1] == "Z"
                        point(it, m, e - 1, 2)
                    if e < len(L0K):
                        round_hi("l0", it, e + 1)
                        point(it, m, e, 0)
                        point(it, m, e, 1)

            layer0((None, 0), None)
            LOOP_A = 4 * 2 + 2
            with act.Fori(0, GR - 1) as r:
                chain.enter(r, LOOP_A)
                layer0((r, 1), (r, 0))
            chain.leave(GR - 1)
            act.wait_ge(om_done, 1 + 18 * (GR - 1))
            for p in range(3 * L0K.count("Z"), 28):
                attend((None, GR - 1), p)
                split_out(range(p - 12, p - 11) if p < 24 else [])
            act.wait_ge(om_done, 1 + 18 * GR)
            split_out(range(12, KT))

            def out_product(ph, clear=()):
                def empty(k, used, blk):
                    pair = pair_of(ph, k)
                    base = KT if ph == "out0" else 3 * KT
                    act.wait_ge(w_used, used)
                    act.wait_ge(sq_used, used - (UNIT0[ph] + 2) + base)
                    fn(two(sqb[:, k % 2, :]), pj(pair), ACT.Square).then_inc(sq_made, 1)
                    fn(obuf[:, ds(blk, 1), :].rearrange("p o (a t) -> p (o a) t", a=2), pj(pair),
                       ACT.Copy).then_inc(freed["a"], 1)

                def ahead(k, r):
                    s = slot_of(ph, k + 1)
                    act.wait_ge(w_in[s], r * 16 + landed_at(ph, it0, k + 1))
                    act.wait_ge(w_used, r * 2 + (UNIT0[ph] + k))
                    fn(w_hi[s][:, :], raw[s][:, :], ACT.Copy).then_inc(hi_done, 1)

                for seg in SEGS[ph]:
                    for r, i, k in blocks_of(act, ph, seg):
                        if not seg[2]:
                            ahead(k, r)
                            for se, v in clear if k == 0 else ():
                                act.wait_ge(se, v)
                        else:
                            g = seg[2][2] + i
                            for j in range(STRIPS):
                                if j == RING:
                                    ahead(k, r)
                                landed = 16 * (2 * (g - 8) + j // RING + 1)
                                act.wait_ge(u_in[j % RING], r * 64 + landed)
                                fn(u_hi[j % RING], u_raw[j % RING], ACT.Copy).then_inc(u_hi_done, 1)
                            act.wait_ge(u_used, r * (2 * STRIPS) + (RING + STRIPS * (g - 7)))
                            act.wait_ge(mod_turned, r * 2 + g)
                            fn(misc[32:50, 0:512], MX[0:18, 2, :], ACT.Copy).then_inc(mod_copied, 1)
                        empty(k, r * 2 + (UNIT0[ph] + k + 1), r * 2 + k)
                ahead(KT - 2, 0)
                empty(KT - 2, UNIT0[ph] + KT - 1, KT - 2)
                if ph == "out0":
                    round_hi("gate", it0, 0)
                empty(KT - 1, UNIT0[ph] + KT, KT - 1)

            out_product("out0")
            root(2)
            squares(2 * KT, x_from=0)
            root(3)
            modulate(1, 1)

            round_hi("l1", it0, 0)
            act.wait_ge(w_used, ended("gate", it0, 0))
            act.wait_ge(spilled, 32)
            act.wait_ge(h_ready, 3 * KT)
            fn(two(LI), pj(pair_of("gate", 0), slice(0, 8)), ACT.Copy).then_inc(gate_a, 1)
            fn(two(LF), pj(pair_of("gate", 0), slice(32, 40)), ACT.Copy).then_inc(freed["a"], 1)

            def gates():
                act.wait_ge(gate_v, 1)
                chain(fn(Bc, Bc, ACT.Exp, scale=-1.0))
                fn(Bc, Bc, ACT.Ln, bias=1.0).then_inc(gate_a, 1)

            def gate_exps():
                act.wait_ge(gate_v, 2)
                fn(R[:, 1, :], R[:, 1, :], ACT.Exp).then_inc(gate_a, 1)
                fn(Wr, Wr, ACT.Exp).then_inc(gate_a, 1)

            def memory(m, p):
                r, c = m
                h = c if r is None else r + c
                if p == 0:
                    act.wait_ge(tr1_ready, val(0, 1, m, 1))
                    for j in range(2):
                        fn(vt1[:, :, P * j:P * j + P], MX[:, 1 + j, :].rearrange("p (c e) -> p c e", c=4),
                           ACT.Copy).then_inc(vt_done, 1)
                    fn(ksv, MX[0:TS, 3, 0:3 * P], ACT.Copy).then_inc(vt_done, 1)
                if p == 1:
                    act.wait_ge(sc1_ready, val(0, 1, m, 1))
                    fn(aB, MX[:, 2, :], ACT.Copy).then_inc(ab_done, 1)
                    fn(emt[:, 0:TP], MX[:, 3, :], ACT.Exp, scale=-1.0).then_inc(emt_done, 1)
                    act.wait_ge(arg_done, val(0, 1, m, 1))
                    for ch in range(4):
                        dc = Dm[:, P * ch:P * ch + P]
                        fn(dc, dc, ACT.Exp, bias=Uc[:, ds(h + 8 * ch, 1)]).then_inc(Dexp_done, 1)
                if p == 2:
                    act.wait_ge(G_ready, val(0, 1, m, 1))
                    fn(sB, MX[:, 3, P:P + 3 * TS].rearrange("p (j t) -> p j t", j=3), ACT.Copy).then_inc(sb_done, 1)
                    act.wait_ge(dsarg_done, val(0, 1, m, 1))
                    fn(Ds[0:TS, :], Ds[0:TS, :], ACT.Exp, bias=Uc[0:TS, ds(h + 32, 1)]).then_inc(dsexp_done, 1)
                    fn(emt[:, TP:T], sB[:, 2, :], ACT.Exp, scale=-1.0).then_inc(emt_done, 1)
                if p == 4:
                    act.wait_ge(num_ready, val(0, 1, m, 1))
                    fn(Dm, MX[:, 2, :], ACT.Abs).then_inc(abs_done, 1)
                if p == 5:
                    act.wait_ge(nums_ready, val(0, 1, m, 1))
                    fn(qn[:, TP:T], MX[:, 3, 64:64 + TS], ACT.Abs).then_inc(abss_done, 1)
                    act.wait_ge(hout_done, val(0, 1, m, 1))
                    for blk in range(2):
                        fn(hsq[:, blk, :], hh[:, blk, :], ACT.Square).then_inc(hsq_done, 1)
                if p == 8:
                    act.wait_ge(ms1_done, val(0, 1, m, 1))
                    fn(qa, qa, ACT.Sqrt).then_inc(rt1_done, 1)

            def empty1(it, m, e, seen):
                kind, pair = L1K[e], pair_of("l1", e)
                act.wait_ge(w_used, ended("l1", it, e))
                r, c = it
                h = c if r is None else r + c
                if kind == "Z":
                    fn(obuf[:, ds(h * 2 + seen, 1), :].rearrange("p o (a t) -> p (o a) t", a=2), pj(pair),
                       ACT.Tanh, scale=0.5).then_inc(th_done, 1)
                if kind == "O":
                    fn(two(misc[:, :]), pj(pair), ACT.Tanh, scale=0.5).then_inc(th_done, 1)
                if kind in "QKV":
                    if m is not None:
                        if kind == "V":
                            act.wait_ge(ss1_ready, val(0, 1, m, 1))
                        else:
                            act.wait_ge(hout_done, val(0, 1, m, 1))
                    dst = {"Q": q1, "K": k1, "V": v1[:, seen, :]}[kind]
                    fn(two(dst), pj(pair), ACT.Copy,
                       scale=float(DK) ** -0.5 if kind == "Q" else 1.0).then_inc(freed["a"], 1)

            def layer1(it, prev):
                seen = dict.fromkeys("ZOQKV", 0)
                for e in range(len(L1K) + 1):
                    if e:
                        empty1(it, prev, e - 1, seen[L1K[e - 1]])
                        seen[L1K[e - 1]] += 1
                    if e < len(L1K):
                        round_hi("l1", it, e + 1)
                    if prev is None and e == 1:
                        gates()
                    if prev is None and e == 2:
                        gate_exps()
                    for at, i in ((e - 1, 1), (e, 0)):
                        if 0 <= at < len(L1K):
                            age, p = memory_points(at, i)
                            if (it, prev)[age] is not None:
                                memory((it, prev)[age], p)

            layer1((None, 0), None)
            with act.Fori(0, MH - 1) as r:
                layer1((r, 1), (r, 0))
            act.wait_ge(head_done, MH)
            split_out(range(10))
            memory((None, MH - 1), 8)
            split_out(range(10, 14))
            act.wait_ge(head_done, 1 + MH)
            split_out(range(14, KT))
            out_product("out1", [(cs_out, 16 * MH)])
            root(4)
            for n, (kg, t) in enumerate(PIECES):
                w = P if t < 4 else TS
                act.wait_ge(fin_ready, n + 1)
                if n >= 8:
                    act.wait_ge(y_out[n // 4 % 2], 16 * 4 * (n // 8))
                fn(raw[n // 4 % 2][0:w, 512 * (n % 4):512 * (n % 4) + 512], MX[0:w, n % 4, :], ACT.Copy)\
                    .then_inc(fin_a, 1)

        @block.vector
        def _(dve):
            chain = Chain(dve, dch)
            tt, ts, stt, cp = dve.tensor_tensor, dve.tensor_scalar, dve.scalar_tensor_tensor, dve.tensor_copy
            it0 = (None, 0)

            chain(dve.memset(cT[:, :].bitcast(mybir.dt.uint32), 0))
            dve.memset(st[:, :], 0.0).then_inc(om_done, 1)
            dve.drain().then_inc(head_done, 1)
            dve.memset(warm[:, :], 1.0).then_inc(warm_set, 1)
            dve.drain().then_inc(mod_taken, 1)
            dve.wait_ge(ct_tanh, 1)
            chain(stt(c_rows, c_tanh, 1.0, c_rows, ALU.add, ALU.mult))
            ts(c_rows, c_rows, 0.5, None, ALU.mult).then_inc(ct_rows, 1)
            dve.wait_ge(ct_full, 1)
            cv3 = c_full.rearrange("p (k s) -> p k s", k=KT)
            cT3 = cT[:, 0:KT * 18].rearrange("p (k s) -> p k s", k=KT)
            chain(cp(cT3[:, :, 0:NSEQ], cv3))
            tt(cT3[:, :, NSEQ:18], cv3, cT3[:, :, 0:NSEQ].bitcast(F32), ALU.subtract).then_inc(ct_ready, 1)
            dve.wait_ge(vec_ps, 1)
            cp(gT[:, :], MX[:, 2, 0:80]).then_inc(g_ready, 1)
            dve.wait_ge(g_ready, 1)
            chain(ts(gT[:, 64:80], gT[:, 64:80], 0.25, None, ALU.mult))

            def split_lo(ph, it, e, j=0):
                s = slot_of(ph, e, j)
                dve.wait_ge(hi_done, unit_no(ph, it, e, j) + 1)
                if ph == "ada0":
                    u = 8 * e + j
                    tt(half_unit(w_lo, u), half_raw(u), half_unit(w_hi, u).bitcast(F32), ALU.subtract)\
                        .then_inc(lo_done, 1)
                elif ph == "gate":
                    view = "p (k a n) -> p k a n"
                    tt(w_lo[s][:, :].rearrange(view, k=KT, n=32)[:, :, 0:2, 0:8],
                       raw[s][:, 0:KT * 16].rearrange(view, k=KT, n=8),
                       w_hi[s][:, :].bitcast(F32).rearrange(view, k=KT, n=32)[:, :, 0:2, 0:8],
                       ALU.subtract).then_inc(lo_done, 1)
                else:
                    tt(w_lo[s][:, :], raw[s][:, :], w_hi[s][:, :].bitcast(F32), ALU.subtract)\
                        .then_inc(lo_done, 1)

            def mod_empty(ph, e, n):
                dve.wait_ge(mod_turned, n + 1)
                cp(modT[:, ds(n * 4, 4), :], PJ[:, 2 * pair_of(ph, e) + 1, 0:36].rearrange("p (k s) -> p k s", k=4))\
                    .then_inc(freed["d"], 1)

            def mean_square(n):
                if n % 2:
                    dve.wait_ge(sq_used, KT * n)
                else:
                    dve.wait_ge(sums_ready, n // 2)
                ts(two(rB), MX[:, 0:2, 0:HT], 1.0 / D, EPS, ALU.mult, ALU.add).then_inc(ms_ready, 1)

            def inverse(n):
                dve.wait_ge(rt_ready, n)
                chain(dve.reciprocal(rB, rB))

            def gain(l):
                A = modT[:, 48 * l + 16:48 * l + 32, :]
                gp = gT[:, KT * l:KT * l + KT].unsqueeze(2).broadcast_to([P, KT, NSEQ])
                stt(A, A, 1.0, gp, ALU.add, ALU.mult).then_inc(A_ready, 1)
                dve.wait_ge(A_ready, l + 1)

            def gate_gain(l):
                G = modT[:, 48 * l + 32:48 * l + 48, :]
                gp = gT[:, 32 + KT * l:32 + KT * l + KT].unsqueeze(2).broadcast_to([P, KT, NSEQ])
                chain(tt(G, G, gp, ALU.mult))

            def norm_split(l, n):
                A = modT[:, 48 * l + 16:48 * l + 32, :]
                xs = obuf[:, :, TP:T]
                x4 = xs.rearrange("p k (b t) -> p k b t", t=ND)
                if n > 1:
                    mean_square(n)
                chain(tt(x4, xw[:, :, TP:T].rearrange("p k (b t) -> p k b t", t=ND), per_seq(A[:, :, 1:NSEQ]), ALU.mult))
                if n > 1:
                    inverse(n)
                chain(tt(xs, xs, rB[:, TP:T].unsqueeze(1).broadcast_to([P, KT, TS]), ALU.mult))
                tt(x4, x4, per_seq(modT[:, 48 * l:48 * l + 16, 1:NSEQ]), ALU.add).then_inc(hs_done, 1)
                row = "p o t -> p (o t)"

                def scale(k):
                    stt(obuf[:, ds(k, 1), 0:TP].rearrange(row), xw[:, ds(k, 1), 0:TP].rearrange(row),
                        A[:, ds(k, 1), 0:1].rearrange("p a b -> p (a b)"), rB[:, 0:TP], ALU.mult, ALU.mult)\
                        .then_inc(xs_done, 1)

                def low(k):
                    dve.wait_ge(hh_hi, k + (2 * KT * l + 1))
                    stt(h_lo[:, ds(k, 1), 0:TP].rearrange(row), obuf[:, ds(k, 1), 0:TP].rearrange(row),
                        modT[:, ds(k + 48 * l, 1), 0:1].rearrange("p a b -> p (a b)"),
                        h_hi[:, ds(k, 1), 0:TP].rearrange(row).bitcast(F32), ALU.add, ALU.subtract)\
                        .then_inc(h_ready, 1)

                scale(0)
                scale(1)
                dve.wait_ge(hs_hi, l + 1)
                tt(h_lo[:, :, TP:T], xs, h_hi[:, :, TP:T].bitcast(F32), ALU.subtract).then_inc(hs_ready, 1)
                with dve.Fori(0, KT // 2 - 1) as r:
                    for i in range(2):
                        scale(r * 2 + (2 + i))
                        low(r * 2 + i)
                low(KT - 2)
                low(KT - 1)

            def split_out(n, blocks):
                for k in blocks:
                    dve.wait_ge(hh_hi, k + (n * KT + 1))
                    tt(h_lo[:, k, :], obuf[:, k, :], h_hi[:, k, :].bitcast(F32), ALU.subtract).then_inc(h_ready, 1)

            for e in range(8):
                for j in range(8):
                    split_lo("ada0", it0, e, j)
                    if j == 5 and e:
                        mod_empty("ada0", e - 1, e - 1)
                    if (e, j) == (7, 3):
                        mean_square(1)
                    if (e, j) == (7, 7):
                        inverse(1)
                if e < 5:
                    n = P if e < 4 else TS
                    dve.wait_ge(xt_done, e + 1)
                    for b in range(2, 4):
                        cp(xw[:, 4 * b:4 * b + 4, P * e:P * e + n],
                           MX[:, b, 0:4 * n].rearrange("p (k t) -> p k t", k=4)).then_inc(xe_d, 1)
            mod_empty("ada0", 7, 7)
            split_lo("l0", it0, 0)
            dve.wait_ge(sink_in, 16 * 9)
            chain(ts(nsink[:, :], nsink[:, :], -1.0, None, ALU.mult))
            gain(0)
            norm_split(0, 1)
            dve.wait_ge(spilled, 16)
            dve.wait_ge(h_ready, KT)
            dve.memset(kT[:, 0:P], 0.0).then_inc(pads, 1)
            dve.memset(kS[:, 0:P], 0.0).then_inc(pads, 1)

            def soft_sample(m, half):
                r, c = m
                g = c if r is None else r + c
                dve.wait_ge(mask_in, 32)
                dve.wait_ge(ss_ready, val(0, 2, m, half + 1))
                slope = fix[:, ds(g * 2 + (C_SLS + half), 1)]
                nsk = nsink[:, ds(g + (QH + 4 * half), 1)]
                chain(stt(SPs[:, 0:1024], negs[:, 0:1024], slope, MX[:, 0:2, :].rearrange("p a t -> p (a t)"),
                          ALU.mult, ALU.add))
                chain(stt(SPs[:, 1024:1056], negs[:, 1024:1056], slope, MX[:, 2, 0:TS], ALU.mult, ALU.add))
                chain(dve.tensor_reduce(st[:, 0:1], SPs, AX, ALU.max, negate=True))
                chain(tt(st[:, 1:2], st[:, 0:1], nsk, ALU.min))
                tt(st[:, 3:4], st[:, 1:2], nsk, ALU.subtract).then_inc(smax_ready, 1)

            def norm_sample(m, half):
                dve.wait_ge(sexp_ready, val(0, 4, m, 2 * half + 2))
                chain(tt(st[:, 5:6], st[:, 2:3], st[:, 4:5], ALU.add))
                chain(dve.reciprocal(st[:, 6:7], st[:, 5:6]))
                ts(SPs, SPs, st[:, 6:7], 0.5, ALU.mult, ALU.mult).then_inc(sp_ready, 1)

            def gate_sample(m, half):
                r, c = m
                g = c if r is None else r + c
                dve.wait_ge(pvs_ready, val(0, 2, m, half + 1))
                hs = slice(64 * half, 64 * half + 64)
                ob = obuf[hs, ds(g * 4, 4), TP:T]
                tt(ob, ob, MX[hs, 3, 0:P].rearrange("p (k t) -> p k t", k=4), ALU.mult).then_inc(om_done, 1)

            def soft(m, x):
                r, c = m
                g = c if r is None else r + c
                j, bp, half = x // 4, x // 2 % 2, x % 2
                pb, o = PP[x % 2], 8 + 16 * (x % 2)
                dve.wait_ge(sc_ready, val(0, 16, m, x + 1))
                if x >= 2:
                    dve.wait_ge(tr_ready, val(0, 16, m, x - 1))
                head = g * 8 + (2 * j + half)
                nsk = nsink[:, ds(head, 1)].broadcast_to([P, 2])
                chain(stt(pb, negd[:, 256 * bp:256 * bp + 512], fix[:, ds(head + C_SLP, 1)], MX[:, half, :],
                          ALU.mult, ALU.add))
                chain(dve.tensor_reduce(st[:, o:o + 2], pb.rearrange("p (b k) -> p b k", b=2), AX, ALU.max,
                                        negate=True))
                chain(tt(st[:, o + 2:o + 4], st[:, o:o + 2], nsk, ALU.min))
                tt(st[:, o + 4:o + 6], st[:, o + 2:o + 4], nsk, ALU.subtract).then_inc(pmax_ready, 1)

            def norm(m, x):
                pb, o = PP[x % 2], 8 + 16 * (x % 2)
                dve.wait_ge(pexp_ready, val(0, 48, m, 3 * x + 3))
                chain(tt(st[:, o + 10:o + 12], st[:, o + 6:o + 8], st[:, o + 8:o + 10], ALU.add))
                chain(dve.reciprocal(st[:, o + 12:o + 14], st[:, o + 10:o + 12]))
                for bl in range(2):
                    q = pb[:, 256 * bl:256 * bl + 256]
                    ts(q, q, st[:, o + 12 + bl:o + 13 + bl], 0.5, ALU.mult, ALU.mult).then_inc(pn_ready, 1)

            def gate_prompt(m, x):
                r, c = m
                g = c if r is None else r + c
                j, bp, half = x // 4, x // 2 % 2, x % 2
                dve.wait_ge(pv_ready, val(0, 16, m, x + 1))
                hs = slice(64 * half, 64 * half + 64)
                ob = obuf[hs, ds(g * 4 + j, 1), 256 * bp:256 * bp + 256].rearrange("p o t -> p (o t)")
                tt(ob, ob, MX[hs, 3, 0:256], ALU.mult).then_inc(om_done, 1)

            def attend(m, p):
                if p == 0:
                    dve.wait_ge(ck_ready, val(0, 1, m, 1))
                    for j in range(2):
                        cols = slice(512 * j, 512 * j + 512)
                        cp(ckT[:, cols], MX[:, 2 + j, :]).then_inc(ck_done, 1)
                        cp(ckS[0:64, cols], MX[64:128, 2 + j, :]).then_inc(ck_done, 1)
                        cp(ckS[64:128, cols], MX[0:64, 2 + j, :]).then_inc(ck_done, 1)
                if p in (2, 5):
                    soft_sample(m, p // 3)
                    norm_sample(m, p // 3)
                if p == 12:
                    gate_sample(m, 0)
                    gate_sample(m, 1)
                if 10 <= p < 26:
                    soft(m, p - 10)
                if 11 <= p < 27:
                    norm(m, p - 11)
                if 13 <= p < 27:
                    gate_prompt(m, p - 13)
                if p == 27:
                    gate_prompt(m, 14)
                    gate_prompt(m, 15)

            def empty_z(ph, it, e, blk, nth):
                dve.wait_ge(th_done, nth)
                ob = obuf[:, ds(blk, 1), :].rearrange("p o (a t) -> p (o a) t", a=2)
                stt(ob, ob, 1.0, pj(pair_of(ph, e)), ALU.add, ALU.mult).then_inc(freed["d"], 1)

            def point(it, prev, e, i):
                age, p = attend_points(e, i)
                if (it, prev)[age] is not None:
                    attend((it, prev)[age], p)

            def layer0(it, m):
                r, c = it
                g = c if r is None else r + c
                nz = 0
                for e in range(len(L0K) + 1):
                    if e:
                        if L0K[e - 1] == "Z":
                            empty_z("l0", it, e - 1, g * 4 + nz, val(0, 4, it, nz + 1))
                            nz += 1
                        point(it, m, e - 1, 2)
                    if e < len(L0K):
                        split_lo("l0", it, e + 1)
                        point(it, m, e, 0)
                        point(it, m, e, 1)

            LOOP_D = 2 * (4 + 2) + 16 * (3 + 2)
            layer0((None, 0), None)
            with dve.Fori(0, GR - 1) as r:
                chain.enter(r, LOOP_D)
                layer0((r, 1), (r, 0))
            chain.leave(GR - 1)
            for p in range(3 * L0K.count("Z"), 28):
                attend((None, GR - 1), p)
                split_out(1, range(p - 12, p - 11) if p < 24 else [])
            dve.wait_ge(om_done, 1 + 18 * GR)
            dve.memset(st[:, 0:1], 0.0).then_inc(u_used, RING)
            split_out(1, range(12, KT))

            def out_product(ph, clear=()):
                base = KT if ph == "out0" else 3 * KT

                def ahead(k, r):
                    s = slot_of(ph, k + 1)
                    dve.wait_ge(hi_done, r * 2 + (UNIT0[ph] + k + 2))
                    tt(w_lo[s][:, :], raw[s][:, :], w_hi[s][:, :].bitcast(F32), ALU.subtract).then_inc(lo_done, 1)

                def add(k, r):
                    dve.wait_ge(acc_done, 1 if ph == "out0" else 2)
                    dve.wait_ge(sq_made, r * 2 + (base + k + 1))
                    dve.wait_ge(sq_used, r * 2 + (base + k))
                    tt(rB, rB, sqb[:, k % 2, :], ALU.add).then_inc(sq_used, 1)

                for seg in SEGS[ph]:
                    for r, i, k in blocks_of(dve, ph, seg):
                        if not seg[2]:
                            ahead(k, r)
                            if k == 0:
                                for se, v in clear:
                                    dve.wait_ge(se, v)
                                dve.memset(rB, 0.0).then_inc(acc_done, 1)
                        else:
                            g = seg[2][2] + i
                            for j in range(STRIPS):
                                if j == RING:
                                    ahead(k, r)
                                dve.wait_ge(u_hi_done, r * (2 * STRIPS) + (STRIPS * (g - 8) + j + 1))
                                tt(u_lo[j % RING], u_raw[j % RING], u_hi[j % RING].bitcast(F32), ALU.subtract)\
                                    .then_inc(u_lo_done, 1)
                            dve.wait_ge(mod_turned, r * 2 + (g + 1))
                            cp(modT[:, ds(r * 8 + 4 * g, 4), :], MX[:, 3, 0:36].rearrange("p (k s) -> p k s", k=4))\
                                .then_inc(mod_taken, 1)
                        add(k, r)
                ahead(KT - 2, 0)
                add(KT - 2, 0)
                if ph == "out0":
                    split_lo("gate", it0, 0)
                    gain(1)
                gate_gain(0 if ph == "out0" else 1)
                add(KT - 1, 0)

            def residual(l, n):
                G = modT[:, 48 * l + 32:48 * l + 48, :]
                mean_square(n)
                dve.wait_ge(freed["a"], FREED0["a"]["out0" if l == 0 else "out1"] + KT)
                dve.wait_ge(reloaded, 16 * (l + 1))
                ys, xs = obuf[:, :, TP:T], xw[:, :, TP:T]
                y4 = ys.rearrange("p k (b t) -> p k b t", t=ND)
                chain(tt(y4, y4, per_seq(G[:, :, 1:NSEQ]), ALU.mult))
                inverse(n)
                chain(tt(ys, ys, rB[:, TP:T].unsqueeze(1).broadcast_to([P, KT, TS]), ALU.mult))
                chain(tt(xs, xs, ys, ALU.add))

                def scaled(k):
                    yk = obuf[:, ds(k, 1), 0:TP].rearrange("p o t -> p (o t)")
                    stt(yk, yk, G[:, ds(k, 1), 0:1].rearrange("p a b -> p (a b)"), rB[:, 0:TP], ALU.mult, ALU.mult)\
                        .then_inc(y_scaled, 1)

                def added(k):
                    dve.wait_ge(y_scaled, k + (KT * l + 1))
                    xk = xw[:, ds(k, 1), 0:TP].rearrange("p o t -> p (o t)")
                    tt(xk, xk, obuf[:, ds(k, 1), 0:TP].rearrange("p o t -> p (o t)"), ALU.add).then_inc(x_ready, 1)

                scaled(0)
                scaled(1)
                with dve.Fori(0, KT // 2 - 1) as r:
                    for i in range(2):
                        scaled(r * 2 + (2 + i))
                        added(r * 2 + i)
                added(KT - 2)
                added(KT - 1)

            out_product("out0")
            residual(0, 2)
            dve.wait_ge(x_ready, KT)
            norm_split(1, 3)

            split_lo("l1", it0, 0)

            def gates():
                dve.wait_ge(gate_a, 1)
                dve.wait_ge(freed["a"], FREED0["a"]["gate"] + 1)
                dve.wait_ge(gl_in, 96)
                chain(ts(LI, LI, bif[:, 0:1], None, ALU.add))
                chain(ts(LF, LF, bif[:, 1:2], None, ALU.add))
                chain(ts(Bc, LF, -1.0, None, ALU.mult))
                tt(Bc, Bc, LF, ALU.max).then_inc(gate_v, 1)
                dve.wait_ge(gate_a, 2)
                chain(ts(LF, LF, 0.0, None, ALU.min))
                chain(tt(LF, LF, Bc, ALU.subtract))
                orow = fix[GP, C_ONE:C_ONE + P]
                for ch in range(4):
                    cc = slice(P * ch, P * ch + P)
                    chain(dve.tensor_tensor_scan(Bc[:, cc], orow, LF[:, cc], 0.0, ALU.mult, ALU.add))
                B4 = Bc[:, TP:T].rearrange("p (b t) -> p b t", t=ND)
                F4 = LF[:, TP:T].rearrange("p (b t) -> p b t", t=ND)
                chain(cp(B4[:, :, 0], F4[:, :, 0]))
                for t in range(1, ND):
                    chain(tt(B4[:, :, t], B4[:, :, t - 1], F4[:, :, t], ALU.add))
                chain(tt(Ub, LI, Bc, ALU.subtract))

            def gate_maxima():
                orow = fix[GP, C_ONE:C_ONE + P]
                U4 = Ub[:, TP:T].rearrange("p (b t) -> p b t", t=ND)
                chain(dve.memset(tg[:, 0:1], 0.0))
                for ch in range(4):
                    cc = slice(P * ch, P * ch + P)
                    chain(dve.tensor_tensor_scan(Mr[:, cc], orow, Ub[:, cc], tg[:, ch:ch + 1], ALU.mult, ALU.max))
                    end = P * ch + P - 1
                    chain(tt(tg[:, ch + 1:ch + 2], Bc[:, end:end + 1], Mr[:, end:end + 1], ALU.add))
                    chain(ts(R[:, 1, cc], Mr[:, cc], tg[:, ch:ch + 1], -1.0, ALU.subtract, ALU.mult))
                    chain(ts(Wr[:, cc], Ub[:, cc], Mr[:, end:end + 1], None, ALU.subtract))
                M4 = Mr[:, TP:T].rearrange("p (b t) -> p b t", t=ND)
                U4 = Ub[:, TP:T].rearrange("p (b t) -> p b t", t=ND)
                chain(tt(M4[:, :, 0], m0s, U4[:, :, 0], ALU.max))
                for t in range(1, ND):
                    chain(tt(M4[:, :, t], M4[:, :, t - 1], U4[:, :, t], ALU.max))
                chain(tt(R[:, 1, TP:T].rearrange("p (b t) -> p b t", t=ND), m0s.unsqueeze(2).broadcast_to([MH, NB, ND]),
                         M4, ALU.subtract))
                chain(tt(Wr[:, TP:T].rearrange("p (b t) -> p b t", t=ND), U4,
                         M4[:, :, 3:4].broadcast_to([MH, NB, ND]), ALU.subtract))
                chain(ts(R[:, 0, :], Mr, -1.0, None, ALU.mult))
                tt(R[:, 2, :], Bc, Mr, ALU.add).then_inc(gate_v, 1)
                dve.wait_ge(gate_v, 2)
                dve.wait_ge(gate_a, 4)
                dve.drain().then_inc(gate_d, 1)
                dve.drain().then_inc(gate_done, 1)

            def gate_columns():
                dve.wait_ge(gate_ps, 1)
                for src, dst in ((0, Uc), (1, wc)):
                    chain(cp(dst[:, 0:32], MX[:, src, 0:32]))
                    chain(cp(dst[0:TS, 32:40], MX[0:TS, src, 32:40]))
                chain(cp(nsT.rearrange("p b h -> p (b h)"), MX[:, 2, 0:64]))
                chain(tt(wb[0:TS], wc[0:TS, 32:40].unsqueeze(2).broadcast_to([TS, MH, NB]),
                         bm[0:TS, :].unsqueeze(1).broadcast_to([TS, MH, NB]), ALU.mult))
                dve.drain().then_inc(gate_cols, 1)

            def memory(m, p):
                r, c = m
                h = c if r is None else r + c
                if p == 0:
                    ts(rows[BP, :], rows[GP, :], fix[GP, ds(h + (C_ID + 64), 1)], None, ALU.mult).then_inc(rb_done, 1)
                    dve.wait_ge(tr1_ready, val(0, 1, m, 1))
                    for ch in range(4):
                        ts(wk[:, ch, :], MX[:, 0, P * ch:P * ch + P], wc[:, ds(h + 8 * ch, 1)], None, ALU.mult)\
                            .then_inc(wk_done, 1)
                    dve.wait_ge(vt_done, val(0, 3, m, 3))
                    tt(wks, MX[0:TS, 3, 0:P].unsqueeze(1).broadcast_to([TS, NB, P]),
                       wb[0:TS, ds(h, 1), :].rearrange("p o b -> p (o b)").unsqueeze(2).broadcast_to([TS, NB, P]),
                       ALU.mult).then_inc(wk_done, 1)
                    cp(wbh, wb[0:TS, ds(h, 1), :].rearrange("p o b -> p (o b)")).then_inc(wk_done, 1)
                if p == 1:
                    dve.wait_ge(sc1_ready, val(0, 1, m, 1))
                    tt(Dm.rearrange("p (c t) -> p c t", c=4), MX[:, 1, :].rearrange("p (c t) -> p c t", c=4),
                       cm.unsqueeze(1).broadcast_to([P, 4, P]), ALU.add).then_inc(arg_done, 1)
                    dve.wait_ge(ab_done, val(0, 1, m, 1))
                    chain(tt(qa[:, 0:TP], q1[:, 0:TP], aB, ALU.mult))
                    dve.wait_ge(Dexp_done, val(0, 4, m, 4))
                    tt(Dm, Dm, MX[:, 0, :], ALU.mult).then_inc(P_done, 1)
                if p == 2:
                    dve.wait_ge(G_ready, val(0, 1, m, 1))
                    dve.wait_ge(sb_done, val(0, 1, m, 1))
                    dve.wait_ge(Sp_out, val(16, 16, m))
                    chain(cp(S[:, 0, :], MX[:, 1, 0:DV]))
                    chain(cp(nn[:, 0:1], MX[:, 3, 0:1]))
                    for ch in range(1, 4):
                        al = aB[:, P * ch + P - 1:P * ch + P]
                        chain(stt(S[:, ch, :], S[:, ch - 1, :], al, MX[:, 1 + ch // 2, DV * (ch % 2):DV * (ch % 2) + DV],
                                  ALU.mult, ALU.add))
                        chain(stt(nn[:, ch:ch + 1], nn[:, ch - 1:ch], al, MX[:, 3, ch:ch + 1], ALU.mult, ALU.add))
                        chain(ts(qn[:, P * ch:P * ch + P], qa[:, P * ch:P * ch + P], nn[:, ch - 1:ch], None, ALU.mult))
                    cp(nout[:, ds(h + 64, 1)], nn[:, 3:4]).then_inc(S_done, 1)
                    tt(Ds[0:TS, :], sB[0:TS, 0, :], sm[0:TS, :], ALU.add).then_inc(dsarg_done, 1)
                    chain(tt(qa[:, TP:T], q1[:, TP:T], sB[:, 1, :], ALU.mult))
                    chain(tt(qn[:, TP:T].rearrange("p (b t) -> p b t", t=ND), qa[:, TP:T].rearrange("p (b t) -> p b t", t=ND),
                             nsT[:, :, ds(h, 1)].broadcast_to([P, NB, ND]), ALU.mult))
                    dve.wait_ge(dsexp_done, val(0, 1, m, 1))
                    tt(Ds[0:TS, :], Ds[0:TS, :], MX[0:TS, 3, 64:64 + TS], ALU.mult).then_inc(Ps_done, 1)
                if p == 4:
                    dve.wait_ge(abs_done, val(0, 1, m, 1))
                    dve.wait_ge(emt_done, val(0, 2, m, 2))
                    chain(tt(Dm, Dm, emt[:, 0:TP], ALU.max))
                    chain(dve.reciprocal(Dm, Dm))
                    chain(tt(hh[:, :, 0:TP], MX[:, 0:2, :], Dm.unsqueeze(1).broadcast_to([P, 2, TP]), ALU.mult))
                if p == 5:
                    dve.wait_ge(abss_done, val(0, 1, m, 1))
                    qs_ = qn[:, TP:T]
                    chain(tt(qs_, qs_, emt[:, TP:T], ALU.max))
                    chain(dve.reciprocal(qs_, qs_))
                    tt(hh[:, :, TP:T], MX[:, 3, 0:64].rearrange("p (a t) -> p a t", a=2),
                       qs_.unsqueeze(1).broadcast_to([P, 2, TS]), ALU.mult).then_inc(hout_done, 1)
                if p == 7:
                    dve.wait_ge(cu_ready, val(0, 1, m, 1))
                    for b in range(NB):
                        stt(cs[:, b, :], cs[:, b, :], sB[:, 1, ND * b + 3:ND * b + 4],
                            MX[:, b // 2, DV * (b % 2):DV * (b % 2) + DV], ALU.mult, ALU.add).then_inc(cnew_done, 1)
                if p == 8:
                    dve.wait_ge(ss1_ready, val(0, 1, m, 1))
                    ts(two(qa), MX[:, 1:3, 0:HT], 1.0 / DV, EPS, ALU.mult, ALU.add).then_inc(ms1_done, 1)
                    no = nout[:, 0:64].rearrange("p (b h) -> p b h", b=NB)[:, :, ds(h, 1)].rearrange("p b o -> p (b o)")
                    al = sB[:, 1, :].rearrange("p (b t) -> p b t", t=ND)[:, :, 3]
                    ns = nsT[:, :, ds(h, 1)].rearrange("p b o -> p (b o)")
                    chain(tt(no, ns, al, ALU.mult))
                    chain(tt(no, no, MX[:, 0, 0:NB], ALU.add))
                    dve.wait_ge(rt1_done, val(0, 1, m, 1))
                    chain(dve.reciprocal(qa, qa))
                    chain(tt(hh, hh, qa.unsqueeze(1).broadcast_to([P, 2, T]), ALU.mult))
                    for blk in range(2):
                        ob = obuf[:, ds(h * 2 + blk, 1), :].rearrange("p o t -> p (o t)")
                        last = stt(ob, hh[:, blk, :], gT[:, ds(h * 2 + (64 + blk), 1)], ob, ALU.mult, ALU.mult)
                        if blk == 0:
                            chain(last)
                    last.then_inc(head_done, 1)

            def empty1(it, e, seen):
                kind = L1K[e]
                r, c = it
                h = c if r is None else r + c
                order = e - 3
                if kind == "Z":
                    empty_z("l1", it, e, h * 2 + seen, val(4 * GR, 4, it, order))
                if kind == "O":
                    dve.wait_ge(th_done, val(4 * GR, 4, it, order))
                    dve.wait_ge(*freed_at("l1", it, e - 1))
                    ob = obuf[:, ds(h * 2 + seen, 1), :].rearrange("p o t -> p (o t)")
                    stt(ob, misc[:, :], 1.0, ob, ALU.add, ALU.mult).then_inc(freed["d"], 1)

            def layer1(it, prev):
                seen = dict.fromkeys("ZOQKV", 0)
                for e in range(len(L1K) + 1):
                    if e:
                        empty1(it, e - 1, seen[L1K[e - 1]])
                        seen[L1K[e - 1]] += 1
                    if prev is None and e == 4:
                        gate_columns()
                    if e < len(L1K):
                        split_lo("l1", it, e + 1)
                    if prev is None and e == 1:
                        gates()
                    if prev is None and e == 2:
                        gate_maxima()
                    for at, i in ((e - 1, 1), (e, 0)):
                        if 0 <= at < len(L1K):
                            age, p = memory_points(at, i)
                            if (it, prev)[age] is not None:
                                memory((it, prev)[age], p)

            LOOP_M = 1 + (2 + 9 + 2) + 3 + 2 + (2 + 2 + 1)
            layer1((None, 0), None)
            with dve.Fori(0, MH - 1) as r:
                chain.enter(r, LOOP_M)
                layer1((r, 1), (r, 0))
            chain.leave(MH - 1)
            split_out(3, range(7))
            memory((None, MH - 1), 8)
            dve.wait_ge(head_done, 1 + MH)
            split_out(3, range(7, KT))
            dve.wait_ge(nT_ps, 1)
            cp(area(A1, "wk")[0:72, 0:P], MX[0:72, 0, 0:P]).then_inc(nT_done, 1)
            out_product("out1", [(cs_out, 16 * MH), (Sp_out, 16 + 16 * MH)])
            residual(1, 4)


_INS = ["x_prompt", "x_sample", "c_prompt", "c_sample", "cache_k", "cache_v", "state_C", "state_n", "state_m",
        "w_ada", "b_ada", "g_pre", "g_post", "w_in_attn", "sinks", "w_out_attn", "w_in_mlstm", "b_if_mlstm",
        "g_head_mlstm", "w_out_mlstm"]
_OUTS = [(1, TP, D), (NB, ND, D), (1, 1, WIN, KVH, HD), (1, 1, WIN, KVH, HD), (1, NB, WIN, KVH, HD),
         (1, NB, WIN, KVH, HD), (1, 1, MH, DK, DV), (1, 1, MH, DK), (1, 1, MH), (1, NB, MH, DK, DV),
         (1, NB, MH, DK), (1, NB, MH)]


def kernel(**inputs):
    import concourse.bacc as _bacc
    from concourse.bass_utils import run_bass_kernel_spmd as _run

    nc = _bacc.Bacc("TRN2", target_bir_lowering=False, num_devices=1)
    arrays, args = {}, []
    given = [(n, np.ascontiguousarray(inputs[n])) for n in _INS] + [("const", constants())]
    for name, a in given:
        arrays[f"in_{name}"] = a
        args.append(nc.dram_tensor(f"in_{name}", a.shape, mybir.dt.from_np(a.dtype), kind="ExternalInput").ap())
    for i, shape in enumerate(_OUTS):
        args.append(nc.dram_tensor(f"out_{i}", shape, F32, kind="ExternalOutput").ap())
    args.append(nc.dram_tensor("x_spill", (P, KT * T), F32, kind="Internal").ap())
    trunk(nc, *args)
    r = _run(nc, [arrays], core_ids=[0])
    return tuple(r.results[0][f"out_{i}"] for i in range(len(_OUTS)))
```
